# Optimizing a Trainium2 kernel written in Bass

```python
import math
import jax
import jax.numpy as jnp
from jax import lax
import numpy as np
import jax, jax.numpy as jnp

D_MODEL = 1024
BATCH = 1
SEQ = 256
DEPTH = 2

HY_WIDTH = D_MODEL // 4
HY_GROUPS = 4
ATT_WIDTH = D_MODEL // 2
ATT_HEADS = 4
ATT_HEAD_DIM = ATT_WIDTH // (2 * ATT_HEADS)
POOL_WINDOWS = (2, 4, 8, 16)
POOL_WIDTH = D_MODEL - HY_WIDTH - ATT_WIDTH
POOL_GROUP = POOL_WIDTH // len(POOL_WINDOWS)
IN_WIDTH = 3 * HY_WIDTH + 3 * ATT_WIDTH + POOL_WIDTH
ROPE_THETA = 500000.0
ROPE_DIM = ATT_HEAD_DIM // 4
Q_BLOCK = 128
HY_EMB = 33
HY_BANDS = (HY_EMB - 1) // 2
HY_FILTER_HIDDEN = 64
HY_DECAY_TARGET = 1e-2
HY_FAST_DECAY = 0.3
HY_SLOW_DECAY = 1.5
HY_SHIFT = 0.0
N_GROUPS = 4
EXPERTS_PER_GROUP = 4
N_EXPERTS = N_GROUPS * EXPERTS_PER_GROUP
TOP_K_IN_GROUP = 2
D_EXPERT = 256
PLE_DIM = 256
LN_EPS = 1e-5
RMS_EPS = 1e-5
DN_ALPHA = (2 * DEPTH) ** 0.25
DN_BETA = (8 * DEPTH) ** -0.25


def layer_norm(x, g, b):
    xf = x.astype(jnp.float32)
    mu = jnp.mean(xf, axis=-1, keepdims=True)
    var = jnp.mean(jnp.square(xf - mu), axis=-1, keepdims=True)
    y = (xf - mu) * lax.rsqrt(var + LN_EPS) * g.astype(jnp.float32) + b.astype(jnp.float32)
    return y.astype(x.dtype)

def rms_norm(x, g):
    xf = x.astype(jnp.float32)
    y = xf * lax.rsqrt(jnp.mean(jnp.square(xf), axis=-1, keepdims=True) + RMS_EPS) * g.astype(jnp.float32)
    return y.astype(x.dtype)

def rope_tables(seq_len):
    pos = jnp.arange(seq_len, dtype=jnp.float32)
    inv_freq = jnp.power(ROPE_THETA, -jnp.arange(0, ROPE_DIM, 2, dtype=jnp.float32) / ROPE_DIM)
    ang = pos[:, None] * inv_freq[None, :]
    ang = jnp.concatenate([ang, ang], axis=-1)
    return jnp.cos(ang), jnp.sin(ang)

def apply_partial_rope(x, cos, sin):
    xf = x.astype(jnp.float32)
    xr, xp = xf[..., :ROPE_DIM], xf[..., ROPE_DIM:]
    half = ROPE_DIM // 2
    rot = jnp.concatenate([-xr[..., half:], xr[..., :half]], axis=-1)
    c = cos[None, :, None, None, :]
    s = sin[None, :, None, None, :]
    return jnp.concatenate([xr * c + rot * s, xp], axis=-1).astype(x.dtype)

def short_conv_centred(u, w, b):
    up = jnp.pad(u, ((0, 0), (1, 1), (0, 0)))
    return up[:, :-2] * w[0] + up[:, 1:-1] * w[1] + up[:, 2:] * w[2] + b

def hyena_filters(seq_len, fw1, fb1, freq1, fw2, fb2, freq2, fw3):
    f32 = jnp.float32
    t = jnp.linspace(0.0, 1.0, seq_len, dtype=f32)[:, None]
    wpos = 2.0 * math.pi * jnp.arange(seq_len, dtype=f32)[:, None] / seq_len
    bands = jnp.linspace(1e-4, HY_BANDS - 1, HY_BANDS, dtype=f32)[None, :]
    z = jnp.concatenate([t, jnp.cos(wpos * bands), -jnp.sin(wpos * bands)], axis=-1)
    hdn = jnp.sin(freq1.astype(f32) * (z @ fw1.astype(f32) + fb1.astype(f32)))
    hdn = jnp.sin(freq2.astype(f32) * (hdn @ fw2.astype(f32) + fb2.astype(f32)))
    filt = hdn @ fw3.astype(f32)
    max_decay = math.log(HY_DECAY_TARGET) / HY_FAST_DECAY
    min_decay = math.log(HY_DECAY_TARGET) / HY_SLOW_DECAY
    deltas = jnp.linspace(min_decay, max_decay, HY_WIDTH, dtype=f32)[None, :]
    window = jnp.exp(-t * jnp.abs(deltas)) + HY_SHIFT
    h_fwd = filt[:, :HY_WIDTH] * window
    h_bwd = filt[:, HY_WIDTH:] * window
    k = jnp.concatenate([h_fwd, jnp.zeros((1, HY_WIDTH), f32), h_bwd[:0:-1]], axis=0)
    return k * lax.rsqrt(jnp.sum(jnp.square(k), axis=0, keepdims=True) + 1e-6)

def hyena_mixer(u, conv_w, conv_b, fw1, fb1, freq1, fw2, fb2, freq2, fw3, bias_d):
    B, L, _ = u.shape
    uc = short_conv_centred(u, conv_w, conv_b)
    x0, x1, v = jnp.split(uc, 3, axis=-1)
    v = (v * x1).astype(jnp.float32)
    k = hyena_filters(L, fw1, fb1, freq1, fw2, fb2, freq2, fw3)
    vf = jnp.fft.rfft(v, n=2 * L, axis=1)
    kf = jnp.fft.rfft(k, axis=0)
    y = jnp.fft.irfft(vf * kf[None], n=2 * L, axis=1)[:, :L]
    y = y + v * bias_d.astype(jnp.float32)
    return (y * x0.astype(jnp.float32)).astype(u.dtype)

def diff_attention(q, k, v, lq1, lk1, lq2, lk2, subln_g, lam_init, cos, sin):
    B, S, _ = q.shape
    q = q.reshape(B, S, ATT_HEADS, 2, ATT_HEAD_DIM)
    k = k.reshape(B, S, ATT_HEADS, 2, ATT_HEAD_DIM)
    v = v.reshape(B, S, ATT_HEADS, 2 * ATT_HEAD_DIM)
    q = apply_partial_rope(q, cos, sin) * (ATT_HEAD_DIM ** -0.5)
    k = apply_partial_rope(k, cos, sin)
    f32 = jnp.float32
    lam = (jnp.exp(jnp.sum(lq1.astype(f32) * lk1.astype(f32)))
           - jnp.exp(jnp.sum(lq2.astype(f32) * lk2.astype(f32))) + lam_init)
    nb = S // Q_BLOCK
    qb = q.reshape(B, nb, Q_BLOCK, ATT_HEADS, 2, ATT_HEAD_DIM).transpose(1, 0, 2, 3, 4, 5)

    def one_block(qblk):
        s = jnp.einsum('bqhcd,bkhcd->bhcqk', qblk, k, preferred_element_type=f32)
        pr = jax.nn.softmax(s, axis=-1)
        a = pr[:, :, 0] - lam * pr[:, :, 1]
        return jnp.einsum('bhqk,bkhe->bqhe', a.astype(v.dtype), v)

    o = lax.map(one_block, qb)
    o = o.transpose(1, 0, 2, 3, 4).reshape(B, S, ATT_HEADS, 2 * ATT_HEAD_DIM)
    o = rms_norm(o, subln_g) * (1.0 - lam_init)
    return o.reshape(B, S, ATT_HEADS * 2 * ATT_HEAD_DIM)

def pool_mixer(u, w, b, scale):
    B, S, _ = u.shape
    G = len(POOL_WINDOWS)
    f32 = jnp.float32
    uf = u.astype(f32).reshape(B, S, G, POOL_GROUP)
    csum = jnp.concatenate([jnp.zeros((B, 1, G, POOL_GROUP), f32), jnp.cumsum(uf, axis=1)], axis=1)
    pos = jnp.arange(S)
    pooled = []
    for g, win in enumerate(POOL_WINDOWS):
        lo = jnp.clip(pos - win // 2, 0, S - 1)
        hi = jnp.clip(pos + win // 2 - 1, 0, S - 1)
        cg = csum[:, :, g]
        cnt = (hi - lo + 1).astype(f32)[None, :, None]
        pooled.append((cg[:, hi + 1] - cg[:, lo]) / cnt)
    y = jnp.stack(pooled, axis=2) - uf
    y = jnp.einsum('bsgc,gcd->bsgd', y, w.astype(f32)) + b.astype(f32)
    return (y.reshape(B, S, POOL_WIDTH) * scale.astype(f32)).astype(u.dtype)

def hier_moe(h, wgc, bgc, wgf, bgf, w1, w3, w2):
    B, S, D = h.shape
    f32 = jnp.float32
    t = h.reshape(B * S, D)
    T = t.shape[0]
    pg = jax.nn.softmax(jnp.dot(t, wgc, preferred_element_type=f32) + bgc.astype(f32), axis=-1)
    gw, gi = lax.top_k(pg, 1)
    fl = (jnp.dot(t, wgf, preferred_element_type=f32) + bgf.astype(f32)).reshape(T, N_GROUPS, EXPERTS_PER_GROUP)
    idx = jnp.broadcast_to(gi[:, :, None], (T, 1, EXPERTS_PER_GROUP))
    fs = jnp.take_along_axis(fl, idx, axis=1)[:, 0]
    tv, ti = lax.top_k(jax.nn.softmax(fs, axis=-1), TOP_K_IN_GROUP)
    tv = tv / jnp.sum(tv, axis=-1, keepdims=True)
    eid = gi * EXPERTS_PER_GROUP + ti
    wts = gw * tv
    gates = jnp.sum(jax.nn.one_hot(eid, N_EXPERTS, dtype=f32) * wts[..., None], axis=1)
    a = jnp.einsum('td,edf->tef', t, w1)
    c = jnp.einsum('td,edf->tef', t, w3)
    act = jax.nn.silu(a) * c * gates[:, :, None].astype(t.dtype)
    y = jnp.einsum('tef,efd->td', act, w2)
    return y.reshape(B, S, D)

def first_inputs(seed: int = 0) -> dict:
    key = jax.random.key(seed)
    ks = iter(jax.random.split(key, 48))
    f32 = jnp.float32

    def nrm(shape, scale):
        return scale * jax.random.normal(next(ks), shape, f32)

    def gain(shape):
        return 1.0 + 0.05 * jax.random.normal(next(ks), shape, f32)

    L = DEPTH
    return {
        'x': nrm((BATCH, SEQ, D_MODEL), 1.0),
        'p': nrm((DEPTH, BATCH, SEQ, PLE_DIM), 1.0),
        'ln0_g': gain((D_MODEL,)),
        'ln0_b': nrm((D_MODEL,), 0.02),
        'w_in': nrm((L, D_MODEL, IN_WIDTH), D_MODEL ** -0.5),
        'hy_conv_w': nrm((L, 3, 3 * HY_WIDTH), 3 ** -0.5),
        'hy_conv_b': nrm((L, 3 * HY_WIDTH), 0.02),
        'hy_fw1': nrm((L, HY_EMB, HY_FILTER_HIDDEN), HY_EMB ** -0.5),
        'hy_fb1': nrm((L, HY_FILTER_HIDDEN), 0.02),
        'hy_freq1': gain((L, HY_FILTER_HIDDEN)),
        'hy_fw2': nrm((L, HY_FILTER_HIDDEN, HY_FILTER_HIDDEN), HY_FILTER_HIDDEN ** -0.5),
        'hy_fb2': nrm((L, HY_FILTER_HIDDEN), 0.02),
        'hy_freq2': gain((L, HY_FILTER_HIDDEN)),
        'hy_fw3': nrm((L, HY_FILTER_HIDDEN, 2 * HY_WIDTH), HY_FILTER_HIDDEN ** -0.5),
        'hy_bias': nrm((L, HY_WIDTH), 1.0),
        'att_lq1': nrm((L, ATT_HEAD_DIM), 0.1),
        'att_lk1': nrm((L, ATT_HEAD_DIM), 0.1),
        'att_lq2': nrm((L, ATT_HEAD_DIM), 0.1),
        'att_lk2': nrm((L, ATT_HEAD_DIM), 0.1),
        'att_subln_g': gain((L, 2 * ATT_HEAD_DIM)),
        'pool_w': nrm((L, len(POOL_WINDOWS), POOL_GROUP, POOL_GROUP), POOL_GROUP ** -0.5),
        'pool_b': nrm((L, len(POOL_WINDOWS), POOL_GROUP), 0.02),
        'pool_scale': gain((L, POOL_WIDTH)),
        'w_out': nrm((L, D_MODEL, D_MODEL), DN_BETA * D_MODEL ** -0.5),
        'ln1_g': gain((L, D_MODEL)),
        'ln1_b': nrm((L, D_MODEL), 0.02),
        'moe_wgc': nrm((L, D_MODEL, N_GROUPS), D_MODEL ** -0.5),
        'moe_bgc': nrm((L, N_GROUPS), 0.01),
        'moe_wgf': nrm((L, D_MODEL, N_EXPERTS), D_MODEL ** -0.5),
        'moe_bgf': nrm((L, N_EXPERTS), 0.01),
        'moe_w1': nrm((L, N_EXPERTS, D_MODEL, D_EXPERT), D_MODEL ** -0.5),
        'moe_w3': nrm((L, N_EXPERTS, D_MODEL, D_EXPERT), D_MODEL ** -0.5),
        'moe_w2': nrm((L, N_EXPERTS, D_EXPERT, D_MODEL), DN_BETA * D_EXPERT ** -0.5),
        'ple_wg': nrm((L, D_MODEL, D_MODEL), D_MODEL ** -0.5),
        'ple_bg': nrm((L, D_MODEL), 0.02),
        'ple_wp': nrm((L, PLE_DIM, D_MODEL), DN_BETA * PLE_DIM ** -0.5),
        'ln2_g': gain((L, D_MODEL)),
        'ln2_b': nrm((L, D_MODEL), 0.02),
    }

def first_block(x, p, ln0_g, ln0_b, w_in, hy_conv_w, hy_conv_b, hy_fw1, hy_fb1, hy_freq1,
              hy_fw2, hy_fb2, hy_freq2, hy_fw3, hy_bias, att_lq1, att_lk1, att_lq2, att_lk2,
              att_subln_g, pool_w, pool_b, pool_scale, w_out, ln1_g, ln1_b, moe_wgc, moe_bgc,
              moe_wgf, moe_bgf, moe_w1, moe_w3, moe_w2, ple_wg, ple_bg, ple_wp, ln2_g, ln2_b):
    S = x.shape[1]
    h = layer_norm(x, ln0_g, ln0_b)
    cos, sin = rope_tables(S)
    o_q = 3 * HY_WIDTH
    o_k = o_q + ATT_WIDTH
    o_v = o_k + ATT_WIDTH
    o_p = o_v + ATT_WIDTH
    for i in range(DEPTH):
        lam_init = 0.8 - 0.6 * math.exp(-0.3 * i)
        u = h @ w_in[i]
        y_hy = hyena_mixer(u[..., :o_q], hy_conv_w[i], hy_conv_b[i], hy_fw1[i], hy_fb1[i],
                           hy_freq1[i], hy_fw2[i], hy_fb2[i], hy_freq2[i], hy_fw3[i], hy_bias[i])
        y_att = diff_attention(u[..., o_q:o_k], u[..., o_k:o_v], u[..., o_v:o_p],
                               att_lq1[i], att_lk1[i], att_lq2[i], att_lk2[i], att_subln_g[i],
                               lam_init, cos, sin)
        y_pool = pool_mixer(u[..., o_p:], pool_w[i], pool_b[i], pool_scale[i])
        mix = jnp.concatenate([y_hy, y_att, y_pool], axis=-1) @ w_out[i]
        h = layer_norm(DN_ALPHA * h + mix, ln1_g[i], ln1_b[i])
        y_moe = hier_moe(h, moe_wgc[i], moe_bgc[i], moe_wgf[i], moe_bgf[i],
                         moe_w1[i], moe_w3[i], moe_w2[i])
        y_ple = jax.nn.sigmoid(h @ ple_wg[i] + ple_bg[i]) * (p[i] @ ple_wp[i])
        h = layer_norm(DN_ALPHA * h + y_moe + y_ple, ln2_g[i], ln2_b[i])
    return h


MEM_LEN = 256
N_MIXERS = 2
N_LAYERS_A = (DEPTH + 1) // 2
N_LAYERS_B = DEPTH // 2

MEM_HEADS = 4
MEM_HEAD_DIM = 128
MEM_W = MEM_HEADS * MEM_HEAD_DIM

CHUNK = 128
A_WIDTH = D_MODEL
A_GROUPS = 8
A_GROUP_DIM = A_WIDTH // A_GROUPS

MLA_HEADS = 8
Q_LORA = 512
KV_LORA = 256
NOPE_DIM = 128
ROPE_DIM_2 = 64
V_DIM = 128
QK_DIM = NOPE_DIM + ROPE_DIM_2
ROPE_BASE = 10000.0

EXPERTS_PER_GROUP_2 = 8
N_EXPERTS_2 = N_GROUPS * EXPERTS_PER_GROUP_2
TOP_K = 2
EXPERT_FF = 256
TOKEN_BLOCK = 2048

EPS = 1e-6


def rms_norm_2(x, g):
    xf = x.astype(jnp.float32)
    y = xf * lax.rsqrt(jnp.mean(xf * xf, axis=-1, keepdims=True) + EPS)
    return (y * g.astype(jnp.float32)).astype(x.dtype)

def layer_norm_2(x, g, b):
    xf = x.astype(jnp.float32)
    mu = jnp.mean(xf, axis=-1, keepdims=True)
    var = jnp.mean(jnp.square(xf - mu), axis=-1, keepdims=True)
    y = (xf - mu) * lax.rsqrt(var + EPS)
    return (y * g.astype(jnp.float32) + b.astype(jnp.float32)).astype(x.dtype)

def rope(x, pos):
    r = x.shape[-1]
    half = r // 2
    inv = ROPE_BASE ** (-(jnp.arange(half, dtype=jnp.float32) * 2.0 / r))
    ang = pos.astype(jnp.float32)[:, :, None, None] * inv
    cos, sin = jnp.cos(ang), jnp.sin(ang)
    xf = x.astype(jnp.float32)
    x1, x2 = xf[..., :half], xf[..., half:]
    return jnp.concatenate([x1 * cos - x2 * sin, x1 * sin + x2 * cos], axis=-1).astype(x.dtype)

def causal_block_attention(q, k, v):
    b, s, h, dk = q.shape
    nb = s // Q_BLOCK
    scale = dk ** -0.5
    qb = q.reshape(b, nb, Q_BLOCK, h, dk).transpose(1, 0, 2, 3, 4)
    kpos = jnp.arange(s)
    neg = jnp.finfo(jnp.float32).min

    def one_block(args):
        i, qi = args
        sc = jnp.einsum('bqhd,bkhd->bhqk', qi, k, preferred_element_type=jnp.float32) * scale
        qpos = i * Q_BLOCK + jnp.arange(Q_BLOCK)
        sc = jnp.where(kpos[None, :] <= qpos[:, None], sc, neg)
        p = jax.nn.softmax(sc, axis=-1)
        return jnp.einsum('bhqk,bkhd->bqhd', p.astype(v.dtype), v)

    out = lax.map(one_block, (jnp.arange(nb), qb))
    return out.transpose(1, 0, 2, 3, 4).reshape(b, s, h, v.shape[-1])

def memory_attention(q, mem_k, mem_v, qn_g, kn_g):
    q = rms_norm_2(q, qn_g)
    k = rms_norm_2(mem_k, kn_g)
    sc = jnp.einsum('bshd,bmhd->bhsm', q, k, preferred_element_type=jnp.float32) * (MEM_HEAD_DIM ** -0.5)
    p = jax.nn.softmax(sc, axis=-1)
    o = jnp.einsum('bhsm,bmhd->bshd', p.astype(mem_v.dtype), mem_v)
    return o.reshape(q.shape[0], q.shape[1], MEM_W)

def gmlp_mixer(h, w_in, ln_g, ln_b, w_s, b_s):
    b, s, _ = h.shape
    z = h @ w_in
    uv = jax.nn.gelu(z[..., :2 * A_WIDTH], approximate=False)
    u, v = uv[..., :A_WIDTH], uv[..., A_WIDTH:]
    q_mem = z[..., 2 * A_WIDTH:].reshape(b, s, MEM_HEADS, MEM_HEAD_DIM)
    v = layer_norm_2(v, ln_g, ln_b)
    vc = v.reshape(b, s // CHUNK, CHUNK, A_GROUPS, A_GROUP_DIM)
    causal = jnp.tril(jnp.ones((CHUNK, CHUNK), dtype=bool))
    w = jnp.where(causal[None], w_s, jnp.zeros((), w_s.dtype))
    mixed = jnp.einsum('gts,bnsgc->bntgc', w, vc) + b_s.T[None, None, :, :, None]
    return u * mixed.reshape(b, s, A_WIDTH), q_mem

def mla_mixer(h, positions, w_in, q_norm_g, kv_norm_g, w_q_up, w_kv_up, qn_g, kn_g):
    b, s, _ = h.shape
    z = h @ w_in
    o1 = Q_LORA
    o2 = o1 + KV_LORA
    o3 = o2 + ROPE_DIM_2
    cq = rms_norm_2(z[..., :o1], q_norm_g)
    ckv = rms_norm_2(z[..., o1:o2], kv_norm_g)
    k_rope = z[..., o2:o3]
    q_mem = z[..., o3:].reshape(b, s, MEM_HEADS, MEM_HEAD_DIM)
    q = (cq @ w_q_up).reshape(b, s, MLA_HEADS, QK_DIM)
    kv = (ckv @ w_kv_up).reshape(b, s, MLA_HEADS, NOPE_DIM + V_DIM)
    k_nope, v = kv[..., :NOPE_DIM], kv[..., NOPE_DIM:]
    k_rope = jnp.broadcast_to(k_rope[:, :, None, :], (b, s, MLA_HEADS, ROPE_DIM_2))
    k = jnp.concatenate([k_nope, k_rope], axis=-1)
    q = rms_norm_2(q, qn_g)
    k = rms_norm_2(k, kn_g)
    q = jnp.concatenate([q[..., :NOPE_DIM], rope(q[..., NOPE_DIM:], positions)], axis=-1)
    k = jnp.concatenate([k[..., :NOPE_DIM], rope(k[..., NOPE_DIM:], positions)], axis=-1)
    o = causal_block_attention(q, k, v)
    return o.reshape(b, s, MLA_HEADS * V_DIM), q_mem

def hierarchical_moe(h, w_group, b_group, w_expert, b_expert, w_gate, w_up, w_down):
    b, s, d = h.shape
    t = h.reshape(-1, d)
    n = t.shape[0]
    g_prob = jax.nn.softmax((t @ w_group).astype(jnp.float32) + b_group.astype(jnp.float32), axis=-1)
    g_idx = jnp.argmax(g_prob, axis=-1)
    g_w = jnp.take_along_axis(g_prob, g_idx[:, None], axis=-1)
    e_logits = ((t @ w_expert).astype(jnp.float32) + b_expert.astype(jnp.float32))
    e_logits = e_logits.reshape(n, N_GROUPS, EXPERTS_PER_GROUP_2)
    e_sel = jnp.take_along_axis(e_logits, g_idx[:, None, None], axis=1)[:, 0]
    e_prob = jax.nn.softmax(e_sel, axis=-1)
    top_w, top_i = lax.top_k(e_prob, TOP_K)
    top_w = top_w / jnp.sum(top_w, axis=-1, keepdims=True)
    expert_id = g_idx[:, None] * EXPERTS_PER_GROUP_2 + top_i
    weights = g_w * top_w
    combine = jnp.sum(jax.nn.one_hot(expert_id, N_EXPERTS_2, dtype=jnp.float32) * weights[..., None], axis=1)
    tb = math.gcd(n, TOKEN_BLOCK)
    nb = n // tb

    def expert_block(args):
        xb, cb = args
        gate = jnp.einsum('td,edf->tef', xb, w_gate)
        up = jnp.einsum('td,edf->tef', xb, w_up)
        act = jax.nn.silu(gate) * up * cb[..., None].astype(xb.dtype)
        return jnp.einsum('tef,efd->td', act, w_down)

    y = lax.map(expert_block, (t.reshape(nb, tb, d), combine.reshape(nb, tb, N_EXPERTS_2)))
    return y.reshape(b, s, d)

def second_inputs(seed: int = 0) -> dict:
    key = jax.random.key(seed)
    ks = iter(jax.random.split(key, 40))
    f32 = jnp.float32

    def nrm(shape, scale):
        return jax.random.normal(next(ks), shape, f32) * scale

    def gain(shape):
        return 1.0 + 0.05 * jax.random.normal(next(ks), shape, f32)

    D = D_MODEL
    a_in = 2 * A_WIDTH + MEM_W
    a_out = A_WIDTH + MEM_W
    b_in = Q_LORA + KV_LORA + ROPE_DIM_2 + MEM_W
    b_out = MLA_HEADS * V_DIM + MEM_W
    x = jax.random.normal(next(ks), (BATCH, SEQ, D), f32)
    mem = jax.random.normal(next(ks), (BATCH, MEM_LEN, D), f32)
    offsets = jax.random.randint(next(ks), (BATCH, 1), 0, 4096, dtype=jnp.int32)
    positions = offsets + jnp.arange(SEQ, dtype=jnp.int32)[None, :]
    return {
        "x": x,
        "mem": mem,
        "positions": positions,
        "mem_norm_g": gain((D,)),
        "w_mem_kv": nrm((D, 2 * MEM_W), D ** -0.5),
        "mem_qn_g": gain((DEPTH, MEM_HEAD_DIM)),
        "mem_kn_g": gain((DEPTH, MEM_HEAD_DIM)),
        "norm1_g": gain((DEPTH, D)),
        "norm2_g": gain((DEPTH, D)),
        "a_w_in": nrm((N_LAYERS_A, D, a_in), D ** -0.5),
        "a_ln_g": gain((N_LAYERS_A, A_WIDTH)),
        "a_ln_b": nrm((N_LAYERS_A, A_WIDTH), 0.02),
        "a_w_s": nrm((N_LAYERS_A, A_GROUPS, CHUNK, CHUNK), CHUNK ** -0.5),
        "a_b_s": gain((N_LAYERS_A, A_GROUPS, CHUNK)),
        "a_w_out": nrm((N_LAYERS_A, a_out, D), a_out ** -0.5),
        "b_w_in": nrm((N_LAYERS_B, D, b_in), D ** -0.5),
        "b_q_norm_g": gain((N_LAYERS_B, Q_LORA)),
        "b_kv_norm_g": gain((N_LAYERS_B, KV_LORA)),
        "b_w_q_up": nrm((N_LAYERS_B, Q_LORA, MLA_HEADS * QK_DIM), Q_LORA ** -0.5),
        "b_w_kv_up": nrm((N_LAYERS_B, KV_LORA, MLA_HEADS * (NOPE_DIM + V_DIM)), KV_LORA ** -0.5),
        "b_qn_g": gain((N_LAYERS_B, QK_DIM)),
        "b_kn_g": gain((N_LAYERS_B, QK_DIM)),
        "b_w_out": nrm((N_LAYERS_B, b_out, D), b_out ** -0.5),
        "moe_w_group": nrm((DEPTH, D, N_GROUPS), D ** -0.5),
        "moe_b_group": nrm((DEPTH, N_GROUPS), 0.01),
        "moe_w_expert": nrm((DEPTH, D, N_EXPERTS_2), D ** -0.5),
        "moe_b_expert": nrm((DEPTH, N_EXPERTS_2), 0.01),
        "moe_w_gate": nrm((DEPTH, N_EXPERTS_2, D, EXPERT_FF), D ** -0.5),
        "moe_w_up": nrm((DEPTH, N_EXPERTS_2, D, EXPERT_FF), D ** -0.5),
        "moe_w_down": nrm((DEPTH, N_EXPERTS_2, EXPERT_FF, D), EXPERT_FF ** -0.5),
    }

def second_block(x, mem, positions, mem_norm_g, w_mem_kv, mem_qn_g, mem_kn_g, norm1_g, norm2_g,
              a_w_in, a_ln_g, a_ln_b, a_w_s, a_b_s, a_w_out,
              b_w_in, b_q_norm_g, b_kv_norm_g, b_w_q_up, b_w_kv_up, b_qn_g, b_kn_g, b_w_out,
              moe_w_group, moe_b_group, moe_w_expert, moe_b_expert, moe_w_gate, moe_w_up, moe_w_down):
    b = x.shape[0]
    m = mem.shape[1]
    mem_kv = rms_norm_2(mem, mem_norm_g) @ w_mem_kv
    mem_k = mem_kv[..., :MEM_W].reshape(b, m, MEM_HEADS, MEM_HEAD_DIM)
    mem_v = mem_kv[..., MEM_W:].reshape(b, m, MEM_HEADS, MEM_HEAD_DIM)
    for i in range(DEPTH):
        h = rms_norm_2(x, norm1_g[i])
        j = i // N_MIXERS
        if i % N_MIXERS == 0:
            mix, q_mem = gmlp_mixer(h, a_w_in[j], a_ln_g[j], a_ln_b[j], a_w_s[j], a_b_s[j])
            w_out = a_w_out[j]
        else:
            mix, q_mem = mla_mixer(h, positions, b_w_in[j], b_q_norm_g[j], b_kv_norm_g[j],
                                   b_w_q_up[j], b_w_kv_up[j], b_qn_g[j], b_kn_g[j])
            w_out = b_w_out[j]
        mem_out = memory_attention(q_mem, mem_k, mem_v, mem_qn_g[i], mem_kn_g[i])
        x = x + jnp.concatenate([mix, mem_out], axis=-1) @ w_out
        x = x + hierarchical_moe(rms_norm_2(x, norm2_g[i]), moe_w_group[i], moe_b_group[i],
                                 moe_w_expert[i], moe_b_expert[i], moe_w_gate[i],
                                 moe_w_up[i], moe_w_down[i])
    return x


def setup_inputs(seed=0):
    out = dict(first_inputs(seed))
    for name, value in second_inputs(seed + 1).items():
        if name != "x":
            out[name + "_2"] = value
    return out


def reference(
    x, p, ln0_g, ln0_b, w_in, hy_conv_w, hy_conv_b, hy_fw1, hy_fb1, hy_freq1, hy_fw2, hy_fb2,
    hy_freq2, hy_fw3, hy_bias, att_lq1, att_lk1, att_lq2, att_lk2, att_subln_g, pool_w, pool_b,
    pool_scale, w_out, ln1_g, ln1_b, moe_wgc, moe_bgc, moe_wgf, moe_bgf, moe_w1, moe_w3, moe_w2,
    ple_wg, ple_bg, ple_wp, ln2_g, ln2_b, mem_2, positions_2, mem_norm_g_2, w_mem_kv_2,
    mem_qn_g_2, mem_kn_g_2, norm1_g_2, norm2_g_2, a_w_in_2, a_ln_g_2, a_ln_b_2, a_w_s_2,
    a_b_s_2, a_w_out_2, b_w_in_2, b_q_norm_g_2, b_kv_norm_g_2, b_w_q_up_2, b_w_kv_up_2,
    b_qn_g_2, b_kn_g_2, b_w_out_2, moe_w_group_2, moe_b_group_2, moe_w_expert_2, moe_b_expert_2,
    moe_w_gate_2, moe_w_up_2, moe_w_down_2,
):
    x = first_block(
        x, p, ln0_g, ln0_b, w_in, hy_conv_w, hy_conv_b, hy_fw1, hy_fb1, hy_freq1, hy_fw2,
        hy_fb2, hy_freq2, hy_fw3, hy_bias, att_lq1, att_lk1, att_lq2, att_lk2, att_subln_g,
        pool_w, pool_b, pool_scale, w_out, ln1_g, ln1_b, moe_wgc, moe_bgc, moe_wgf, moe_bgf,
        moe_w1, moe_w3, moe_w2, ple_wg, ple_bg, ple_wp, ln2_g, ln2_b,
    )
    return second_block(
        x, mem_2, positions_2, mem_norm_g_2, w_mem_kv_2, mem_qn_g_2, mem_kn_g_2, norm1_g_2,
        norm2_g_2, a_w_in_2, a_ln_g_2, a_ln_b_2, a_w_s_2, a_b_s_2, a_w_out_2, b_w_in_2,
        b_q_norm_g_2, b_kv_norm_g_2, b_w_q_up_2, b_w_kv_up_2, b_qn_g_2, b_kn_g_2, b_w_out_2,
        moe_w_group_2, moe_b_group_2, moe_w_expert_2, moe_b_expert_2, moe_w_gate_2, moe_w_up_2,
        moe_w_down_2,
    )


_drawn_inputs = setup_inputs


def setup_inputs(seed=0):
    import zlib

    import numpy as np

    out = dict(_drawn_inputs(seed))
    spreads = {}
    factors = {'moe_bgf': 3.57,
     'ple_bg': 3.264,
     'mem_norm_g_2': 2.699,
     'mem_qn_g_2': 3.821,
     'mem_kn_g_2': 4.442,
     'b_q_norm_g_2': 5.398,
     'b_qn_g_2': 4.496,
     'b_kn_g_2': 5.039,
     'moe_b_expert_2': 5.022}
    for name, (base, spread) in spreads.items():
        noise = np.random.default_rng([zlib.crc32(name.encode()), seed]).standard_normal(out[name].shape)
        drawn = base * np.exp(spread * noise) if base else spread * noise
        out[name] = jnp.asarray(drawn.astype(out[name].dtype))
    for name, factor in factors.items():
        out[name] = (out[name] * factor).astype(out[name].dtype)
    return out
```

```python
from contextlib import ExitStack

import concourse.bass as bass
from concourse import mybir

F32 = mybir.dt.float32
F32R = mybir.dt.float32r
I32 = mybir.dt.int32
ALU = mybir.AluOpType
ACT = mybir.ActivationFunctionType
X_AXIS = mybir.AxisListType.X

P = 128
T = 256
TB = T // P
D = 1024
DC = D // P
DEPTH = 2
UNIT = 2048
RING = 4
PARTS = 3
TURN = 12
HY = 256
HEADS = 4
ALPHA = (2 * DEPTH) ** 0.25
LN_EPS = 1e-5
EPS = 1e-6
TWO_PI = 6.283185307179586
ROUND = 12582912.0
GROUPS = 4
MLA_HEADS = 8


TURN1, TURN2, TURN3 = 6.28125, 0.0019350051879882812, 3.0199159819567e-07


class Signal:

    def __init__(self, sem, values, step=1):
        self.sem, self.values, self.step, self.n = sem, values, step, 0

    def tick(self, key):
        self.n += self.step
        self.values[key] = self.n
        return self.sem, self.step

    def at(self, key):
        return self.sem, self.values.get(key, self.step)


class LoopSignal:

    def __init__(self, sem, values):
        self.sem, self.values, self.n = sem, values, 0

    def tick(self, key):
        self.n += 1
        self.values[key] = self.n
        self.values["per pass"] = max(self.n, self.values.get("per pass", 1))
        return self.sem, 1

    def at(self, p, key):
        return self.sem, p * self.values.get("per pass", 1) + self.values.get(key, 1)


class Stream:

    def __init__(self):
        self.unit, self.turns = 0, 0

    def slot(self):
        return self.unit % RING

    def part(self):
        return self.unit % PARTS

    def landed(self):
        return (self.turns * (TURN // RING) + (self.unit // RING + 1)) * 32

    def count(self, ahead):
        return self.turns * TURN + (self.unit + ahead)

    def early(self, ahead):
        return type(self.turns) is int and self.turns == 0 and self.unit + ahead <= 0


class Chain:

    def __init__(self, eng, sem):
        self.eng, self.sem, self.n = eng, sem, 0

    def go(self, ins):
        self.n += 1
        ins.then_inc(self.sem, 1)

    def sync(self):
        self.eng.wait_ge(self.sem, self.n)

    def do(self, ins):
        self.go(ins)
        self.sync()


class LoopChain:

    def __init__(self, eng, sem, p, values):
        self.eng, self.sem, self.p, self.n, self.values = eng, sem, p, 0, values

    def go(self, ins):
        self.n += 1
        self.values["per pass"] = max(self.n, self.values.get("per pass", 1))
        ins.then_inc(self.sem, 1)

    def sync(self):
        self.eng.wait_ge(self.sem, self.p * self.values.get("per pass", 1) + self.n)

    def do(self, ins):
        self.go(ins)
        self.sync()


def strips_of(n, w=512):
    return [(a, min(w, n - a)) for a in range(0, n, w)]


LINEARS = {
    "w_in": (8, 2560, 512), "w_out": (8, 1024, 512), "ple_g": (8, 1024, 512), "ple_p": (2, 1024, 1024),
    "mem": (8, 1024, 512), "a_in": (8, 2560, 512), "a_out": (12, 1024, 512), "b_in": (8, 1344, 512),
    "q_up": (4, 1536, 512), "kv_up": (2, 2048, 1024), "b_out": (12, 1024, 512),
}


def program(nc, A, seen):
    ctx = ExitStack()
    with ctx:
        sems = {}

        def sem(name):
            if name not in sems:
                sems[name] = ctx.enter_context(nc.semaphore(name))
            return sems[name]

        def signal(name, step=1):
            return Signal(sem(name), seen.setdefault(name, {}), step)

        top = [16512]

        def region(size):
            at = top[0]
            top[0] += size
            return at

        names = [0]

        def sb(name, shape, at, dt=F32, base=[0]):
            names[0] += 1
            return nc.alloc_sbuf_tensor_at(f"{name}_at{names[0]}", shape, dt, offset=at)

        class Space:

            def __init__(self, at, size):
                self.at, self.end = at, at + size

            def take(self, name, shape, dt=F32):
                n = 4
                for s in shape[1:]:
                    n *= s
                n = (n + 31) // 32 * 32
                at = self.at
                self.at += n
                assert self.at <= self.end, (name, self.at - self.end)
                return sb(name, shape, at, dt)

        RAW = sb("raw", [P, RING, UNIT], region(RING * UNIT * 4))
        WH = sb("w_hi", [P, PARTS, UNIT], region(PARTS * UNIT * 4), F32R)
        WL = sb("w_lo", [P, PARTS, UNIT], region(PARTS * UNIT * 4), F32R)
        X = sb("x", [P, TB, D], region(8192))
        y_at = region(8192)
        th_at = region(24576)
        row_at = region(8192)
        small_at = region(10240)
        z_at = top[0]
        z_size = 229344 - z_at
        Y = sb("y", [P, TB, D], y_at)
        TH = sb("t_hi", [P, 12, T], th_at, F32R)
        TL = sb("t_lo", [P, 12, T], th_at + 12288, F32R)
        ROW = sb("row", [P, 2, D], row_at)

        small = Space(small_at, 10240)
        CW = A["c_small"].shape[1]
        CS = small.take("consts", [P, CW])
        SROW = small.take("srow", [P, 1024])
        NST = small.take("stats", [P, 8, 6])
        MV = small.take("mv", [P, 8, 2])
        RS = small.take("rs", [P, 16])
        RT = small.take("rt", [P, 16])
        MX = small.take("mx", [P, 8])
        NM = small.take("nm", [P, 8])
        SU = small.take("su", [P, 8])
        RC = small.take("rc", [P, 8])
        LAM = small.take("lam", [P, 8])
        KEY = small.take("key", [P, 2])
        JP = small.take("jp", [P, 2])
        TABF = small.take("tabf", [P, 8])
        TAB = small.take("tab", [P, 8], I32)
        GQK = small.take("gqk", [P, 4])
        BST = small.take("bst", [P, 8])
        HCOL = small.take("hcol", [64, 8])
        MEMG = small.take("memg", [P, 8])
        POS = small.take("pos", [P, TB], I32)
        LQ = small.take("lq", [P, 4, 64])
        POSF = small.take("posf", [P, TB])

        at = [0]

        def const(n):
            a = at[0]
            at[0] += n
            return CS[:, a:a + n]

        IDENT, LOWER, ONES, IOTA, UPPER1, CMASK = (const(P) for _ in range(6))
        PCOL, PRI4, PRI8, IDX4, ZERO = const(1), const(4), const(8), const(4), const(1)
        COS8, SIN8, INVF = const(16), const(16), const(32)

        z = Space(z_at, z_size - 8192)
        MKT = sb("mem_kt", [P, HEADS, T], z_at + z_size - 8192)
        MV_ = sb("mem_v", [P, TB, 512], z_at + z_size - 4096)
        z = Space(z_at, z_size)
        U = z.take("u", [P, TB, 2560])
        CAT8 = z.take("cat8", [P, TB, D])
        um_at = z.at
        UM = z.take("u_before", [P, TB, 768])
        UP = z.take("u_after", [P, TB, 768])
        ks = Space(um_at + 6144, 6144)
        KR, KI, K2 = (ks.take(n, [P, 2, HY]) for n in ("kr", "ki", "k2"))
        BAND = z.take("band", [P, TB, 4, T])
        DC_, DS_ = z.take("dft_c", [P, 2, T]), z.take("dft_s", [P, 2, T])
        DS0, DC2 = z.take("dft_s0", [P, 2, P]), z.take("dft_c2", [P, 2, P])
        INV = z.take("dft_inv", [P, 4, T])
        PA = z.take("probs_a", [P, 4, T])
        ZT, FW1, FW2 = z.take("zt", [33, T]), z.take("fw1", [33, 64]), z.take("fw2", [64, 64])
        ARG, PW = z.take("arg", [64, T]), z.take("pool_w", [64, 4, 64])
        ty = Space(y_at, 8192)
        YPT = ty.take("ypt", [64, 4, T])
        FW3, H1, H2 = ty.take("fw3", [64, 512]), ty.take("h1", [64, T]), ty.take("h2", [64, T])
        FR = PA[0:64, 0, :]
        QKT = sb("qkt", [P, 8, T], th_at)
        ATA = sb("at_a", [P, 4, P], th_at + 8192)
        tl = Space(th_at + 12288, 12288)
        WIN, VV = tl.take("win", [P, 2, HY]), tl.take("vv", [P, TB, HY])
        FF, YF = tl.take("ff", [P, 2, 512]), tl.take("yf", [P, 4, HY])
        z = Space(z_at, z_size - 8192)
        UV = z.take("uv", [P, TB, 2560])
        CAT12 = z.take("cat12", [P, TB, 1536])
        WST, WSR = z.take("ws_t", [P, 8, P]), z.take("ws", [P, 8, P])
        PB = z.take("probs_b", [P, 4, T])
        QMT = sb("qm_t", [P, HEADS, T], th_at)
        ATB = sb("at_b", [P, 8, P], th_at + 4096)
        z = Space(z_at, z_size - 8192)
        ZB = z.take("zb", [P, TB, 1344])
        CAT12B = z.take("cat12b", [P, TB, 1536])
        QQ = z.take("qq", [P, TB, 1536])
        KV = z.take("kv", [P, TB, 2048])
        ktn_at = z.at
        KTN = z.take("ktn", [P, 8, T])
        KRP = sb("krp", [P, TB, 512], y_at)
        ATC = sb("at_c", [P, 8, P], y_at + 4096)
        QTN, QTR = sb("qtn", [P, 8, T], th_at), sb("qtr", [64, 8, T], th_at + 8192)
        KTR = sb("ktr", [64, 8, T], th_at + 16384)
        PC = sb("probs_c", [P, 4, T], row_at + 4096)
        SCR = sb("scr", [P, 1536], th_at + 8192)
        QMT2 = sb("qm_t2", [P, HEADS, T], th_at)
        TRIG = sb("trig", [P, 6, TB, 32], ktn_at)
        z = Space(z_at, z_size - 8192)
        HH, HL = (z.take(n, [P, TB, D], F32R) for n in ("tok_hi", "tok_lo"))
        XH, XL = (z.take(n, [P, DC, P], F32R) for n in ("xs_hi", "xs_lo"))
        YH, YL = (z.take(n, [P, D], F32R) for n in ("ys_hi", "ys_lo"))
        ST, SP = z.take("sel_t", [P, T], F32R), z.take("sel", [P, TB, P], F32R)
        PKROW = z.take("key_row", [P, T])
        DG = z.take("key_diag", [P, TB, P])
        RW, RWH, RWL = z.take("rw", [P, DC, 36]), z.take("rw_hi", [P, DC, 36], F32R), z.take("rw_lo", [P, DC, 36], F32R)
        AH, AL = (z.take(n, [P, 2, P], F32R) for n in ("act_hi", "act_lo"))
        SIL, GLU = z.take("silu", [P, 256]), z.take("glu", [P, 256])
        ZR = z.take("zeros", [P, P], F32R)
        GS = z.take("gate_sel", [P, 8])
        GH, GL = (z.take(n, [P, TB, 8], F32R) for n in ("gate_hi", "gate_lo"))
        LG, RB = z.take("logits", [P, TB, 36]), z.take("route_b", [P, 36])
        r1, r2, r3, r4 = (z.take(n, [P, TB, 32]) for n in ("ra", "rb", "rc_", "rd"))
        OH4 = z.take("oh4", [P, TB, 4])
        OH1, OH2, FS = (z.take(n, [P, TB, 8]) for n in ("oh1", "oh2", "fs"))
        v = [z.take(f"v{i}", [P, TB]) for i in range(12)]
        PT = z.take("p_in", [P, TB, 256])
        PTH, PTL = (z.take(n, [P, 2, T], F32R) for n in ("p_hi", "p_lo"))
        SG = z.take("sg", [P, TB, D])

        BK = [ctx.enter_context(nc.psum_tensor(f"bank{i}", [P, 512], F32)) for i in range(8)]

        raw_in = [sem(f"raw_in{i}") for i in range(RING)]
        hi_done = sem("hi_done")
        split_done = sem("split_done")
        unit_used = sem("unit_used")
        consts_in = signal("consts_in", 16)
        rows_in = signal("rows_in", 16)
        params_in = {n: signal(f"{n}_in", 16) for n in ("hy", "hy2", "route", "p", "mem", "ws")}
        shift_in = signal("shift_in", 16)
        x_in = signal("x_in", 16)
        out_done = signal("out_done", 16)
        turned, turn_hi, turn_lo = signal("turned"), signal("turn_hi"), signal("turn_lo")
        evac_a, evac_d = signal("evac_a"), signal("evac_d")
        small_ready = signal("small_ready")
        scores_ready, negmax_ready, probs_ready = signal("scores_ready"), signal("negmax_ready"), signal("probs_ready")
        weights_ready, pturned, at_ready = signal("weights_ready"), signal("pturned"), signal("at_ready")
        heads_ready, heads_taken = signal("heads_ready"), signal("heads_taken")
        dve_ready = signal("dve_ready")
        act_ready = signal("act_ready")
        pool_ready = signal("pool_ready")

        class MoeSignals:
            def __init__(self, L):
                def ls(n):
                    return LoopSignal(sem(f"m{L}_{n}"), seen.setdefault(f"m{L}_{n}", {}))
                self.sel, self.gathered, self.xh, self.xl = ls("sel"), ls("gathered"), ls("xh"), ls("xl")
                self.silu, self.glu, self.at, self.ah, self.al = ls("silu"), ls("glu"), ls("at"), ls("ah"), ls("al")
                self.yh, self.yl, self.scattered = ls("yh"), ls("yl"), ls("scattered")
                self.chain, self.chain_values = sem(f"m{L}_chain"), seen.setdefault(f"m{L}_chain", {})

        moe_signals = [MoeSignals(L) for L in range(4)]
        chain_sem = {n: sem(f"chain_{n}") for n in ("dve", "act", "pool", "pe")}
        for n in chain_sem:
            seen.setdefault(n, {})

        EPG = [4, 4, 8, 8]
        NR = [20, 20, 36, 36]
        MOE_W = [(A["moe_w1"][0], A["moe_w3"][0], A["moe_w2"][0]), (A["moe_w1"][1], A["moe_w3"][1], A["moe_w2"][1]),
                 (A["moe_w_gate_2"][0], A["moe_w_up_2"][0], A["moe_w_down_2"][0]),
                 (A["moe_w_gate_2"][1], A["moe_w_up_2"][1], A["moe_w_down_2"][1])]
        DRAM_W = {"w_in0": A["w_in"][0], "w_in1": A["w_in"][1], "w_out0": A["w_out"][0], "w_out1": A["w_out"][1],
                  "ple_g0": A["ple_wg"][0], "ple_g1": A["ple_wg"][1], "ple_p0": A["ple_wp"][0],
                  "ple_p1": A["ple_wp"][1], "mem": A["w_mem_kv_2"], "a_in": A["a_w_in_2"][0],
                  "a_out": A["a_w_out_2"][0], "b_in": A["b_w_in_2"][0], "q_up": A["b_w_q_up_2"][0],
                  "kv_up": A["b_w_kv_up_2"][0], "b_out": A["b_w_out_2"][0]}

        def linear_shape(key):
            chunks, n, w = LINEARS[key.rstrip("01")]
            per_unit = 2 if w == 1024 else 4
            return chunks, strips_of(n, w), per_unit

        block = ctx.enter_context(nc.Block())

        @block.sync
        def _(sp):
            s = Stream()

            def load(dst_src):
                if not s.early(1 - RING):
                    sp.wait_ge(split_done, s.count(1 - RING))
                for dst, src in dst_src:
                    sp.dma_start(dst, src).then_inc(raw_in[s.slot()], 16)
                s.unit += 1

            def load_linear(key):
                chunks, strips, per_unit = linear_shape(key)
                w = DRAM_W[key]
                for n0, width in strips:
                    for c0 in range(0, chunks, per_unit):
                        dst = RAW[:, s.slot(), 0:per_unit * width].rearrange("p (k n) -> p k n", n=width)
                        src = w[c0 * P:(c0 + per_unit) * P, n0:n0 + width].rearrange("(k p) n -> p k n", p=P)
                        h = per_unit // 2
                        load([(dst[:, 0:h, :], src[:, 0:h, :]), (dst[:, h:, :], src[:, h:, :])])

            def load_pass(L, group):
                w1, w3, w2 = MOE_W[L]

                def up(e, half):
                    dst = RAW[:, s.slot(), :].rearrange("p (k m n) -> p k m n", k=4, m=2)
                    load([(dst[:, :, m, :], w[bass.ds(group * EPG[L] + e, 1), half * 512:half * 512 + 512, :]
                           .rearrange("a (k p) n -> p (a k) n", p=P)) for m, w in enumerate((w1, w3))])

                def down(e):
                    dst = RAW[:, s.slot(), :].rearrange("p (k n) -> p k n", k=2)
                    src = w2[bass.ds(group * EPG[L] + e, 1), :, :].rearrange("a (k p) n -> p (a k) n", p=P)
                    load([(dst[:, k:k + 1, :], src[:, k:k + 1, :]) for k in range(2)])

                for e in range(EPG[L]):
                    up(e, 0)
                    up(e, 1)
                    if e:
                        down(e - 1)
                down(EPG[L] - 1)

            def load_experts(L):
                turns = EPG[L] * 3 // TURN
                start, unit = s.turns, s.unit
                load_pass(L, 0)
                sp.wait_ge(*dve_ready.at(("table", L)))
                passes = sp.value_load(TAB[0:1, 0:1], min_val=4, max_val=5)
                with sp.Fori(1, passes) as p:
                    group = sp.value_load(TAB[0:1, bass.ds(p + 1, 1)], min_val=0, max_val=3)
                    s.unit, s.turns = unit, start + p * turns
                    load_pass(L, group)
                s.unit, s.turns = unit, sp.snap(start + passes * turns)

            for L in range(DEPTH):
                for key in ("w_in", "w_out", "ple_g", "ple_p"):
                    load_linear(f"{key}{L}")
                load_experts(L)
            for key in ("mem", "a_in", "a_out"):
                load_linear(key)
            load_experts(2)
            for key in ("b_in", "q_up", "kv_up", "b_out"):
                load_linear(key)
            load_experts(3)
            sp.wait_ge(*dve_ready.at("out"))
            for tb in range(TB):
                sp.dma_start(A["out"][0, tb * P:(tb + 1) * P, :], X[:, tb, :]).then_inc(*out_done.tick(tb))
            sp.wait_ge(*out_done.at(TB - 1))

        @block.gpsimd
        def _(pool):
            ch = Chain(pool, chain_sem["pool"])

            def row(src, slot, a=0):
                n = src.shape[-1]
                pool.dma_start(ROW[:, slot, a:a + n], src.partition_broadcast(P)).then_inc(*rows_in.tick(None))

            def rows(key, lines, free):
                if free is not None:
                    pool.wait_ge(*free)
                for src, slot, a in lines:
                    row(src, slot, a)
                rows_in.values[key] = rows_in.n

            def param(kind, key, dst, src):
                pool.dma_start(dst, src).then_inc(*params_in[kind].tick(key))

            pool.dma_start(CS[:, :], A["c_small"]).then_inc(*consts_in.tick("consts"))
            for tb in range(TB):
                pool.dma_start(X[:, tb, :], A["x"][0, tb * P:(tb + 1) * P, :]).then_inc(*x_in.tick("x"))
            rows("ln0", [(A["ln0_g"], 0, 0), (A["ln0_b"], 1, 0)], None)

            def hyena_params(L):
                if L:
                    pool.wait_ge(*dve_ready.at(("moe_out", L - 1)))
                param("hy", L, BAND[:, :, :, :], A["c_band"])
                param("hy", L, DC_[:, :, :], A["c_dc"])
                param("hy", L, DS_[:, :, :], A["c_ds"])
                param("hy", L, DS0[:, :, :], A["c_ds0"])
                param("hy", L, DC2[:, :, :], A["c_dc2"])
                param("hy", L, INV[:, :, :], A["c_inv"])
                param("hy", L, ZT[:, :], A["c_zt"])
                param("hy", L, FW1[:, :], A["hy_fw1"][L])
                param("hy", L, FW2[:, :], A["hy_fw2"][L])
                param("hy", L, PW[:, :, :], A["pool_w"][L].rearrange("g c d -> c g d"))
                for i, n in enumerate(("hy_fb1", "hy_freq1", "hy_fb2", "hy_freq2")):
                    param("hy", L, HCOL[:, i:i + 1], A[n][L].rearrange("(p a) -> p a", a=1))
                for a, n in ((0, "hy_bias"), (256, "att_subln_g"), (640, "pool_scale")):
                    src = A[n][L]
                    param("hy", L, SROW[:, a:a + src.shape[0]], src.partition_broadcast(P))
                for i, n in enumerate(("att_lq1", "att_lk1", "att_lq2", "att_lk2")):
                    param("hy", L, LQ[:, i, :], A[n][L].partition_broadcast(P))
                param("hy", L, SROW[:, 384:640], A["pool_b"][L].rearrange("g d -> (g d)").partition_broadcast(P))
                param("hy2", L, FW3[:, :], A["hy_fw3"][L])
                pool.wait_ge(*evac_d.at((f"w_in{L}", 4)))
                pool.wait_ge(*evac_a.at((f"w_in{L}", 4)))
                param("hy2", L, WIN[:, :, :], A["c_win"])

            def hyena(L):
                conv_w, conv_b = A["hy_conv_w"][L], A["hy_conv_b"][L]
                rows(("hy_a", L), [(conv_w[0], 0, 0), (conv_w[1], 1, 0)],
                     dve_ready.at("ln0") if L == 0 else dve_ready.at(("ln2", 0)))
                ch.go(pool.memset(UM[:, 0, :], 0.0))
                ch.go(pool.memset(UP[:, 1, :], 0.0))
                ch.sync()
                for s_ in range(2):
                    pool.wait_ge(*evac_a.at((f"w_in{L}", s_)))
                    pool.wait_ge(*evac_d.at((f"w_in{L}", s_)))
                for dst, src in ((UM[1:P, 0, :], U[0:P - 1, 0, 0:768]), (UM[1:P, 1, :], U[0:P - 1, 1, 0:768]),
                                 (UM[0:1, 1, :], U[P - 1:P, 0, 0:768]), (UP[0:P - 1, 0, :], U[1:P, 0, 0:768]),
                                 (UP[0:P - 1, 1, :], U[1:P, 1, 0:768]), (UP[P - 1:P, 0, :], U[0:1, 1, 0:768])):
                    pool.dma_start(dst, src).then_inc(*shift_in.tick(L))
                pool.wait_ge(*shift_in.at(L))
                pool.wait_ge(*rows_in.at(("hy_a", L)))
                for tb in range(TB):
                    ch.go(pool.tensor_tensor(UM[:, tb, :], UM[:, tb, :], ROW[:, 0, 0:768], ALU.mult))
                    ch.go(pool.tensor_tensor(U[:, tb, 0:768], U[:, tb, 0:768], ROW[:, 1, 0:768], ALU.mult))
                ch.sync()
                for tb in range(TB):
                    ch.go(pool.tensor_tensor(UM[:, tb, :], UM[:, tb, :], U[:, tb, 0:768], ALU.add))
                rows(("hy_b", L), [(conv_w[2], 0, 0), (conv_b, 1, 0)], None)
                pool.wait_ge(*rows_in.at(("hy_b", L)))
                for tb in range(TB):
                    ch.go(pool.tensor_tensor(UP[:, tb, :], UP[:, tb, :], ROW[:, 0, 0:768], ALU.mult))
                ch.sync()
                for tb in range(TB):
                    ch.do(pool.tensor_tensor(UP[:, tb, :], UP[:, tb, :], ROW[:, 1, 0:768], ALU.add))
                    ch.do(pool.tensor_tensor(UM[:, tb, :], UM[:, tb, :], UP[:, tb, :], ALU.add))
                pool.wait_ge(*evac_d.at((f"w_in{L}", 4)))
                for tb in range(TB):
                    ins = pool.tensor_tensor(VV[:, tb, :], UM[:, tb, 512:768], UM[:, tb, 256:512], ALU.mult)
                    ch.go(ins)
                ch.sync()
                pool.nop().then_inc(*pool_ready.tick(("conv", L)))
                rows(("ln1", L), [(A["ln1_g"][L], 0, 0), (A["ln1_b"][L], 1, 0)], None)

            def route_params(L, name_w, name_b, i):
                wg, we = A[name_w[0]][i], A[name_w[1]][i]
                n = we.shape[-1]
                for c in range(DC):
                    param("route", L, RW[:, c, 0:4], wg[c * P:(c + 1) * P, :])
                    param("route", L, RW[:, c, 4:4 + n], we[c * P:(c + 1) * P, :])
                param("route", L, RB[:, 0:4], A[name_b[0]][i].partition_broadcast(P))
                param("route", L, RB[:, 4:4 + n], A[name_b[1]][i].partition_broadcast(P))

            for L in range(DEPTH):
                hyena_params(L)
                hyena(L)
                pool.wait_ge(*turn_lo.at((("cat", L), 3)))
                route_params(L, ("moe_wgc", "moe_wgf"), ("moe_bgc", "moe_bgf"), L)
                for tb in range(TB):
                    param("p", L, PT[:, tb, :], A["p"][L, 0, tb * P:(tb + 1) * P, :])
                rows(("ple", L), [(A["ple_bg"][L], 0, 0)], dve_ready.at(("ln1", L)))
                rows(("ln2", L), [(A["ln2_g"][L], 0, 0), (A["ln2_b"][L], 1, 0)], dve_ready.at(("ple_b", L)))

            pool.wait_ge(*dve_ready.at(("ln2", 1)))
            for tb in range(TB):
                param("mem", 0, Y[:, tb, :], A["mem_2"][0, tb * P:(tb + 1) * P, :])
            for tb in range(TB):
                param("mem", 0, POS[:, tb:tb + 1], A["positions_2"][0, tb * P:(tb + 1) * P].rearrange("(p a) -> p a", a=1))
            for i in range(2):
                param("mem", 0, GQK[:, 2 * i:2 * i + 1], A["mem_qn_g_2"][i].rearrange("(p a) -> p a", a=1))
                param("mem", 0, GQK[:, 2 * i + 1:2 * i + 2], A["mem_kn_g_2"][i].rearrange("(p a) -> p a", a=1))
            for g in range(8):
                param("mem", 0, BST[:, g:g + 1], A["a_b_s_2"][0, g, :].rearrange("(p a) -> p a", a=1))
            rows("memg", [(A["mem_norm_g_2"], 0, 0), (A["norm1_g_2"][0], 1, 0)], None)
            param("ws", 0, WSR[:, :, :], A["a_w_s_2"][0].rearrange("g t s -> t g s"))
            rows("aln", [(A["a_ln_g_2"][0], 0, 0), (A["a_ln_b_2"][0], 1, 0)], dve_ready.at(("norm1", 2)))
            rows(("norm2", 2), [(A["norm2_g_2"][0], 0, 0)], dve_ready.at("aln"))
            pool.wait_ge(*turn_lo.at((("cat", 2), 5)))
            route_params(2, ("moe_w_group_2", "moe_w_expert_2"), ("moe_b_group_2", "moe_b_expert_2"), 0)
            rows(("norm1", 3), [(A["norm1_g_2"][1], 0, 0)], dve_ready.at(("norm2", 2)))
            rows("bq", [(A["b_q_norm_g_2"][0], 0, 0), (A["b_kv_norm_g_2"][0], 0, 512)], dve_ready.at(("norm1", 3)))
            rows("qkn", [(A["b_qn_g_2"][0], 0, 0), (A["b_kn_g_2"][0], 0, 192)], dve_ready.at("bq"))
            rows(("norm2", 3), [(A["norm2_g_2"][1], 0, 0)], dve_ready.at("qkn"))
            pool.wait_ge(*turn_lo.at((("cat", 3), 5)))
            route_params(3, ("moe_w_group_2", "moe_w_expert_2"), ("moe_b_group_2", "moe_b_expert_2"), 1)

        @block.tensor
        def _(pe):
            s = Stream()
            owner = {}

            def claim(*banks):
                for b in banks:
                    if b in owner:
                        pe.wait_ge(*owner.pop(b))

            def three(out, ah, al, bh, bl, start, stop, loose=False):
                pe.matmul(out, ah, bh, start=start, stop=False, skip_group_check=loose)
                pe.matmul(out, ah, bl, start=False, stop=False, skip_group_check=loose)
                return pe.matmul(out, al, bh, start=False, stop=stop, skip_group_check=loose)

            def turn(key, src, chunks, after, low=True):
                for w in after:
                    pe.wait_ge(*w)
                for g in range(chunks // 2):
                    b = 4 + g % 2
                    claim(b)
                    for c in range(2):
                        for tb in range(TB):
                            a = (2 * g + c) * P
                            ins = pe.transpose(BK[b][:, c * T + tb * P:c * T + tb * P + P], src[:, tb, a:a + P], IDENT)
                    ins.then_inc(*turned.tick((key, g)))
                    owner[b] = (turn_lo if low else turn_hi).at((key, g))

            def linear(key, th=TH, tl_=TL):
                chunks, strips, per_unit = linear_shape(key)
                for i, (n0, width) in enumerate(strips):
                    wide = width > 512
                    banks = {(tb, j): 2 * tb + j if wide else 2 * (i % 2) + tb for tb in range(TB)
                             for j in range(2 if wide else 1)}
                    claim(*banks.values())
                    for c0 in range(0, chunks, per_unit):
                        pe.wait_ge(split_done, s.count(1))
                        for c in range(per_unit):
                            for (tb, j), b in banks.items():
                                w = min(width, 512)
                                a = c * width + j * 512
                                ins = three(BK[b][:, 0:w], th[:, c0 + c, tb * P:(tb + 1) * P],
                                            tl_[:, c0 + c, tb * P:(tb + 1) * P], WH[:, s.part(), a:a + w],
                                            WL[:, s.part(), a:a + w], c0 + c == 0, c0 + c == chunks - 1)
                        ins.then_inc(unit_used, 1)
                        s.unit += 1
                    for (tb, j), b in banks.items():
                        owner[b] = (evac_d if tb else evac_a).at((key, i))

            def attention(key, rounds, score, value):
                def scores(r):
                    claim(2 * (r % 2), 2 * (r % 2) + 1)
                    for i in range(4):
                        ins = score(r, i, BK[2 * (r % 2) + i % 2][:, (i // 2) * T:(i // 2) * T + P * rounds[r][1]])
                    ins.then_inc(*scores_ready.tick((key, r)))
                    for b in (2 * (r % 2), 2 * (r % 2) + 1):
                        owner[b] = probs_ready.at((key, r))

                scores(0)
                for r, (qb, kbs, heads, step, probs, at_) in enumerate(rounds):
                    if r + 1 < len(rounds):
                        scores(r + 1)
                    pe.wait_ge(*weights_ready.at((key, r)))
                    claim(4, 5)
                    for h in range(heads):
                        for kb in range(kbs):
                            n = h * kbs + kb
                            ins = pe.transpose(BK[4 + n // 4][:, (n % 4) * P:(n % 4) * P + P],
                                               probs[:, h * step, kb * P:(kb + 1) * P], IDENT)
                    ins.then_inc(*pturned.tick((key, r)))
                    owner[4] = owner[5] = at_ready.at((key, r))
                    pe.wait_ge(*at_ready.at((key, r)))
                    b = 6 + r % 2
                    claim(b)
                    for h in range(heads):
                        for kb in range(kbs):
                            ins = pe.matmul(BK[b][:, h * P:(h + 1) * P], at_[:, h * kbs + kb, :],
                                            value(r, h, kb), start=kb == 0, stop=kb == kbs - 1)
                    ins.then_inc(*heads_ready.tick((key, r)))
                    owner[b] = heads_taken.at((key, r))

            def experts(L):
                m = moe_signals[L]
                E = EPG[L]
                turns = E * 3 // TURN
                pe.wait_ge(*dve_ready.at(("rw", L)))
                claim(6, 7)
                for tb in range(TB):
                    for c in range(DC):
                        t_ = slice(tb * P, tb * P + P)
                        ins = three(BK[6][:, tb * 64:tb * 64 + NR[L]], TH[:, c, t_], TL[:, c, t_],
                                    RWH[:, c, 0:NR[L]], RWL[:, c, 0:NR[L]], c == 0, c == DC - 1)
                ins.then_inc(*small_ready.tick(("logits", L)))
                pe.wait_ge(*dve_ready.at(("onehot", L)))
                R = BK[7]
                pe.matmul(R[:, 0:4], LOWER, OH4[:, 0, :], start=True, stop=True)
                pe.matmul(R[:, 4:8], LOWER, OH4[:, 1, :], start=True, stop=False)
                pe.matmul(R[:, 4:8], ONES, OH4[:, 0, :], start=False, stop=True)
                pe.matmul(R[:, 8:12], ONES, OH4[:, 0, :], start=True, stop=False)
                pe.matmul(R[:, 8:12], ONES, OH4[:, 1, :], start=False, stop=True)\
                    .then_inc(*small_ready.tick(("ranks", L)))
                pe.wait_ge(*dve_ready.at(("diag", L)))
                for tb in range(TB):
                    ins = pe.matmul(BK[6][:, tb * P:tb * P + P], ONES, DG[:, tb, :], start=True, stop=True)
                ins.then_inc(*small_ready.tick(("keyrow", L)))
                if L < DEPTH:
                    pe.wait_ge(*params_in["p"].at(L))
                    turn(("p", L), PT, 2, [])
                    linear(f"ple_g{L}")
                    pe.wait_ge(*turn_lo.at((("p", L), 0)))
                    linear(f"ple_p{L}", PTH, PTL)
                claim(0, 1, 2, 3, 4, 5, 6, 7)
                pe.wait_ge(*dve_ready.at(("table", L)))
                passes = pe.value_load(TAB[0:1, 0:1], min_val=4, max_val=5)
                for b in range(4):
                    pe.matmul(BK[b][:, :], ZR[:, :], TH[:, 0:2, :].rearrange("p a b -> p (a b)"), start=True, stop=True)
                start, unit = s.turns, s.unit
                with pe.Fori(0, passes) as p:
                    s.unit, s.turns = unit, start + p * turns
                    pe.wait_ge(*m.sel.at(p, "sel"))
                    for q in range(2):
                        for c in range(4):
                            a = (4 * q + c) * P
                            o = BK[6 + q][:, c * P:(c + 1) * P]
                            for tb in range(TB):
                                pe.matmul(o, HH[:, tb, a:a + P], SP[:, tb, :], start=tb == 0, stop=False)
                                ins = pe.matmul(o, HL[:, tb, a:a + P], SP[:, tb, :], start=False, stop=tb == 1)
                        if q == 0:
                            ins.then_inc(*m.gathered.tick(0))
                    for tb in range(TB):
                        pe.matmul(BK[4][:, 0:8], SP[:, tb, :], GH[:, tb, :], start=tb == 0, stop=False)
                        ins = pe.matmul(BK[4][:, 0:8], SP[:, tb, :], GL[:, tb, :], start=False, stop=tb == 1)
                    ins.then_inc(*m.gathered.tick(1))

                    def up(e):
                        for half in range(2):
                            pe.wait_ge(split_done, s.count(1))
                            if half == 0:
                                if e == 0:
                                    pe.wait_ge(*m.xl.at(p, 1))
                                else:
                                    pe.wait_ge(*m.glu.at(p, e - 1))
                            for k in range(4):
                                c = half * 4 + k
                                ins = three(BK[6][:, :], XH[:, c, :], XL[:, c, :],
                                            WH[:, s.part(), k * 512:k * 512 + 512],
                                            WL[:, s.part(), k * 512:k * 512 + 512], c == 0, c == 7)
                            ins.then_inc(unit_used, 1)
                            s.unit += 1

                    def down(e):
                        pe.wait_ge(split_done, s.count(1))
                        pe.wait_ge(*m.al.at(p, e))
                        for f in range(2):
                            for half in range(2):
                                a = f * 1024 + half * 512
                                ins = three(BK[4 + half][:, :], AH[:, f, :], AL[:, f, :], WH[:, s.part(), a:a + 512],
                                            WL[:, s.part(), a:a + 512], e == 0 and f == 0, e == E - 1 and f == 1,
                                            True)
                        ins.then_inc(unit_used, 1)
                        s.unit += 1

                    for e in range(E):
                        up(e)
                        if e:
                            down(e - 1)
                        pe.wait_ge(*m.glu.at(p, e))
                        for f in range(2):
                            ins = pe.transpose(BK[7][:, f * P:(f + 1) * P], GLU[:, f * P:(f + 1) * P], IDENT)
                        ins.then_inc(*m.at.tick(e))
                    down(E - 1)
                    pe.wait_ge(*m.yl.at(p, 1))
                    for tb in range(TB):
                        for half in range(2):
                            for y in (YH, YL):
                                ins = pe.matmul(BK[2 * tb + half][:, :], ST[:, tb * P:(tb + 1) * P],
                                                y[:, half * 512:half * 512 + 512], start=False, stop=False,
                                                skip_group_check=True)
                    ins.then_inc(*m.scattered.tick(0))
                s.unit, s.turns = unit, pe.snap(start + passes * turns)
                for b in range(8):
                    owner[b] = dve_ready.at(("moe_out", L))

            pe.wait_ge(*consts_in.at("consts"))
            for L in range(DEPTH):
                turn(("h", L), X, DC, [dve_ready.at("ln0" if L == 0 else ("ln2", 0))])
                pe.wait_ge(*turn_lo.at((("h", L), 3)))
                linear(f"w_in{L}")
                turn(("qk", L), U[:, :, 768:1792], 8, [dve_ready.at(("rope", L))], low=False)
                pe.wait_ge(*turn_hi.at((("qk", L), 3)))
                rounds = [(qb, 2, 2, 2, PA, ATA) for qb in range(TB) for _ in range(2)]

                def score(r, i, out):
                    qb, h, c = r // 2, 2 * (r % 2) + i // 2, i % 2
                    part = slice(64 * c, 64 * c + 64)
                    return pe.matmul(out, QKT[part, h, qb * P:(qb + 1) * P], QKT[part, 4 + h, :], start=True, stop=True)

                def value(r, h, kb):
                    a = 1792 + (2 * (r % 2) + h) * P
                    return U[:, kb, a:a + P]

                attention(("att", L), rounds, score, value)
                pe.wait_ge(*params_in["hy"].at(L))
                for g in range(4):
                    b = 4 + g // 2
                    if g % 2 == 0:
                        claim(b)
                    for kb in range(TB):
                        ins = pe.matmul(BK[b][0:64, (g % 2) * T:(g % 2) * T + T], U[:, kb, 2304 + 64 * g:2368 + 64 * g],
                                        BAND[:, kb, g, :], start=kb == 0, stop=kb == 1)
                    if g % 2:
                        ins.then_inc(*small_ready.tick(("pool", L, g // 2)))
                        owner[b] = act_ready.at(("pool", L, g // 2))
                for q in range(2):
                    pe.wait_ge(*act_ready.at(("pool", L, q)))
                claim(6)
                for tb in range(TB):
                    for g in range(4):
                        ins = pe.matmul(BK[6][:, tb * 256 + g * 64:tb * 256 + g * 64 + 64],
                                        YPT[:, g, tb * P:(tb + 1) * P], PW[:, g, :], start=True, stop=True)
                ins.then_inc(*small_ready.tick(("pool2", L)))
                owner[6] = dve_ready.at(("pool", L))
                claim(7)
                pe.wait_ge(*params_in["hy2"].at(L))
                pe.matmul(BK[7][0:64, 0:T], FW1[:, :], ZT[:, :], start=True, stop=True)\
                    .then_inc(*small_ready.tick(("f1", L)))
                pe.wait_ge(*act_ready.at(("sin1", L)))
                pe.matmul(BK[7][0:64, T:2 * T], FW2[:, :], H1[:, :], start=True, stop=True)\
                    .then_inc(*small_ready.tick(("f2", L)))
                pe.wait_ge(*act_ready.at(("sin2", L)))
                claim(4, 5)
                for tb in range(TB):
                    ins = pe.matmul(BK[4 + tb][:, :], H2[:, tb * P:(tb + 1) * P], FW3[:, :], start=True, stop=True)
                ins.then_inc(*small_ready.tick(("f3", L)))
                owner[4] = owner[5] = dve_ready.at(("filt", L))
                pe.wait_ge(*act_ready.at(("fsq", L)))
                claim(0)
                for tb in range(TB):
                    ins = pe.matmul(BK[0][:, :], ONES, YF[:, 2 * tb:2 * tb + 2, :].rearrange("p a b -> p (a b)"),
                                    start=tb == 0, stop=tb == 1)
                ins.then_inc(*small_ready.tick(("energy", L)))
                pe.wait_ge(*dve_ready.at(("fnorm", L)))
                claim(4, 5, 6)

                def spectrum(out, mat, cols, rhs):
                    for kb in range(2):
                        ins = pe.matmul(out, mat[:, kb, cols], rhs(kb), start=kb == 0, stop=kb == 1)
                    return ins

                fsum, fdif = (lambda kb: FF[:, kb, 0:HY]), (lambda kb: FF[:, kb, HY:2 * HY])
                b0, b1 = slice(0, P), slice(P, 2 * P)
                spectrum(BK[4][:, 0:HY], DC_, b0, fsum)
                spectrum(BK[4][:, HY:2 * HY], DC_, b1, fsum)
                spectrum(BK[5][:, 0:HY], DS0, b0, fdif)
                spectrum(BK[5][:, HY:2 * HY], DS_, b1, fdif)
                spectrum(BK[6][:, 0:HY], DC2, b0, fsum).then_inc(*small_ready.tick(("kspec", L)))
                owner[4] = owner[5] = owner[6] = dve_ready.at(("kspec", L))
                pe.wait_ge(*pool_ready.at(("conv", L)))
                claim(1, 2)
                vv = lambda kb: VV[:, kb, :]
                spectrum(BK[1][:, 0:HY], DC_, b0, vv)
                spectrum(BK[1][:, HY:2 * HY], DC_, b1, vv)
                spectrum(BK[2][:, 0:HY], DS_, b0, vv)
                spectrum(BK[2][:, HY:2 * HY], DS_, b1, vv).then_inc(*small_ready.tick(("vspec", L)))
                pe.wait_ge(*dve_ready.at(("yspec", L)))
                owner[1] = owner[2] = dve_ready.at(("yspec", L))
                claim(3)
                for tb in range(TB):
                    for k in range(4):
                        ins = pe.matmul(BK[3][:, tb * HY:(tb + 1) * HY], INV[:, k, tb * P:(tb + 1) * P], YF[:, k, :],
                                        start=k == 0, stop=k == 3)
                ins.then_inc(*small_ready.tick(("conv", L)))
                owner[0] = owner[7] = owner[3] = dve_ready.at(("cat", L))
                turn(("cat", L), CAT8, 8, [dve_ready.at(("cat", L))])
                pe.wait_ge(*turn_lo.at((("cat", L), 3)))
                linear(f"w_out{L}")
                turn(("h1", L), X, DC, [dve_ready.at(("ln1", L))])
                pe.wait_ge(*turn_lo.at((("h1", L), 3)))
                experts(L)

            turn("mem", Y, DC, [dve_ready.at("memn")])
            pe.wait_ge(*turn_lo.at(("mem", 3)))
            linear("mem")
            turn("mk", U[:, :, 0:512], 4, [dve_ready.at("mk")], low=False)

            def mem_attention(L, qt, probs, at_):
                rounds = [(qb, 2, 4, 1, probs, at_) for qb in range(TB)]
                attention(("mem", L), rounds,
                          lambda r, i, out: pe.matmul(out, qt[:, i, r * P:(r + 1) * P], MKT[:, i, :],
                                                      start=True, stop=True),
                          lambda r, h, kb: MV_[:, kb, h * P:(h + 1) * P])

            turn(("n1", 2), Y, DC, [dve_ready.at(("norm1", 2))])
            pe.wait_ge(*turn_lo.at((("n1", 2), 3)))
            linear("a_in")
            pe.wait_ge(*params_in["ws"].at(0))
            for g in range(2):
                claim(4 + g)
                for k in range(4):
                    ins = pe.transpose(BK[4 + g][:, k * P:(k + 1) * P], WSR[:, 4 * g + k, :], IDENT)
                ins.then_inc(*small_ready.tick(("ws", g)))
                owner[4 + g] = dve_ready.at(("ws", g))
            turn(("qm", 2), UV[:, :, 2048:2560], 4, [dve_ready.at(("qm", 2))], low=False)
            pe.wait_ge(*turn_hi.at((("qm", 2), 1)))
            mem_attention(2, QMT, PB, ATB)
            pe.wait_ge(*dve_ready.at(("ws", 1)))
            pe.wait_ge(*dve_ready.at("aln"))
            for g in range(8):
                b = g // 2
                if g % 2 == 0:
                    claim(b)
                ins = pe.matmul(BK[b][:, (g % 2) * T:(g % 2) * T + T], WST[:, g, :],
                                UV[:, :, D + g * P:D + (g + 1) * P], start=True, stop=True)
                if g % 2:
                    ins.then_inc(*small_ready.tick(("spatial", g // 2)))
                    owner[b] = dve_ready.at(("spatial", g // 2))
            turn(("cat", 2), CAT12, 12, [dve_ready.at(("cat", 2))])
            pe.wait_ge(*turn_lo.at((("cat", 2), 5)))
            linear("a_out")
            turn(("h1", 2), Y, DC, [dve_ready.at(("norm2", 2))])
            pe.wait_ge(*turn_lo.at((("h1", 2), 3)))
            experts(2)

            turn(("n1", 3), Y, DC, [dve_ready.at(("norm1", 3))])
            pe.wait_ge(*turn_lo.at((("n1", 3), 3)))
            linear("b_in")
            turn("cq", ZB[:, :, 0:512], 4, [dve_ready.at("bq")])
            pe.wait_ge(*turn_lo.at(("cq", 1)))
            linear("q_up")
            turn("ckv", ZB[:, :, 512:768], 2, [])
            pe.wait_ge(*turn_lo.at(("ckv", 0)))
            linear("kv_up")
            turn(("qm", 3), ZB[:, :, 832:1344], 4, [dve_ready.at(("qm", 3))], low=False)
            pe.wait_ge(*turn_hi.at((("qm", 3), 1)))
            mem_attention(3, QMT2, PC, ATC)
            pe.wait_ge(*dve_ready.at("qkn"))
            n = 0
            for what, src, rot in (("q", lambda h: QQ[:, :, 192 * h:192 * h + P], lambda h: QQ[:, :, 192 * h + P:192 * h + 192]),
                                   ("k", lambda h: KV[:, :, 256 * h:256 * h + P], lambda h: KRP[:, :, 64 * h:64 * h + 64])):
                for h2 in range(4):
                    for part, f in (("n", src), ("r", rot)):
                        b = 4 + n % 2
                        n += 1
                        claim(b)
                        rowsn = P if part == "n" else 64
                        for h in range(2):
                            for tb in range(TB):
                                ins = pe.transpose(BK[b][0:rowsn, h * T + tb * P:h * T + tb * P + P],
                                                   f(2 * h2 + h)[:, tb, :], IDENT)
                        ins.then_inc(*turned.tick((what, part, h2)))
                        owner[b] = turn_hi.at((what, part, h2))
            pe.wait_ge(*turn_hi.at(("k", "r", 3)))
            rounds = [(qb, qb + 1, 4, 1, PC, ATC) for qb in range(TB) for _ in range(2)]

            def mla_score(r, i, out):
                qb, h, w = r // 2, 4 * (r % 2) + i, P * (r // 2 + 1)
                pe.matmul(out, QTN[:, h, qb * P:(qb + 1) * P], KTN[:, h, 0:w], start=True, stop=False)
                return pe.matmul(out, QTR[:, h, qb * P:(qb + 1) * P], KTR[:, h, 0:w], start=False, stop=True)

            def mla_value(r, h, kb):
                a = 256 * (4 * (r % 2) + h) + P
                return KV[:, kb, a:a + P]

            attention(("mla", 3), rounds, mla_score, mla_value)
            turn(("cat", 3), CAT12B, 12, [dve_ready.at(("cat", 3))])
            pe.wait_ge(*turn_lo.at((("cat", 3), 5)))
            linear("b_out")
            turn(("h1", 3), Y, DC, [dve_ready.at(("norm2", 3))])
            pe.wait_ge(*turn_lo.at((("h1", 3), 3)))
            experts(3)

        @block.scalar
        def _(act):
            s = Stream()
            ch = Chain(act, chain_sem["act"])

            def split(width=UNIT):
                act.wait_ge(raw_in[s.slot()], s.landed())
                if not s.early(1 - PARTS):
                    act.wait_ge(unit_used, s.count(1 - PARTS))
                act.activation(WH[:, s.part(), 0:width], RAW[:, s.slot(), 0:width], ACT.Copy).then_inc(hi_done, 1)
                s.unit += 1

            def turn(key, chunks, dst, free=None):
                if free is not None:
                    act.wait_ge(*free)
                for g in range(chunks // 2):
                    act.wait_ge(*turned.at((key, g)))
                    act.activation(dst[:, 2 * g:2 * g + 2, :],
                                   BK[4 + g % 2][:, :].rearrange("p (c t) -> p c t", c=2), ACT.Copy)\
                       .then_inc(*turn_hi.tick((key, g)))

            def linear(key, evac):
                chunks, strips, per_unit = linear_shape(key)
                ends = []

                def ahead(i):
                    for _ in range(chunks // per_unit):
                        split(per_unit * strips[i][1])
                    ends.append(s.count(0))
                ahead(0)
                for i, (n0, width) in enumerate(strips):
                    if i + 1 < len(strips):
                        ahead(i + 1)
                    act.wait_ge(unit_used, ends[i])
                    if width > 512:
                        evac(n0, 512, BK[0])
                        evac(n0 + 512, 512, BK[1]).then_inc(*evac_a.tick((key, i)))
                    else:
                        evac(n0, width, BK[2 * (i % 2)]).then_inc(*evac_a.tick((key, i)))

            def copy_to(dst):
                return lambda n0, w, bank: act.activation(dst[:, 0, n0:n0 + w], bank[:, 0:w], ACT.Copy)

            def root(key, n):
                act.wait_ge(*dve_ready.at(("var", key)))
                act.activation(RT[:, 0:n], RS[:, 0:n], ACT.Sqrt).then_inc(*act_ready.tick(("root", key)))

            def attention(key, rounds, scale):
                for r, (qb, kbs, heads, step, probs, at_) in enumerate(rounds):
                    act.wait_ge(*negmax_ready.at((key, r)))
                    if r:
                        act.wait_ge(*pturned.at((key, r - 1)))
                    for i in range(4):
                        b = BK[2 * (r % 2) + i % 2]
                        ins = act.activation(probs[:, i, 0:P * kbs], b[:, (i // 2) * T:(i // 2) * T + P * kbs], ACT.Exp,
                                             bias=NM[:, i:i + 1], scale=scale, accum_out=SU[:, i:i + 1])
                        ch.go(ins)
                    ch.sync()
                    act.nop().then_inc(*probs_ready.tick((key, r)))
                    act.wait_ge(*pturned.at((key, r)))
                    if r:
                        act.wait_ge(*heads_ready.at((key, r - 1)))
                    n = heads * kbs
                    for b in range((n + 3) // 4):
                        k = min(4, n - 4 * b)
                        ch.go(act.activation(at_[:, 4 * b:4 * b + k, :],
                                             BK[4 + b][:, 0:k * P].rearrange("p (c t) -> p c t", t=P), ACT.Copy))
                    ch.sync()
                    act.nop().then_inc(*at_ready.tick((key, r)))

            def experts(L):
                m = moe_signals[L]
                E = EPG[L]
                turns = E * 3 // TURN
                src = X if L < DEPTH else Y
                act.wait_ge(*dve_ready.at(("ln1", L) if L < DEPTH else ("norm2", L)))
                act.wait_ge(*params_in["route"].at(L))
                act.activation(RWH[:, :, 0:NR[L]], RW[:, :, 0:NR[L]], ACT.Copy).then_inc(*act_ready.tick(("rwh", L)))
                act.activation(HH[:, :, :], src[:, :, :], ACT.Copy).then_inc(*act_ready.tick(("hh", L)))
                turn(("h1", L), DC, TH)
                act.wait_ge(*dve_ready.at(("diffs", L)))
                act.activation(r1[:, :, 0:4], r2[:, :, 0:4], ACT.Exp).then_inc(*act_ready.tick(("exp4", L)))
                act.wait_ge(*dve_ready.at(("diff2", L)))
                act.activation(v[1][:, :], v[0][:, :], ACT.Exp).then_inc(*act_ready.tick(("exp2", L)))
                if L < DEPTH:
                    turn(("p", L), 2, PTH)

                    def sig(n0, w, bank):
                        act.wait_ge(*evac_d.at((f"ple_g{L}", n0 // 512)))
                        ch.do(act.activation(SG[:, 0, n0:n0 + w], SG[:, 0, n0:n0 + w], ACT.Sigmoid))
                        return act.activation(SG[:, 1, n0:n0 + w], SG[:, 1, n0:n0 + w], ACT.Sigmoid)
                    linear(f"ple_g{L}", sig)
                    linear(f"ple_p{L}", lambda n0, w, bank: act.activation(Y[:, 0, n0:n0 + w], bank[:, 0:w], ACT.Copy))
                act.wait_ge(*dve_ready.at(("table", L)))
                passes = act.value_load(TAB[0:1, 0:1], min_val=4, max_val=5)
                start, unit = s.turns, s.unit
                with act.Fori(0, passes) as p:
                    s.unit, s.turns = unit, start + p * turns
                    split()
                    split()
                    for q in range(2):
                        act.wait_ge(*m.gathered.at(p, q))
                        act.activation(XH[:, 4 * q:4 * q + 4, :], BK[6 + q][:, :].rearrange("p (c t) -> p c t", t=P),
                                       ACT.Copy).then_inc(*m.xh.tick(q))
                    split()
                    for e in range(E):
                        act.wait_ge(unit_used, s.count(-1))
                        act.activation(SIL[:, :], BK[6][:, 0:256], ACT.Silu).then_inc(*m.silu.tick(e))
                        if e + 1 < E:
                            split()
                        act.wait_ge(*m.at.at(p, e))
                        act.activation(AH[:, :, :], BK[7][:, 0:256].rearrange("p (c t) -> p c t", t=P), ACT.Copy)\
                           .then_inc(*m.ah.tick(e))
                        if e + 1 < E:
                            split()
                            if e + 2 < E:
                                split()
                        else:
                            split()
                    act.wait_ge(unit_used, s.count(0))
                    for half in range(2):
                        act.activation(YH[:, half * 512:half * 512 + 512], BK[4 + half][:, :], ACT.Copy)\
                           .then_inc(*m.yh.tick(half))
                s.unit, s.turns = unit, act.snap(start + passes * turns)

            root("ln0", 2)
            for L in range(DEPTH):
                turn(("h", L), DC, TH)
                linear(f"w_in{L}", copy_to(U))
                act.wait_ge(*evac_d.at((f"w_in{L}", 4)))
                turn(("qk", L), 8, QKT)
                act.wait_ge(*dve_ready.at(("lamd", L)))
                act.activation(LAM[:, 2:4], LAM[:, 0:2], ACT.Exp).then_inc(*act_ready.tick(("lam", L)))
                attention(("att", L), [(qb, 2, 2, 2, PA, ATA) for qb in range(TB) for _ in range(2)], 64 ** -0.5)
                for q in range(2):
                    act.wait_ge(*small_ready.at(("pool", L, q)))
                    act.activation(YPT[:, 2 * q:2 * q + 2, :], BK[4 + q][0:64, :].rearrange("p (c t) -> p c t", c=2),
                                   ACT.Copy).then_inc(*act_ready.tick(("pool", L, q)))
                for i, h in ((1, H1), (2, H2)):
                    act.wait_ge(*dve_ready.at((f"arg{i}", L)))
                    act.activation(h[:, :], ARG[:, :], ACT.Sin, scale=6.2831845).then_inc(*act_ready.tick((f"sin{i}", L)))
                act.wait_ge(*dve_ready.at(("filt", L)))
                act.activation(YF[:, :, :].rearrange("p (a b) c -> p a (b c)", a=2), FF[:, :, :], ACT.Square)\
                    .then_inc(*act_ready.tick(("fsq", L)))
                act.wait_ge(*dve_ready.at(("energy", L)))
                act.activation(PA[:, 0, :], PA[:, 0, :], ACT.Sqrt).then_inc(*act_ready.tick(("energy", L)))
                for qb in range(TB):
                    root(("subln", L, qb), 4)
                turn(("cat", L), 8, TH)
                linear(f"w_out{L}", copy_to(Y))
                root(("ln1", L), 2)
                experts(L)
                root(("ln2", L), 2)
            root("memn", 2)
            turn("mem", DC, TH)
            linear("mem", copy_to(U))
            root("mk", 8)
            act.wait_ge(*evac_d.at(("mem", 1)))
            for g in range(2):
                act.wait_ge(*turned.at(("mk", g)))
                act.activation(MKT[:, 2 * g:2 * g + 2, :], BK[4 + g][:, :].rearrange("p (c t) -> p c t", c=2), ACT.Copy)\
                   .then_inc(*turn_hi.tick(("mk", g)))
            root(("n1", 2), 2)

            def mem_attention(L, qt, probs, at_):
                root(("qm", L), 8)
                for g in range(2):
                    act.wait_ge(*turned.at((("qm", L), g)))
                    act.activation(qt[:, 2 * g:2 * g + 2, :], BK[4 + g][:, :].rearrange("p (c t) -> p c t", c=2),
                                   ACT.Copy, scale=MEMG[:, L - 2:L - 1]).then_inc(*turn_hi.tick((("qm", L), g)))
                attention(("mem", L), [(qb, 2, 4, 1, probs, at_) for qb in range(TB)], P ** -0.5)

            turn(("n1", 2), DC, TH)

            def gelu(n0, w, bank):
                f = ACT.Gelu if n0 < 2 * D else ACT.Copy
                other = BK[BK.index(bank) + 1]
                ch.do(act.activation(UV[:, 0, n0:n0 + w], bank[:, 0:w], f))
                return act.activation(UV[:, 1, n0:n0 + w], other[:, 0:w], f)
            linear("a_in", gelu)
            mem_attention(2, QMT, PB, ATB)
            root("aln", 2)
            turn(("cat", 2), 12, TH)
            linear("a_out", copy_to(Y))
            root(("n2", 2), 2)
            experts(2)
            root(("n1", 3), 2)
            turn(("n1", 3), DC, TH)
            linear("b_in", copy_to(ZB))
            root("bq", 4)
            turn("cq", 4, TH)
            linear("q_up", copy_to(QQ))
            turn("ckv", 2, TH)
            linear("kv_up", copy_to(KV))
            mem_attention(3, QMT2, PC, ATC)
            act.wait_ge(*dve_ready.at("angles"))
            ch.do(act.activation(TRIG[:, 0:2, :, :], TRIG[:, 2:4, :, :], ACT.Sin, scale=6.2831845))
            act.nop().then_inc(*act_ready.tick("trig"))
            for b in range(2):
                root(("qkn", b), 16)
            n = 0
            for what, dn, dr in (("q", QTN, QTR), ("k", KTN, KTR)):
                for h2 in range(4):
                    for part, dst, rowsn in (("n", dn, P), ("r", dr, 64)):
                        act.wait_ge(*turned.at((what, part, h2)))
                        act.activation(dst[0:rowsn, 2 * h2:2 * h2 + 2, :],
                                       BK[4 + n % 2][0:rowsn, :].rearrange("p (c t) -> p c t", c=2), ACT.Copy)\
                           .then_inc(*turn_hi.tick((what, part, h2)))
                        n += 1
            attention(("mla", 3), [(qb, qb + 1, 4, 1, PC, ATC) for qb in range(TB) for _ in range(2)], 192 ** -0.5)
            turn(("cat", 3), 12, TH)
            linear("b_out", copy_to(Y))
            root(("n2", 3), 2)
            experts(3)


        @block.vector
        def _(dve):
            s = Stream()
            ch = Chain(dve, chain_sem["dve"])
            go, do, sync = ch.go, ch.do, ch.sync

            def done(key):
                sync()
                dve.nop().then_inc(*dve_ready.tick(key))

            def bc(ap, shape):
                return ap.to_broadcast(shape)

            def split(width=UNIT):
                dve.wait_ge(hi_done, s.count(1))
                dve.tensor_tensor(WL[:, s.part(), 0:width], RAW[:, s.slot(), 0:width],
                                  WH[:, s.part(), 0:width].bitcast(F32), ALU.subtract).then_inc(split_done, 1)
                s.unit += 1

            def turn(key, chunks, dh, dl):
                for g in range(chunks // 2):
                    dve.wait_ge(*turn_hi.at((key, g)))
                    dve.tensor_tensor(dl[:, 2 * g:2 * g + 2, :],
                                      BK[4 + g % 2][:, :].rearrange("p (c t) -> p c t", c=2),
                                      dh[:, 2 * g:2 * g + 2, :].bitcast(F32), ALU.subtract)\
                       .then_inc(*turn_lo.tick((key, g)))

            def linear(key, evac):
                chunks, strips, per_unit = linear_shape(key)
                ends = []

                def ahead(i):
                    for _ in range(chunks // per_unit):
                        split(per_unit * strips[i][1])
                    ends.append(s.count(0))
                ahead(0)
                for i, (n0, width) in enumerate(strips):
                    if i + 1 < len(strips):
                        ahead(i + 1)
                    dve.wait_ge(unit_used, ends[i])
                    if width > 512:
                        do(evac(n0, 512, BK[2]))
                        evac(n0 + 512, 512, BK[3]).then_inc(*evac_d.tick((key, i)))
                    else:
                        evac(n0, width, BK[2 * (i % 2) + 1]).then_inc(*evac_d.tick((key, i)))

            def copy_to(dst):
                return lambda n0, w, bank: dve.tensor_copy(dst[:, 1, n0:n0 + w], bank[:, 0:w])

            def stats(src, n, width, i):
                for k in range(n):
                    c = max(1, width // 512)
                    for j in range(c):
                        a = k * width + j * min(width, 512)
                        go(dve.bn_stats(NST[:, j, :], src[:, a:a + min(width, 512)]))
                    sync()
                    do(dve.bn_aggr(MV[:, i + k, :], NST[:, 0:c, :]))

            def inverse_root(key, n, rms, eps, gain=1.0):
                if rms:
                    do(dve.tensor_tensor(RS[:, 0:n], MV[:, 0:n, 0], MV[:, 0:n, 0], ALU.mult))
                    do(dve.tensor_tensor(RS[:, 0:n], RS[:, 0:n], MV[:, 0:n, 1], ALU.add))
                    do(dve.tensor_scalar(RS[:, 0:n], RS[:, 0:n], eps, None, ALU.add))
                else:
                    do(dve.tensor_scalar(RS[:, 0:n], MV[:, 0:n, 1], eps, None, ALU.add))
                finish_root(key, n, gain)

            def finish_root(key, n, gain=1.0):
                dve.nop().then_inc(*dve_ready.tick(("var", key)))
                dve.wait_ge(*act_ready.at(("root", key)))
                do(dve.reciprocal(RS[:, 0:n], RT[:, 0:n]))
                if gain != 1.0:
                    do(dve.tensor_scalar(RS[:, 0:n], RS[:, 0:n], gain, None, ALU.mult))

            def layer_norm(key, buf, eps, rows_key, width=D, at=0):
                for tb in range(TB):
                    stats(buf[:, tb, at:at + width], 1, width, tb)
                inverse_root(key, TB, False, eps)
                dve.wait_ge(*rows_in.at(rows_key))
                for tb in range(TB):
                    go(dve.tensor_scalar(buf[:, tb, at:at + width], buf[:, tb, at:at + width], MV[:, tb, 0:1],
                                         RS[:, tb:tb + 1], ALU.subtract, ALU.mult))
                sync()
                for slot, op in ((0, ALU.mult), (1, ALU.add)):
                    for tb in range(TB):
                        go(dve.tensor_tensor(buf[:, tb, at:at + width], buf[:, tb, at:at + width], ROW[:, slot, 0:width], op))
                    sync()

            def rms_norm(key, dst, src, rows_key, slot):
                for tb in range(TB):
                    stats(src[:, tb, :], 1, D, tb)
                inverse_root(key, TB, True, EPS)
                dve.wait_ge(*rows_in.at(rows_key))
                for tb in range(TB):
                    go(dve.scalar_tensor_tensor(dst[:, tb, :], src[:, tb, :], RS[:, tb:tb + 1], ROW[:, slot, 0:D],
                                                ALU.mult, ALU.mult))
                sync()

            def attention(key, rounds, scale, cat, col, diff=False, causal=False):
                def negmax(r):
                    qb, kbs = rounds[r][0:2]
                    dve.wait_ge(*scores_ready.at((key, r)))
                    w = P * kbs
                    for b in range(2):
                        ps = BK[2 * (r % 2) + b][:, :].rearrange("p (c t) -> p c t", c=2)
                        if causal:
                            do(dve.tensor_tensor(ps[:, :, w - P:w], ps[:, :, w - P:w],
                                                 bc(CMASK.unsqueeze(1), [P, 2, P]), ALU.add))
                        do(dve.tensor_reduce(MX[:, b:4:2], ps[:, :, 0:w], X_AXIS, ALU.max))
                    dve.tensor_scalar(NM[:, 0:4], MX[:, 0:4], -scale, None, ALU.mult)\
                       .then_inc(*negmax_ready.tick((key, r)))

                negmax(0)
                for r, (qb, kbs, heads, step, probs, at_) in enumerate(rounds):
                    dve.wait_ge(*probs_ready.at((key, r)))
                    if r:
                        dve.wait_ge(*heads_taken.at((key, r - 1)))
                    do(dve.reciprocal(RC[:, 0:4], SU[:, 0:4]))
                    if diff:
                        do(dve.tensor_scalar(RC[:, 1:4:2], RC[:, 1:4:2], LAM[:, 4:5], None, ALU.mult))
                        for h in range(2):
                            go(dve.tensor_scalar(probs[:, 2 * h, :], probs[:, 2 * h, :], RC[:, 2 * h:2 * h + 1], None,
                                                 ALU.mult))
                        sync()
                        for h in range(2):
                            go(dve.scalar_tensor_tensor(probs[:, 2 * h, :], probs[:, 2 * h + 1, :],
                                                        RC[:, 2 * h + 1:2 * h + 2], probs[:, 2 * h, :],
                                                        ALU.mult, ALU.add))
                        sync()
                    dve.nop().then_inc(*weights_ready.tick((key, r)))
                    if r + 1 < len(rounds):
                        negmax(r + 1)
                    dve.wait_ge(*heads_ready.at((key, r)))
                    bank = BK[6 + r % 2]
                    a = col + (r * heads % 4 if diff else 4 * (r % 2) if causal else 0) * P
                    n = heads * P
                    if diff:
                        ins = dve.tensor_copy(cat[:, qb, a:a + n], bank[:, 0:n])
                    else:
                        ins = dve.tensor_tensor(cat[:, qb, a:a + n].rearrange("p (h c) -> p h c", c=P),
                                                bank[:, 0:n].rearrange("p (h c) -> p h c", c=P),
                                                bc(RC[:, 0:heads].unsqueeze(2), [P, heads, P]), ALU.mult)
                    ins.then_inc(*heads_taken.tick((key, r)))
                dve.wait_ge(*heads_taken.at((key, len(rounds) - 1)))

            def first_best(score, n, pri, out, m, t):
                full = [P, TB, n]
                do(dve.tensor_reduce(m, score, X_AXIS, ALU.max))
                do(dve.tensor_tensor(t, score, bc(m.unsqueeze(2), full), ALU.is_equal))
                do(dve.tensor_tensor(t, t, bc(pri.unsqueeze(1), full), ALU.mult))
                do(dve.tensor_reduce(v[11][:, :], t, X_AXIS, ALU.max))
                do(dve.tensor_tensor(out, t, bc(v[11][:, :].unsqueeze(2), full), ALU.is_equal))

            def experts(L):
                m = moe_signals[L]
                E = EPG[L]
                turns = E * 3 // TURN
                src = X if L < DEPTH else Y
                do(dve.memset(ZR[:, :].bitcast(F32), 0.0))
                dve.wait_ge(*params_in["route"].at(L))
                dve.wait_ge(*act_ready.at(("rwh", L)))
                do(dve.tensor_tensor(RWL[:, :, 0:NR[L]], RW[:, :, 0:NR[L]], RWH[:, :, 0:NR[L]].bitcast(F32), ALU.subtract))
                done(("rw", L))
                dve.wait_ge(*act_ready.at(("hh", L)))
                do(dve.tensor_tensor(HL[:, :, :], src[:, :, :], HH[:, :, :].bitcast(F32), ALU.subtract))
                turn(("h1", L), DC, TH, TL)
                dve.wait_ge(*small_ready.at(("logits", L)))
                full = [P, TB, E]
                for tb in range(TB):
                    go(dve.tensor_tensor(LG[:, tb, 0:NR[L]], BK[6][:, tb * 64:tb * 64 + NR[L]], RB[:, 0:NR[L]], ALU.add))
                sync()
                V = [x[:, :] for x in v]
                first_best(LG[:, :, 0:4], 4, PRI4, OH4[:, :, :], V[2], r1[:, :, 0:4])
                done(("onehot", L))
                do(dve.tensor_tensor(r2[:, :, 0:4], LG[:, :, 0:4], bc(V[2].unsqueeze(2), [P, TB, 4]), ALU.subtract))
                done(("diffs", L))
                for tb in range(TB):
                    go(dve.tensor_tensor(r3[:, tb, 0:4 * E].rearrange("p (g e) -> p g e", g=4),
                                         LG[:, tb, 4:4 + 4 * E].rearrange("p (g e) -> p g e", g=4),
                                         bc(OH4[:, tb, :].unsqueeze(2), [P, 4, E]), ALU.mult))
                sync()
                for tb in range(TB):
                    go(dve.tensor_reduce(FS[:, tb, 0:E], r3[:, tb, 0:4 * E].rearrange("p (g e) -> p e g", g=4), X_AXIS, ALU.add))
                sync()
                pri = PRI4 if E == 4 else PRI8
                dve.wait_ge(*act_ready.at(("exp4", L)))
                do(dve.tensor_reduce(V[4], r1[:, :, 0:4], X_AXIS, ALU.add))
                first_best(FS[:, :, 0:E], E, pri, OH1[:, :, 0:E], V[2], r4[:, :, 0:E])
                do(dve.scalar_tensor_tensor(FS[:, :, 0:E], OH1[:, :, 0:E], -1e30, FS[:, :, 0:E], ALU.mult, ALU.add))
                first_best(FS[:, :, 0:E], E, pri, OH2[:, :, 0:E], V[3], r4[:, :, 0:E])
                do(dve.tensor_tensor(V[0], V[3], V[2], ALU.subtract))
                done(("diff2", L))
                do(dve.reciprocal(V[4], V[4]))
                dve.wait_ge(*act_ready.at(("exp2", L)))
                do(dve.tensor_scalar(V[5], V[1], 1.0, None, ALU.add))
                do(dve.reciprocal(V[5], V[5]))
                do(dve.tensor_tensor(V[5], V[5], V[4], ALU.mult))
                do(dve.tensor_tensor(V[6], V[5], V[1], ALU.mult))
                do(dve.tensor_tensor(OH1[:, :, 0:E], OH1[:, :, 0:E], bc(V[5].unsqueeze(2), full), ALU.mult))
                do(dve.tensor_tensor(OH2[:, :, 0:E], OH2[:, :, 0:E], bc(V[6].unsqueeze(2), full), ALU.mult))
                if E < 8:
                    do(dve.memset(FS[:, :, E:8], 0.0))
                do(dve.tensor_tensor(FS[:, :, 0:E], OH1[:, :, 0:E], OH2[:, :, 0:E], ALU.add))
                do(dve.tensor_copy(GH[:, :, :], FS[:, :, :]))
                do(dve.tensor_tensor(GL[:, :, :], FS[:, :, :], GH[:, :, :].bitcast(F32), ALU.subtract))
                dve.wait_ge(*small_ready.at(("ranks", L)))
                do(dve.tensor_tensor(r1[:, :, 0:4], BK[7][:, 0:8].rearrange("p (t g) -> p t g", g=4), OH4[:, :, :], ALU.mult))
                do(dve.tensor_reduce(V[7], r1[:, :, 0:4], X_AXIS, ALU.add))
                do(dve.tensor_tensor(r1[:, :, 0:4], OH4[:, :, :], bc(IDX4.unsqueeze(1), [P, TB, 4]), ALU.mult))
                do(dve.tensor_reduce(V[8], r1[:, :, 0:4], X_AXIS, ALU.add))
                do(dve.tensor_scalar(V[8], V[8], 128.0, None, ALU.mult))
                do(dve.tensor_scalar(V[9], V[7], 128.0, None, ALU.is_ge))
                do(dve.tensor_scalar(V[10], V[8], -1.0, 384.0, ALU.mult, ALU.add))
                do(dve.tensor_tensor(V[10], V[10], V[9], ALU.mult))
                do(dve.tensor_tensor(V[7], V[7], V[8], ALU.add))
                do(dve.tensor_tensor(KEY[:, :], V[7], V[10], ALU.add))
                for tb in range(TB):
                    go(dve.tensor_scalar(DG[:, tb, :], IDENT, KEY[:, tb:tb + 1], None, ALU.mult))
                done(("diag", L))
                do(dve.tensor_copy(JP[:, 0:1], PCOL))
                do(dve.tensor_scalar(r2[:, 0, 0:4], BK[7][:, 8:12], 128.0, None, ALU.is_gt))
                do(dve.tensor_reduce(r2[:, 0, 4:5], r2[:, 0, 0:4], X_AXIS, ALU.add))
                do(dve.tensor_scalar(TABF[:, 0:1], r2[:, 0, 4:5], 4.0, None, ALU.add))
                do(dve.tensor_copy(TABF[:, 1:5], IDX4))
                do(dve.tensor_tensor(r2[:, 0, 0:4], r2[:, 0, 0:4], IDX4, ALU.mult))
                do(dve.tensor_reduce(TABF[:, 5:6], r2[:, 0, 0:4], X_AXIS, ALU.add))
                do(dve.tensor_copy(TAB[:, 0:6], TABF[:, 0:6]))
                dve.wait_ge(*small_ready.at(("keyrow", L)))
                do(dve.tensor_copy(PKROW[:, :], BK[6][:, 0:T]))
                done(("table", L))
                if L < DEPTH:
                    turn(("p", L), 2, PTH, PTL)
                    dve.wait_ge(*rows_in.at(("ple", L)))

                    def bias(n0, w, bank):
                        other = BK[BK.index(bank) - 1]
                        do(dve.tensor_tensor(SG[:, 0, n0:n0 + w], other[:, 0:w], ROW[:, 0, n0:n0 + w], ALU.add))
                        return dve.tensor_tensor(SG[:, 1, n0:n0 + w], bank[:, 0:w], ROW[:, 0, n0:n0 + w], ALU.add)
                    linear(f"ple_g{L}", bias)
                    sync()
                    dve.wait_ge(*evac_d.at((f"ple_g{L}", 1)))
                    done(("ple_b", L))
                    linear(f"ple_p{L}", copy_to(Y))
                    dve.wait_ge(*evac_a.at((f"ple_p{L}", 0)))
                    dve.wait_ge(*evac_d.at((f"ple_p{L}", 0)))
                    for tb in range(TB):
                        go(dve.tensor_tensor(Y[:, tb, :], Y[:, tb, :], SG[:, tb, :], ALU.mult))
                    sync()
                    for tb in range(TB):
                        go(dve.scalar_tensor_tensor(X[:, tb, :], X[:, tb, :], ALPHA, Y[:, tb, :], ALU.mult, ALU.add))
                    sync()
                passes = dve.value_load(TAB[0:1, 0:1], min_val=4, max_val=5)
                start, unit = s.turns, s.unit
                with dve.Fori(0, passes) as p:
                    s.unit, s.turns = unit, start + p * turns
                    lc = LoopChain(dve, m.chain, p, m.chain_values)
                    for tb in range(TB):
                        lc.go(dve.tensor_scalar(SP[:, tb, :], IOTA, KEY[:, tb:tb + 1], None, ALU.is_equal))
                    lc.do(dve.tensor_scalar(ST[:, :], PKROW[:, :], JP[:, 0:1], None, ALU.is_equal))
                    dve.nop().then_inc(*m.sel.tick("sel"))
                    lc.go(dve.tensor_scalar(KEY[:, :], KEY[:, :], -128.0, None, ALU.add))
                    lc.do(dve.tensor_scalar(JP[:, 0:1], JP[:, 0:1], 128.0, None, ALU.add))
                    split()
                    split()
                    for q in range(2):
                        dve.wait_ge(*m.xh.at(p, q))
                        if q == 1:
                            lc.go(dve.tensor_copy(GS[:, :], BK[4][:, 0:8]))
                            lc.sync()
                        dve.tensor_tensor(XL[:, 4 * q:4 * q + 4, :], BK[6 + q][:, :].rearrange("p (c t) -> p c t", t=P),
                                          XH[:, 4 * q:4 * q + 4, :].bitcast(F32), ALU.subtract).then_inc(*m.xl.tick(q))
                    split()
                    for e in range(E):
                        dve.wait_ge(*m.silu.at(p, e))
                        dve.scalar_tensor_tensor(GLU[:, :], SIL[:, :], GS[:, e:e + 1], BK[6][:, 256:512],
                                                 ALU.mult, ALU.mult).then_inc(*m.glu.tick(e))
                        if e + 1 < E:
                            split()
                        dve.wait_ge(*m.ah.at(p, e))
                        dve.tensor_tensor(AL[:, :, :], BK[7][:, 0:256].rearrange("p (c t) -> p c t", t=P),
                                          AH[:, :, :].bitcast(F32), ALU.subtract).then_inc(*m.al.tick(e))
                        if e + 1 < E:
                            split()
                            if e + 2 < E:
                                split()
                        else:
                            split()
                    for half in range(2):
                        dve.wait_ge(*m.yh.at(p, half))
                        a = slice(half * 512, half * 512 + 512)
                        dve.tensor_tensor(YL[:, a], BK[4 + half][:, :], YH[:, a].bitcast(F32), ALU.subtract)\
                           .then_inc(*m.yl.tick(half))
                    dve.wait_ge(*m.scattered.at(p, 0))
                s.unit, s.turns = unit, dve.snap(start + passes * turns)
                for tb in range(TB):
                    for half in range(2):
                        a = slice(half * 512, half * 512 + 512)
                        go(dve.tensor_tensor(X[:, tb, a], X[:, tb, a], BK[2 * tb + half][:, :], ALU.add))
                done(("moe_out", L))

            dve.wait_ge(*x_in.at("x"))
            layer_norm("ln0", X, LN_EPS, "ln0")
            done("ln0")
            for L in range(DEPTH):
                lam_init = (0.2, 0.8 - 0.6 * 0.7408182206817179)[L]
                turn(("h", L), DC, TH, TL)
                linear(f"w_in{L}", copy_to(U))
                dve.wait_ge(*evac_d.at((f"w_in{L}", 4)))
                dve.wait_ge(*evac_a.at((f"w_in{L}", 4)))
                for tb in range(TB):
                    qk = U[:, tb, 768:1792].rearrange("p (h c) -> p h c", c=64)
                    x1, x2 = qk[:, :, 0:8], qk[:, :, 8:16]
                    c = bc(COS8[:, tb * 8:tb * 8 + 8].unsqueeze(1), [P, 16, 8])
                    sn = bc(SIN8[:, tb * 8:tb * 8 + 8].unsqueeze(1), [P, 16, 8])
                    t = [PA[:, i, 0:128].rearrange("p (h c) -> p h c", c=8) for i in range(4)]
                    for o, a, b in ((0, x1, c), (1, x2, sn), (2, x1, sn), (3, x2, c)):
                        go(dve.tensor_tensor(t[o], a, b, ALU.mult))
                    sync()
                    go(dve.tensor_tensor(x1, t[0], t[1], ALU.subtract))
                    do(dve.tensor_tensor(x2, t[2], t[3], ALU.add))
                done(("rope", L))
                dve.wait_ge(*params_in["hy"].at(L))
                for i in range(2):
                    do(dve.tensor_tensor_reduce(PA[:, i, 0:64], LQ[:, 2 * i, :], LQ[:, 2 * i + 1, :], 1.0, 0.0,
                                                ALU.mult, ALU.add, LAM[:, i:i + 1]))
                done(("lamd", L))
                dve.wait_ge(*act_ready.at(("lam", L)))
                do(dve.tensor_tensor(LAM[:, 4:5], LAM[:, 3:4], LAM[:, 2:3], ALU.subtract))
                do(dve.tensor_scalar(LAM[:, 4:5], LAM[:, 4:5], -lam_init, None, ALU.add))
                attention(("att", L), [(qb, 2, 2, 2, PA, ATA) for qb in range(TB) for _ in range(2)], 64 ** -0.5,
                          CAT8, 256, diff=True)
                dve.wait_ge(*small_ready.at(("pool2", L)))
                for tb in range(TB):
                    go(dve.tensor_tensor(CAT8[:, tb, 768:1024], BK[6][:, tb * 256:tb * 256 + 256], SROW[:, 384:640], ALU.add))
                sync()
                for tb in range(TB):
                    go(dve.tensor_tensor(CAT8[:, tb, 768:1024], CAT8[:, tb, 768:1024], SROW[:, 640:896], ALU.mult))
                done(("pool", L))
                for i, (cb, cf) in ((1, (0, 1)), (2, (2, 3))):
                    dve.wait_ge(*small_ready.at((f"f{i}", L)))
                    ps = BK[7][0:64, (i - 1) * T:i * T]
                    do(dve.tensor_scalar(ARG[:, :], ps, HCOL[:, cb:cb + 1], HCOL[:, cf:cf + 1], ALU.add, ALU.mult))
                    do(dve.tensor_scalar(ARG[:, :], ARG[:, :], 1.0 / TWO_PI, None, ALU.mult))
                    do(dve.tensor_scalar(FR[:, :], ARG[:, :], ROUND, None, ALU.add))
                    do(dve.tensor_scalar(FR[:, :], FR[:, :], -ROUND, None, ALU.add))
                    do(dve.tensor_tensor(ARG[:, :], ARG[:, :], FR[:, :], ALU.subtract))
                    done((f"arg{i}", L))
                dve.wait_ge(*small_ready.at(("f3", L)))
                dve.wait_ge(*params_in["hy2"].at(L))
                for tb in range(TB):
                    for half in range(2):
                        a = slice(half * HY, (half + 1) * HY)
                        go(dve.tensor_tensor(FF[:, tb, a], BK[4 + tb][:, a], WIN[:, tb, :], ALU.mult))
                sync()
                do(dve.memset(FF[0:1, 0, HY:2 * HY], 0.0))
                done(("filt", L))
                dve.wait_ge(*small_ready.at(("energy", L)))
                do(dve.tensor_scalar(PA[:, 0, :], BK[0][:, 0:HY], 1e-6, None, ALU.add))
                do(dve.tensor_tensor(PA[:, 0, :], PA[:, 0, :], BK[0][:, HY:2 * HY], ALU.add))
                done(("energy", L))
                go(dve.tensor_tensor(PA[:, 1:3, :], FF[:, :, 0:HY], FF[:, :, HY:2 * HY], ALU.add))
                do(dve.tensor_tensor(FF[:, :, HY:2 * HY], FF[:, :, 0:HY], FF[:, :, HY:2 * HY], ALU.subtract))
                dve.wait_ge(*act_ready.at(("energy", L)))
                do(dve.reciprocal(PA[:, 3, :], PA[:, 0, :]))
                for src_, a in ((PA[:, 1:3, :], 0), (FF[:, :, HY:2 * HY], HY)):
                    go(dve.tensor_tensor(FF[:, :, a:a + HY], src_, bc(PA[:, 3, :].unsqueeze(1), [P, 2, HY]), ALU.mult))
                done(("fnorm", L))
                dve.wait_ge(*small_ready.at(("kspec", L)))
                dve.wait_ge(*pool_ready.at(("conv", L)))
                go(dve.tensor_copy(KR[:, :, :], BK[4][:, :].rearrange("p (b c) -> p b c", b=2)))
                go(dve.tensor_copy(KI[:, :, :], BK[5][:, :].rearrange("p (b c) -> p b c", b=2)))
                go(dve.tensor_copy(K2[:, 0, :], BK[6][:, 0:HY]))
                go(dve.tensor_copy(K2[:, 1, :], BK[4][:, HY:2 * HY]))
                done(("kspec", L))
                dve.wait_ge(*small_ready.at(("vspec", L)))
                vr = BK[1][:, :].rearrange("p (b c) -> p b c", b=2)
                vi = BK[2][:, :].rearrange("p (b c) -> p b c", b=2)
                go(dve.tensor_tensor(YF[:, 0:2, :], vr, KR[:, :, :], ALU.mult))
                go(dve.tensor_tensor(YF[:, 2:4, :], vr, KI[:, :, :], ALU.mult))
                go(dve.tensor_tensor(PA[:, 0:2, :], vi, KI[:, :, :], ALU.mult))
                go(dve.tensor_tensor(PA[:, 2:4, :], vi, K2[:, :, :], ALU.mult))
                sync()
                go(dve.tensor_tensor(YF[:, 0:2, :], YF[:, 0:2, :], PA[:, 0:2, :], ALU.subtract))
                go(dve.tensor_tensor(YF[:, 2:4, :], YF[:, 2:4, :], PA[:, 2:4, :], ALU.add))
                done(("yspec", L))
                for tb in range(TB):
                    go(dve.tensor_tensor(VV[:, tb, :], VV[:, tb, :], SROW[:, 0:HY], ALU.mult))
                sync()
                dve.wait_ge(*small_ready.at(("conv", L)))
                for tb in range(TB):
                    go(dve.tensor_tensor(VV[:, tb, :], VV[:, tb, :], BK[3][:, tb * HY:(tb + 1) * HY], ALU.add))
                sync()
                for tb in range(TB):
                    go(dve.tensor_tensor(CAT8[:, tb, 0:HY], VV[:, tb, :], UM[:, tb, 0:HY], ALU.mult))
                sync()
                for qb in range(TB):
                    stats(CAT8[:, qb, 256:768], 4, P, 0)
                    inverse_root(("subln", L, qb), 4, True, LN_EPS, 1.0 - lam_init)
                    hd = CAT8[:, qb, 256:768].rearrange("p (h c) -> p h c", c=P)
                    do(dve.tensor_tensor(hd, hd, bc(RS[:, 0:4].unsqueeze(2), [P, 4, P]), ALU.mult))
                    do(dve.tensor_tensor(hd, hd, bc(SROW[:, 256:384].unsqueeze(1), [P, 4, P]), ALU.mult))
                done(("cat", L))
                turn(("cat", L), 8, TH, TL)
                linear(f"w_out{L}", copy_to(Y))
                dve.wait_ge(*evac_d.at((f"w_out{L}", 1)))
                dve.wait_ge(*evac_a.at((f"w_out{L}", 1)))
                for tb in range(TB):
                    go(dve.scalar_tensor_tensor(X[:, tb, :], X[:, tb, :], ALPHA, Y[:, tb, :], ALU.mult, ALU.add))
                sync()
                layer_norm(("ln1", L), X, LN_EPS, ("ln1", L))
                done(("ln1", L))
                experts(L)
                layer_norm(("ln2", L), X, LN_EPS, ("ln2", L))
                done(("ln2", L))

            dve.wait_ge(*params_in["mem"].at(0))
            rms_norm("memn", Y, Y, "memg", 0)
            done("memn")
            turn("mem", DC, TH, TL)
            linear("mem", copy_to(U))
            dve.wait_ge(*evac_d.at(("mem", 1)))
            dve.wait_ge(*evac_a.at(("mem", 1)))

            def head_norm(key, src, done_key):
                for tb in range(TB):
                    stats(src(tb), 4, P, 4 * tb)
                inverse_root(key, 8, True, EPS)
                for tb in range(TB):
                    hd = src(tb).rearrange("p (h c) -> p h c", c=P)
                    go(dve.tensor_tensor(hd, hd, bc(RS[:, 4 * tb:4 * tb + 4].unsqueeze(2), [P, 4, P]), ALU.mult))
                done(done_key)

            for i in range(2):
                do(dve.tensor_tensor(MEMG[:, i:i + 1], GQK[:, 2 * i:2 * i + 1], GQK[:, 2 * i + 1:2 * i + 2], ALU.mult))
            head_norm("mk", lambda tb: U[:, tb, 0:512], "mk")
            for tb in range(TB):
                go(dve.tensor_copy(MV_[:, tb, :], U[:, tb, 512:1024]))
            sync()
            rms_norm(("n1", 2), Y, X, "memg", 1)
            done(("norm1", 2))
            turn(("n1", 2), DC, TH, TL)

            def gelu_done(n0, w, bank):
                dve.wait_ge(*evac_a.at(("a_in", n0 // 512)))
                return dve.nop()
            linear("a_in", gelu_done)
            dve.wait_ge(*evac_d.at(("a_in", 4)))
            for g in range(2):
                dve.wait_ge(*small_ready.at(("ws", g)))
                do(dve.tensor_tensor(WST[:, 4 * g:4 * g + 4, :], BK[4 + g][:, :].rearrange("p (c t) -> p c t", t=P),
                                     bc(UPPER1.unsqueeze(1), [P, 4, P]), ALU.mult))
                done(("ws", g))
            head_norm(("qm", 2), lambda tb: UV[:, tb, 2048:2560], ("qm", 2))
            attention(("mem", 2), [(qb, 2, 4, 1, PB, ATB) for qb in range(TB)], P ** -0.5, CAT12, 1024)
            layer_norm("aln", UV, EPS, "aln", D, D)
            done("aln")
            for q in range(4):
                dve.wait_ge(*small_ready.at(("spatial", q)))
                for g in (2 * q, 2 * q + 1):
                    a = slice(g * P, g * P + P)
                    go(dve.scalar_tensor_tensor(CAT12[:, :, a], BK[q][:, (g % 2) * T:(g % 2) * T + T]
                                                .rearrange("p (b c) -> p b c", b=2), BST[:, g:g + 1], UV[:, :, a],
                                                ALU.add, ALU.mult))
                done(("spatial", q))
            done(("cat", 2))
            turn(("cat", 2), 12, TH, TL)

            def residual(key):
                dve.wait_ge(*evac_d.at((key, 1)))
                dve.wait_ge(*evac_a.at((key, 1)))
                for tb in range(TB):
                    go(dve.tensor_tensor(X[:, tb, :], X[:, tb, :], Y[:, tb, :], ALU.add))
                sync()

            linear("a_out", copy_to(Y))
            residual("a_out")
            rms_norm(("n2", 2), Y, X, ("norm2", 2), 0)
            done(("norm2", 2))
            experts(2)
            rms_norm(("n1", 3), Y, X, ("norm1", 3), 0)
            done(("norm1", 3))
            turn(("n1", 3), DC, TH, TL)
            linear("b_in", copy_to(ZB))
            dve.wait_ge(*evac_d.at(("b_in", 2)))
            dve.wait_ge(*evac_a.at(("b_in", 2)))
            for tb in range(TB):
                stats(ZB[:, tb, 0:512], 1, 512, tb)
                stats(ZB[:, tb, 512:768], 1, 256, 2 + tb)
            inverse_root("bq", 4, True, EPS)
            dve.wait_ge(*rows_in.at("bq"))
            for tb in range(TB):
                go(dve.scalar_tensor_tensor(ZB[:, tb, 0:512], ZB[:, tb, 0:512], RS[:, tb:tb + 1], ROW[:, 0, 0:512],
                                            ALU.mult, ALU.mult))
                go(dve.scalar_tensor_tensor(ZB[:, tb, 512:768], ZB[:, tb, 512:768], RS[:, 2 + tb:3 + tb],
                                            ROW[:, 0, 512:768], ALU.mult, ALU.mult))
            done("bq")
            turn("cq", 4, TH, TL)
            linear("q_up", copy_to(QQ))
            turn("ckv", 2, TH, TL)
            linear("kv_up", copy_to(KV))
            dve.wait_ge(*evac_d.at(("kv_up", 1)))
            dve.wait_ge(*evac_a.at(("kv_up", 1)))
            dve.wait_ge(*evac_a.at(("q_up", 2)))
            head_norm(("qm", 3), lambda tb: ZB[:, tb, 832:1344], ("qm", 3))
            attention(("mem", 3), [(qb, 2, 4, 1, PC, ATC) for qb in range(TB)], P ** -0.5, CAT12B, 1024)
            do(dve.tensor_copy(POSF[:, :], POS[:, :]))
            for tb in range(TB):
                a, k = TRIG[:, 4, tb, :], TRIG[:, 5, tb, :]
                do(dve.tensor_scalar(a, INVF, POSF[:, tb:tb + 1], None, ALU.mult))
                for dst, shift in ((TRIG[:, 2, tb, :], 0.25), (TRIG[:, 3, tb, :], 0.0)):
                    do(dve.tensor_scalar(k, a, 1.0 / TWO_PI, shift, ALU.mult, ALU.add))
                    do(dve.tensor_scalar(k, k, ROUND, None, ALU.add))
                    do(dve.tensor_scalar(k, k, -ROUND, None, ALU.add))
                    do(dve.scalar_tensor_tensor(dst, k, -TURN1, a, ALU.mult, ALU.add))
                    do(dve.scalar_tensor_tensor(dst, k, -TURN2, dst, ALU.mult, ALU.add))
                    do(dve.scalar_tensor_tensor(dst, k, -TURN3, dst, ALU.mult, ALU.add))
                    do(dve.tensor_scalar(dst, dst, 1.0 / TWO_PI, shift, ALU.mult, ALU.add))
                    do(dve.tensor_scalar(k, dst, ROUND, None, ALU.add))
                    do(dve.tensor_scalar(k, k, -ROUND, None, ALU.add))
                    do(dve.tensor_tensor(dst, dst, k, ALU.subtract))
            done("angles")
            for tb in range(TB):
                do(dve.tensor_tensor(SCR[:, :], QQ[:, tb, :], QQ[:, tb, :], ALU.mult))
                do(dve.tensor_reduce(RS[:, 8 * tb:8 * tb + 8], SCR[:, :].rearrange("p (h c) -> p h c", c=192), X_AXIS, ALU.add))
            do(dve.tensor_scalar(RS[:, :], RS[:, :], 1.0 / 192, EPS, ALU.mult, ALU.add))
            finish_root(("qkn", 0), 16)
            dve.wait_ge(*rows_in.at("qkn"))
            for tb in range(TB):
                q3 = QQ[:, tb, :].rearrange("p (h c) -> p h c", c=192)
                do(dve.tensor_tensor(q3, q3, bc(RS[:, 8 * tb:8 * tb + 8].unsqueeze(2), [P, 8, 192]), ALU.mult))
                do(dve.tensor_tensor(q3, q3, bc(ROW[:, 0, 0:192].unsqueeze(1), [P, 8, 192]), ALU.mult))
            for tb in range(TB):
                kn = KV[:, tb, :].rearrange("p (h c) -> p h c", c=256)[:, :, 0:P]
                do(dve.tensor_tensor(SCR[:, 0:1024].rearrange("p (h c) -> p h c", c=P), kn, kn, ALU.mult))
                do(dve.tensor_reduce(RS[:, 8 * tb:8 * tb + 8], SCR[:, 0:1024].rearrange("p (h c) -> p h c", c=P), X_AXIS, ALU.add))
                kr = ZB[:, tb, 768:832]
                do(dve.tensor_tensor(SCR[:, 0:64], kr, kr, ALU.mult))
                do(dve.tensor_reduce(SCR[:, 64:65], SCR[:, 0:64], X_AXIS, ALU.add))
                do(dve.tensor_scalar(RS[:, 8 * tb:8 * tb + 8], RS[:, 8 * tb:8 * tb + 8], SCR[:, 64:65], None, ALU.add))
            do(dve.tensor_scalar(RS[:, :], RS[:, :], 1.0 / 192, EPS, ALU.mult, ALU.add))
            finish_root(("qkn", 1), 16)
            for tb in range(TB):
                kn = KV[:, tb, :].rearrange("p (h c) -> p h c", c=256)[:, :, 0:P]
                rb = RS[:, 8 * tb:8 * tb + 8].unsqueeze(2)
                do(dve.tensor_tensor(kn, kn, bc(rb, [P, 8, P]), ALU.mult))
                do(dve.tensor_tensor(kn, kn, bc(ROW[:, 0, 192:320].unsqueeze(1), [P, 8, P]), ALU.mult))
                kr = KRP[:, tb, :].rearrange("p (h c) -> p h c", c=64)
                do(dve.tensor_tensor(kr, bc(ZB[:, tb, 768:832].unsqueeze(1), [P, 8, 64]), bc(rb, [P, 8, 64]), ALU.mult))
                do(dve.tensor_tensor(kr, kr, bc(ROW[:, 0, 320:384].unsqueeze(1), [P, 8, 64]), ALU.mult))
            dve.wait_ge(*act_ready.at("trig"))
            for tb in range(TB):
                c = bc(TRIG[:, 0, tb, :].unsqueeze(1), [P, 8, 32])
                sn = bc(TRIG[:, 1, tb, :].unsqueeze(1), [P, 8, 32])
                for x3 in (QQ[:, tb, :].rearrange("p (h c) -> p h c", c=192)[:, :, 128:192],
                           KRP[:, tb, :].rearrange("p (h c) -> p h c", c=64)):
                    x1, x2 = x3[:, :, 0:32], x3[:, :, 32:64]
                    t = [SCR[:, 256 * i:256 * i + 256].rearrange("p (h c) -> p h c", c=32) for i in range(4)]
                    for o, a, b in ((0, x1, c), (1, x2, sn), (2, x1, sn), (3, x2, c)):
                        go(dve.tensor_tensor(t[o], a, b, ALU.mult))
                    sync()
                    go(dve.tensor_tensor(x1, t[0], t[1], ALU.subtract))
                    do(dve.tensor_tensor(x2, t[2], t[3], ALU.add))
            done("qkn")
            attention(("mla", 3), [(qb, qb + 1, 4, 1, PC, ATC) for qb in range(TB) for _ in range(2)], 192 ** -0.5,
                      CAT12B, 0, causal=True)
            done(("cat", 3))
            turn(("cat", 3), 12, TH, TL)
            linear("b_out", copy_to(Y))
            residual("b_out")
            rms_norm(("n2", 3), Y, X, ("norm2", 3), 0)
            done(("norm2", 3))
            experts(3)
            done("out")


_INS = ['x', 'p', 'ln0_g', 'ln0_b', 'w_in', 'hy_conv_w', 'hy_conv_b', 'hy_fw1', 'hy_fb1', 'hy_freq1', 'hy_fw2',
        'hy_fb2', 'hy_freq2', 'hy_fw3', 'hy_bias', 'att_lq1', 'att_lk1', 'att_lq2', 'att_lk2', 'att_subln_g',
        'pool_w', 'pool_b', 'pool_scale', 'w_out', 'ln1_g', 'ln1_b', 'moe_wgc', 'moe_bgc', 'moe_wgf', 'moe_bgf',
        'moe_w1', 'moe_w3', 'moe_w2', 'ple_wg', 'ple_bg', 'ple_wp', 'ln2_g', 'ln2_b', 'mem_2', 'positions_2',
        'mem_norm_g_2', 'w_mem_kv_2', 'mem_qn_g_2', 'mem_kn_g_2', 'norm1_g_2', 'norm2_g_2', 'a_w_in_2', 'a_ln_g_2',
        'a_ln_b_2', 'a_w_s_2', 'a_b_s_2', 'a_w_out_2', 'b_w_in_2', 'b_q_norm_g_2', 'b_kv_norm_g_2', 'b_w_q_up_2',
        'b_w_kv_up_2', 'b_qn_g_2', 'b_kn_g_2', 'b_w_out_2', 'moe_w_group_2', 'moe_b_group_2', 'moe_w_expert_2',
        'moe_b_expert_2', 'moe_w_gate_2', 'moe_w_up_2', 'moe_w_down_2']


def constants():
    import numpy as np

    f = np.float32
    i, j = np.arange(P)[:, None], np.arange(P)[None, :]
    inv8 = np.power(f(500000.0), -np.arange(0, 16, 2, dtype=f) / f(16)).astype(f)
    ang = np.arange(T, dtype=f)[:, None] * inv8[None, :]
    by_block = lambda a: a.reshape(TB, P, -1).transpose(1, 0, 2)
    inv32 = np.power(f(10000.0), -(np.arange(32, dtype=f) * f(2.0) / f(64))).astype(f)
    parts = [i == j, i < j, np.ones((P, P)), np.broadcast_to(j, (P, P)), i <= j, np.where(j <= i, 0.0, -1e30), i,
             np.broadcast_to(4 - np.arange(4), (P, 4)), np.broadcast_to(8 - np.arange(8), (P, 8)),
             np.broadcast_to(np.arange(4), (P, 4)), np.zeros((P, 1)), by_block(np.cos(ang)).reshape(P, 16),
             by_block(np.sin(ang)).reshape(P, 16), np.broadcast_to(inv32, (P, 32))]
    c = {"c_small": np.concatenate([np.asarray(a, f) for a in parts], axis=1)}
    band = np.zeros((T, 4, T))
    pos = np.arange(T)
    for g, win in enumerate((2, 4, 8, 16)):
        lo, hi = np.clip(pos - win // 2, 0, T - 1), np.clip(pos + win // 2 - 1, 0, T - 1)
        inside = (pos[:, None] >= lo[None, :]) & (pos[:, None] <= hi[None, :])
        band[:, g, :] = inside / (hi - lo + 1)[None, :] - np.eye(T)
    c["c_band"] = band.reshape(TB, P, 4, T).transpose(1, 0, 2, 3)
    n = 2 * T
    tau, fr = np.arange(T)[:, None], np.arange(T)[None, :]
    a = 2 * np.pi * ((tau * fr) % n) / n
    alt = (-1.0) ** np.arange(T)
    dc, ds0 = np.cos(a), -np.sin(a)
    ds, dc2 = ds0.copy(), dc[:, 0:P].copy()
    ds[:, 0], dc2[:, 0] = alt, alt
    c["c_dc"], c["c_ds"], c["c_ds0"], c["c_dc2"] = (by_block(m) for m in (dc, ds, ds0[:, 0:P], dc2))
    w = np.full((T, 1), 2.0)
    w[0] = 1.0
    ir, ii = w * np.cos(a) / n, -2.0 * np.sin(a) / n
    ii[0] = alt / n
    c["c_inv"] = np.concatenate([ir, ii]).reshape(4, P, T).transpose(1, 0, 2)
    t = np.linspace(0.0, 1.0, T, dtype=f)[:, None]
    wpos = f(2.0 * np.pi) * np.arange(T, dtype=f)[:, None] / f(T)
    bands = np.linspace(1e-4, 15, 16, dtype=f)[None, :]
    c["c_zt"] = np.concatenate([t, np.cos(wpos * bands), -np.sin(wpos * bands)], axis=-1).T
    deltas = np.linspace(np.log(1e-2) / 1.5, np.log(1e-2) / 0.3, HY, dtype=f)[None, :]
    c["c_win"] = by_block(np.exp(-t * np.abs(deltas)))
    return {k: np.ascontiguousarray(m.astype(f)) for k, m in c.items()}


def kernel(**inputs):
    import numpy as _np
    import concourse.bacc as _bacc
    from concourse import mybir as _mybir
    from concourse.bass_utils import run_bass_kernel_spmd as _run

    consts = constants()
    arrays, seen = {}, {}
    for build in range(2):
        nc = _bacc.Bacc("TRN2", target_bir_lowering=False, num_devices=1)
        tensors = {}
        for name in _INS:
            a = _np.ascontiguousarray(inputs[name])
            arrays[f"in_{name}_dram"] = a
            tensors[name] = nc.dram_tensor(f"in_{name}_dram", a.shape, _mybir.dt.from_np(a.dtype), kind="ExternalInput").ap()
        for name, a in consts.items():
            arrays[f"{name}_dram"] = a
            tensors[name] = nc.dram_tensor(f"{name}_dram", a.shape, _mybir.dt.float32, kind="ExternalInput").ap()
        tensors["out"] = nc.dram_tensor("out_0_dram", (1, T, D), _mybir.dt.float32, kind="ExternalOutput").ap()
        program(nc, tensors, seen)
    r = _run(nc, [arrays], core_ids=[0])
    return r.results[0]["out_0_dram"]
```

```python
from contextlib import ExitStack

import concourse.bass as bass
from concourse import mybir

F32 = mybir.dt.float32
F32R = mybir.dt.float32r
I32 = mybir.dt.int32
ALU = mybir.AluOpType
ACT = mybir.ActivationFunctionType
X_AXIS = mybir.AxisListType.X

P = 128
T = 256
TB = T // P
D = 1024
DC = D // P
DEPTH = 2
UNIT = 2048
RING = 4
PARTS = 3
TURN = 12
HY = 256
HEADS = 4
ALPHA = (2 * DEPTH) ** 0.25
LN_EPS = 1e-5
EPS = 1e-6
TWO_PI = 6.283185307179586
ROUND = 12582912.0
GROUPS = 4
MLA_HEADS = 8


TURN1, TURN2, TURN3 = 6.28125, 0.0019350051879882812, 3.0199159819567e-07


class Signal:

    def __init__(self, sem, values, step=1):
        self.sem, self.values, self.step, self.n = sem, values, step, 0

    def tick(self, key):
        self.n += self.step
        self.values[key] = self.n
        return self.sem, self.step

    def at(self, key):
        return self.sem, self.values.get(key, self.step)


class LoopSignal:

    def __init__(self, sem, values):
        self.sem, self.values, self.n = sem, values, 0

    def tick(self, key):
        self.n += 1
        self.values[key] = self.n
        self.values["per pass"] = max(self.n, self.values.get("per pass", 1))
        return self.sem, 1

    def at(self, p, key):
        return self.sem, p * self.values.get("per pass", 1) + self.values.get(key, 1)

    def enter(self):
        self.n = 0


class Stream:

    def __init__(self):
        self.unit, self.turns = 0, 0

    def slot(self):
        return self.unit % RING

    def part(self):
        return self.unit % PARTS

    def landed(self):
        return (self.turns * (TURN // RING) + (self.unit // RING + 1)) * 32

    def count(self, ahead):
        return self.turns * TURN + (self.unit + ahead)

    def early(self, ahead):
        return type(self.turns) is int and self.turns == 0 and self.unit + ahead <= 0


class Chain:

    def __init__(self, eng, sem):
        self.eng, self.sem, self.n = eng, sem, 0

    def go(self, ins):
        self.n += 1
        ins.then_inc(self.sem, 1)

    def sync(self):
        self.eng.wait_ge(self.sem, self.n)

    def do(self, ins):
        self.go(ins)
        self.sync()


class LoopChain:

    def __init__(self, eng, sem, p, values):
        self.eng, self.sem, self.p, self.n, self.values = eng, sem, p, 0, values

    def go(self, ins):
        self.n += 1
        self.values["per pass"] = max(self.n, self.values.get("per pass", 1))
        ins.then_inc(self.sem, 1)

    def sync(self):
        self.eng.wait_ge(self.sem, self.p * self.values.get("per pass", 1) + self.n)

    def do(self, ins):
        self.go(ins)
        self.sync()


def strips_of(n, w=512):
    return [(a, min(w, n - a)) for a in range(0, n, w)]


LINEARS = {
    "w_in": (8, 2560, 512), "w_out": (8, 1024, 512), "ple_g": (8, 1024, 512), "ple_p": (2, 1024, 1024),
    "mem": (8, 1024, 512), "a_in": (8, 2560, 512), "a_out": (12, 1024, 512), "b_in": (8, 1344, 512),
    "q_up": (4, 1536, 512), "kv_up": (2, 2048, 1024), "b_out": (12, 1024, 512),
}


def program(nc, A, seen):
    ctx = ExitStack()
    with ctx:
        sems = {}

        def sem(name):
            if name not in sems:
                sems[name] = ctx.enter_context(nc.semaphore(name))
            return sems[name]

        def signal(name, step=1):
            return Signal(sem(name), seen.setdefault(name, {}), step)

        top = [16512]

        def region(size):
            at = top[0]
            top[0] += size
            return at

        names = [0]

        def sb(name, shape, at, dt=F32, base=[0]):
            names[0] += 1
            return nc.alloc_sbuf_tensor_at(f"{name}_at{names[0]}", shape, dt, offset=at)

        class Space:

            def __init__(self, at, size):
                self.at, self.end = at, at + size

            def take(self, name, shape, dt=F32):
                n = 4
                for s in shape[1:]:
                    n *= s
                n = (n + 31) // 32 * 32
                at = self.at
                self.at += n
                assert self.at <= self.end, (name, self.at - self.end)
                return sb(name, shape, at, dt)

        RAW = sb("raw", [P, RING, UNIT], region(RING * UNIT * 4))
        WH = sb("w_hi", [P, PARTS, UNIT], region(PARTS * UNIT * 4), F32R)
        WL = sb("w_lo", [P, PARTS, UNIT], region(PARTS * UNIT * 4), F32R)
        X = sb("x", [P, TB, D], region(8192))
        y_at = region(8192)
        th_at = region(24576)
        row_at = region(8192)
        small_at = region(10240)
        z_at = top[0]
        z_size = 229344 - z_at
        Y = sb("y", [P, TB, D], y_at)
        TH = sb("t_hi", [P, 12, T], th_at, F32R)
        TL = sb("t_lo", [P, 12, T], th_at + 12288, F32R)
        ROW = sb("row", [P, 2, D], row_at)

        small = Space(small_at, 10240)
        CW = A["c_small"].shape[1]
        CS = small.take("consts", [P, CW])
        SROW = small.take("srow", [P, 1024])
        NST = small.take("stats", [P, 8, 6])
        MV = small.take("mv", [P, 8, 2])
        RS = small.take("rs", [P, 16])
        RT = small.take("rt", [P, 16])
        MX = small.take("mx", [P, 8])
        NM = small.take("nm", [P, 8])
        SU = small.take("su", [P, 8])
        RC = small.take("rc", [P, 8])
        LAM = small.take("lam", [P, 8])
        KEY = small.take("key", [P, 2])
        JP = small.take("jp", [P, 2])
        TABF = small.take("tabf", [P, 8])
        TAB = small.take("tab", [P, 8], I32)
        GQK = small.take("gqk", [P, 4])
        BST = small.take("bst", [P, 8])
        HCOL = small.take("hcol", [64, 8])
        MEMG = small.take("memg", [P, 8])
        POS = small.take("pos", [P, TB], I32)
        LQ = small.take("lq", [P, 4, 64])
        POSF = small.take("posf", [P, TB])

        at = [0]

        def const(n):
            a = at[0]
            at[0] += n
            return CS[:, a:a + n]

        IDENT, LOWER, ONES, IOTA, UPPER1, CMASK = (const(P) for _ in range(6))
        PCOL, PRI4, PRI8, IDX4, ZERO = const(1), const(4), const(8), const(4), const(1)
        COS8, SIN8, INVF = const(16), const(16), const(32)

        z = Space(z_at, z_size - 8192)
        MKT = sb("mem_kt", [P, HEADS, T], z_at + z_size - 8192)
        MV_ = sb("mem_v", [P, TB, 512], z_at + z_size - 4096)
        MEM = sb("mem", [P, TB, D], z_at + z_size - 8192)
        GROW = [sb(f"gain{i}", [P, D], th_at + a) for i, a in enumerate((8192, 20480))]
        z = Space(z_at, z_size)
        U = z.take("u", [P, TB, 2560])
        CAT8 = z.take("cat8", [P, TB, D])
        um_at = z.at
        UM = z.take("u_before", [P, TB, 768])
        UP = z.take("u_after", [P, TB, 768])
        BAND = z.take("band", [P, TB, 4, T])
        DC_, DS_ = z.take("dft_c", [P, 2, T]), z.take("dft_s", [P, 2, T])
        DS0, DC2 = z.take("dft_s0", [P, 2, P]), z.take("dft_c2", [P, 2, P])
        INV = z.take("dft_inv", [P, 4, T])
        PA = z.take("probs_a", [P, 4, T])
        ZT, FW1, FW2 = z.take("zt", [33, T]), z.take("fw1", [33, 64]), z.take("fw2", [64, 64])
        ARG, PW = z.take("arg", [64, T]), z.take("pool_w", [64, 4, 64])
        ty = Space(y_at, 8192)
        YPT = ty.take("ypt", [64, 4, T])
        WIN = sb("win", [P, 2, HY], y_at)
        FW3, H1, H2 = ty.take("fw3", [64, 512]), ty.take("h1", [64, T]), ty.take("h2", [64, T])
        FR = PA[0:64, 0, :]
        KR = sb("kr", [P, 2, HY], th_at + 10240)
        QKT = sb("qkt", [P, 8, T], th_at)
        ATA = sb("at_a", [P, 4, P], th_at + 8192)
        tl = Space(th_at + 12288, 8192)
        VV, YF = tl.take("vv", [P, TB, HY]), tl.take("yf", [P, 4, HY])
        FF = sb("ff", [P, 2, 512], th_at + 20480)
        KI, K2 = sb("ki", [P, 2, HY], th_at + 20480), sb("k2", [P, 2, HY], th_at + 22528)
        z = Space(z_at, z_size - 8192)
        UV = z.take("uv", [P, TB, 2560])
        CAT12 = z.take("cat12", [P, TB, 1536])
        MK = sb("mem_k", [P, TB, 512], z_at + 20480)
        WST, WSR = z.take("ws_t", [P, 8, P]), z.take("ws", [P, 8, P])
        PB = z.take("probs_b", [P, 4, T])
        QMT = sb("qm_t", [P, HEADS, T], th_at)
        ATB = sb("at_b", [P, 8, P], th_at + 4096)
        z = Space(z_at, z_size - 8192)
        ZB = z.take("zb", [P, TB, 1344])
        CAT12B = z.take("cat12b", [P, TB, 1536])
        QQ = z.take("qq", [P, TB, 1536])
        KV = z.take("kv", [P, TB, 2048])
        ktn_at = z.at
        KTN = z.take("ktn", [P, 8, T])
        KRP = sb("krp", [P, TB, 512], y_at)
        ATC = sb("at_c", [P, 8, P], y_at + 4096)
        QTN, QTR = sb("qtn", [P, 8, T], th_at), sb("qtr", [64, 8, T], th_at + 8192)
        KTR = sb("ktr", [64, 8, T], th_at + 16384)
        PC = sb("probs_c", [P, 4, T], row_at + 4096)
        SCR = sb("scr", [P, 1536], th_at + 14336)
        QMT2 = sb("qm_t2", [P, HEADS, T], th_at)
        TRIG = sb("trig", [P, 6, TB, 32], ktn_at)
        z = Space(z_at, z_size - 8192)
        HH, HL = (z.take(n, [P, TB, D], F32R) for n in ("tok_hi", "tok_lo"))
        XH, XL = (z.take(n, [P, DC, P], F32R) for n in ("xs_hi", "xs_lo"))
        YH, YL = (z.take(n, [P, D], F32R) for n in ("ys_hi", "ys_lo"))
        ST, SP = z.take("sel_t", [P, T], F32R), z.take("sel", [P, TB, P], F32R)
        PKROW = z.take("key_row", [P, T])
        DG = z.take("key_diag", [P, TB, P])
        RW, RWH, RWL = z.take("rw", [P, DC, 36]), z.take("rw_hi", [P, DC, 36], F32R), z.take("rw_lo", [P, DC, 36], F32R)
        AH, AL = (z.take(n, [P, 2, P], F32R) for n in ("act_hi", "act_lo"))
        SIL, GLU = z.take("silu", [P, 256]), z.take("glu", [P, 256])
        ZR = z.take("zeros", [P, P], F32R)
        GS = z.take("gate_sel", [P, 8])
        GH, GL = (z.take(n, [P, TB, 8], F32R) for n in ("gate_hi", "gate_lo"))
        LG, RB = z.take("logits", [P, TB, 36]), z.take("route_b", [P, 36])
        r1, r2, r3, r4 = (z.take(n, [P, TB, 32]) for n in ("ra", "rb", "rc_", "rd"))
        OH4 = z.take("oh4", [P, TB, 4])
        OH1, OH2, FS = (z.take(n, [P, TB, 8]) for n in ("oh1", "oh2", "fs"))
        v = [z.take(f"v{i}", [P, TB]) for i in range(12)]
        PT = z.take("p_in", [P, TB, 256])
        PTH, PTL = (z.take(n, [P, 2, T], F32R) for n in ("p_hi", "p_lo"))
        SG = z.take("sg", [P, TB, D])

        BK = [ctx.enter_context(nc.psum_tensor(f"bank{i}", [P, 512], F32)) for i in range(8)]

        raw_in = [sem(f"raw_in{i}") for i in range(RING)]
        hi_done = sem("hi_done")
        split_done = sem("split_done")
        unit_used = sem("unit_used")
        consts_in = signal("consts_in", 16)
        rows_in = signal("rows_in", 16)
        params_in = {n: signal(f"{n}_in", 16) for n in ("hy", "filt", "route", "p", "mem", "ws")}
        shift_in = signal("shift_in", 16)
        x_in = signal("x_in", 16)
        out_done = signal("out_done", 16)
        turned, turn_hi, turn_lo = signal("turned"), signal("turn_hi"), signal("turn_lo")
        evac_a, evac_d = signal("evac_a"), signal("evac_d")
        small_ready = signal("small_ready")
        scores_ready, negmax_ready, probs_ready = signal("scores_ready"), signal("negmax_ready"), signal("probs_ready")
        weights_ready, pturned, at_ready = signal("weights_ready"), signal("pturned"), signal("at_ready")
        heads_ready, heads_taken = signal("heads_ready"), signal("heads_taken")
        dve_ready = signal("dve_ready")
        act_ready = signal("act_ready")
        pool_ready = signal("pool_ready")

        class MoeSignals:
            def __init__(self, L):
                def ls(n):
                    return LoopSignal(sem(f"m{L}_{n}"), seen.setdefault(f"m{L}_{n}", {}))
                self.sel, self.gather_a, self.xh_a, self.xl_a, self.gs = ls("sel"), ls("gather_a"), ls("xh_a"), ls("xl_a"), ls("gs")
                self.gather_b, self.xh_b, self.xl_b = ls("gather_b"), ls("xh_b"), ls("xl_b")
                self.silu, self.glu, self.at, self.ah, self.al = ls("silu"), ls("glu"), ls("at"), ls("ah"), ls("al")
                self.yh, self.yl, self.scattered = ls("yh"), ls("yl"), ls("scattered")
                self.chain, self.chain_values = sem(f"m{L}_chain"), seen.setdefault(f"m{L}_chain", {})

        moe_signals = [MoeSignals(L) for L in range(4)]
        chain_sem = {n: sem(f"chain_{n}") for n in ("dve", "act", "pool", "pe")}
        for n in chain_sem:
            seen.setdefault(n, {})

        EPG = [4, 4, 8, 8]
        NR = [20, 20, 36, 36]
        MOE_W = [(A["moe_w1"][0], A["moe_w3"][0], A["moe_w2"][0]), (A["moe_w1"][1], A["moe_w3"][1], A["moe_w2"][1]),
                 (A["moe_w_gate_2"][0], A["moe_w_up_2"][0], A["moe_w_down_2"][0]),
                 (A["moe_w_gate_2"][1], A["moe_w_up_2"][1], A["moe_w_down_2"][1])]
        DRAM_W = {"w_in0": A["w_in"][0], "w_in1": A["w_in"][1], "w_out0": A["w_out"][0], "w_out1": A["w_out"][1],
                  "ple_g0": A["ple_wg"][0], "ple_g1": A["ple_wg"][1], "ple_p0": A["ple_wp"][0],
                  "ple_p1": A["ple_wp"][1], "mem": A["w_mem_kv_2"], "a_in": A["a_w_in_2"][0],
                  "a_out": A["a_w_out_2"][0], "b_in": A["b_w_in_2"][0], "q_up": A["b_w_q_up_2"][0],
                  "kv_up": A["b_w_kv_up_2"][0], "b_out": A["b_w_out_2"][0]}

        def linear_shape(key):
            chunks, n, w = LINEARS[key.rstrip("01")]
            per_unit = 2 if w == 1024 else 4
            return chunks, strips_of(n, w), per_unit

        block = ctx.enter_context(nc.Block())

        @block.sync
        def _(sp):
            s = Stream()

            def load(dst_src):
                if not s.early(1 - RING):
                    sp.wait_ge(split_done, s.count(1 - RING))
                for dst, src in dst_src:
                    sp.dma_start(dst, src).then_inc(raw_in[s.slot()], 16)
                s.unit += 1

            def load_linear(key):
                chunks, strips, per_unit = linear_shape(key)
                w = DRAM_W[key]
                for n0, width in strips:
                    for c0 in range(0, chunks, per_unit):
                        dst = RAW[:, s.slot(), 0:per_unit * width].rearrange("p (k n) -> p k n", n=width)
                        src = w[c0 * P:(c0 + per_unit) * P, n0:n0 + width].rearrange("(k p) n -> p k n", p=P)
                        h = per_unit // 2
                        load([(dst[:, 0:h, :], src[:, 0:h, :]), (dst[:, h:, :], src[:, h:, :])])

            def load_pass(L, group):
                w1, w3, w2 = MOE_W[L]

                def up(e, half):
                    dst = RAW[:, s.slot(), :].rearrange("p (k m n) -> p k m n", k=4, m=2)
                    load([(dst[:, :, m, :], w[bass.ds(group * EPG[L] + e, 1), half * 512:half * 512 + 512, :]
                           .rearrange("a (k p) n -> p (a k) n", p=P)) for m, w in enumerate((w1, w3))])

                def down(e):
                    dst = RAW[:, s.slot(), :].rearrange("p (k n) -> p k n", k=2)
                    src = w2[bass.ds(group * EPG[L] + e, 1), :, :].rearrange("a (k p) n -> p (a k) n", p=P)
                    load([(dst[:, k:k + 1, :], src[:, k:k + 1, :]) for k in range(2)])

                for e in range(EPG[L]):
                    up(e, 0)
                    up(e, 1)
                    if e:
                        down(e - 1)
                down(EPG[L] - 1)

            def load_experts(L):
                turns = EPG[L] * 3 // TURN
                start, unit = s.turns, s.unit
                load_pass(L, 0)
                sp.wait_ge(*dve_ready.at(("table", L)))
                passes = sp.value_load(TAB[0:1, 0:1], min_val=4, max_val=5)
                with sp.Fori(1, passes) as p:
                    group = sp.value_load(TAB[0:1, bass.ds(p + 1, 1)], min_val=0, max_val=3)
                    s.unit, s.turns = unit, start + p * turns
                    load_pass(L, group)
                s.unit, s.turns = unit, sp.snap(start + passes * turns)

            for tb in range(TB):
                sp.dma_start(X[:, tb, :], A["x"][0, tb * P:(tb + 1) * P, :]).then_inc(*x_in.tick("x"))
            for L in range(DEPTH):
                for key in ("w_in", "w_out", "ple_g", "ple_p"):
                    load_linear(f"{key}{L}")
                load_experts(L)
            for key in ("mem", "a_in", "a_out"):
                load_linear(key)
            load_experts(2)
            for key in ("b_in", "q_up", "kv_up", "b_out"):
                load_linear(key)
            load_experts(3)
            dst = RAW[:, s.slot(), 0:8]
            load([(dst[:, 4 * i:4 * i + 4], A["c_small"][:, 4 * i:4 * i + 4]) for i in range(2)])
            sp.wait_ge(*dve_ready.at("out"))
            for tb in range(TB):
                sp.dma_start(A["out"][0, tb * P:(tb + 1) * P, :], X[:, tb, :]).then_inc(*out_done.tick(tb))
            sp.wait_ge(*out_done.at(TB - 1))

        @block.gpsimd
        def _(pool):
            ch = Chain(pool, chain_sem["pool"])

            def row(src, slot, a=0):
                n = src.shape[-1]
                pool.dma_start(ROW[:, slot, a:a + n], src.partition_broadcast(P)).then_inc(*rows_in.tick(None))

            def rows(key, lines, free):
                if free is not None:
                    pool.wait_ge(*free)
                for src, slot, a in lines:
                    row(src, slot, a)
                rows_in.values[key] = rows_in.n

            def param(kind, key, dst, src):
                pool.dma_start(dst, src).then_inc(*params_in[kind].tick(key))

            rows("ln0", [(A["ln0_g"], 0, 0), (A["ln0_b"], 1, 0)], None)
            pool.dma_start(CS[:, :], A["c_small"]).then_inc(*consts_in.tick("consts"))

            def hyena_params(L):
                if L:
                    pool.wait_ge(*dve_ready.at(("moe_out", L - 1)))
                param("filt", L, ZT[:, :], A["c_zt"])
                param("filt", L, FW1[:, :], A["hy_fw1"][L])
                for i, n in enumerate(("hy_fb1", "hy_freq1", "hy_fb2", "hy_freq2")):
                    param("filt", L, HCOL[:, i:i + 1], A[n][L].rearrange("(p a) -> p a", a=1))
                param("filt", L, FW2[:, :], A["hy_fw2"][L])
                param("filt", L, FW3[:, :], A["hy_fw3"][L])
                param("filt", L, WIN[:, :, :], A["c_win"])
                param("hy", L, DC_[:, :, :], A["c_dc"])
                param("hy", L, DS_[:, :, :], A["c_ds"])
                param("hy", L, DS0[:, :, :], A["c_ds0"])
                param("hy", L, DC2[:, :, :], A["c_dc2"])
                for i, n in enumerate(("att_lq1", "att_lk1", "att_lq2", "att_lk2")):
                    param("hy", L, LQ[:, i, :], A[n][L].partition_broadcast(P))
                param("hy", L, BAND[:, :, :, :], A["c_band"])
                param("hy", L, INV[:, :, :], A["c_inv"])
                param("hy", L, PW[:, :, :], A["pool_w"][L].rearrange("g c d -> c g d"))
                for a, n in ((0, "hy_bias"), (256, "att_subln_g"), (640, "pool_scale")):
                    src = A[n][L]
                    param("hy", L, SROW[:, a:a + src.shape[0]], src.partition_broadcast(P))
                param("hy", L, SROW[:, 384:640], A["pool_b"][L].rearrange("g d -> (g d)").partition_broadcast(P))

            def hyena(L):
                conv_w, conv_b = A["hy_conv_w"][L], A["hy_conv_b"][L]
                rows(("hy_a", L), [(conv_w[0], 0, 0), (conv_w[1], 1, 0)],
                     dve_ready.at("ln0") if L == 0 else dve_ready.at(("ln2", 0)))
                ch.go(pool.memset(UM[:, 0, :], 0.0))
                ch.go(pool.memset(UP[:, 1, :], 0.0))
                ch.sync()
                for s_ in range(2):
                    pool.wait_ge(*evac_a.at((f"w_in{L}", s_)))
                    pool.wait_ge(*evac_d.at((f"w_in{L}", s_)))
                for dst, src in ((UM[1:P, 0, :], U[0:P - 1, 0, 0:768]), (UM[1:P, 1, :], U[0:P - 1, 1, 0:768]),
                                 (UM[0:1, 1, :], U[P - 1:P, 0, 0:768]), (UP[0:P - 1, 0, :], U[1:P, 0, 0:768]),
                                 (UP[0:P - 1, 1, :], U[1:P, 1, 0:768]), (UP[P - 1:P, 0, :], U[0:1, 1, 0:768])):
                    pool.dma_start(dst, src).then_inc(*shift_in.tick(L))
                pool.wait_ge(*shift_in.at(L))
                pool.wait_ge(*rows_in.at(("hy_a", L)))
                for tb in range(TB):
                    ch.go(pool.tensor_tensor(UM[:, tb, :], UM[:, tb, :], ROW[:, 0, 0:768], ALU.mult))
                    ch.go(pool.tensor_tensor(U[:, tb, 0:768], U[:, tb, 0:768], ROW[:, 1, 0:768], ALU.mult))
                ch.sync()
                for tb in range(TB):
                    ch.go(pool.tensor_tensor(UM[:, tb, :], UM[:, tb, :], U[:, tb, 0:768], ALU.add))
                rows(("hy_b", L), [(conv_w[2], 0, 0), (conv_b, 1, 0)], None)
                pool.wait_ge(*rows_in.at(("hy_b", L)))
                for tb in range(TB):
                    ch.go(pool.tensor_tensor(UP[:, tb, :], UP[:, tb, :], ROW[:, 0, 0:768], ALU.mult))
                ch.sync()
                for tb in range(TB):
                    ch.do(pool.tensor_tensor(UP[:, tb, :], UP[:, tb, :], ROW[:, 1, 0:768], ALU.add))
                    ch.do(pool.tensor_tensor(UM[:, tb, :], UM[:, tb, :], UP[:, tb, :], ALU.add))
                pool.wait_ge(*evac_d.at((f"w_in{L}", 4)))
                for tb in range(TB):
                    ins = pool.tensor_tensor(VV[:, tb, :], UM[:, tb, 512:768], UM[:, tb, 256:512], ALU.mult)
                    ch.go(ins)
                ch.sync()
                pool.nop().then_inc(*pool_ready.tick(("conv", L)))
                rows(("ln1", L), [(A["ln1_g"][L], 0, 0), (A["ln1_b"][L], 1, 0)], None)

            def route_params(L, name_w, name_b, i):
                wg, we = A[name_w[0]][i], A[name_w[1]][i]
                n = we.shape[-1]
                for c in range(DC):
                    param("route", L, RW[:, c, 0:4], wg[c * P:(c + 1) * P, :])
                    param("route", L, RW[:, c, 4:4 + n], we[c * P:(c + 1) * P, :])
                param("route", L, RB[:, 0:4], A[name_b[0]][i].partition_broadcast(P))
                param("route", L, RB[:, 4:4 + n], A[name_b[1]][i].partition_broadcast(P))

            for L in range(DEPTH):
                hyena_params(L)
                hyena(L)
                pool.wait_ge(*turn_lo.at((("cat", L), 3)))
                route_params(L, ("moe_wgc", "moe_wgf"), ("moe_bgc", "moe_bgf"), L)
                for tb in range(TB):
                    param("p", L, PT[:, tb, :], A["p"][L, 0, tb * P:(tb + 1) * P, :])
                rows(("ple", L), [(A["ple_bg"][L], 0, 0)], dve_ready.at(("ln1", L)))
                rows(("ln2", L), [(A["ln2_g"][L], 0, 0), (A["ln2_b"][L], 1, 0)], dve_ready.at(("ple_b", L)))
                for signal_ in (evac_a, evac_d):
                    pool.wait_ge(*signal_.at((f"ple_p{L}", 0)))
                for tb in range(TB):
                    ch.go(pool.tensor_tensor(Y[:, tb, :], Y[:, tb, :], SG[:, tb, :], ALU.mult))
                    ch.go(pool.tensor_scalar(X[:, tb, :], X[:, tb, :], ALPHA, None, ALU.mult))
                ch.sync()
                for tb in range(TB):
                    ch.go(pool.tensor_tensor(X[:, tb, :], X[:, tb, :], Y[:, tb, :], ALU.add))
                ch.sync()
                pool.nop().then_inc(*pool_ready.tick(("ple", L)))
                if L == DEPTH - 1:
                    for tb in range(TB):
                        param("mem", 0, MEM[:, tb, :], A["mem_2"][0, tb * P:(tb + 1) * P, :])
                        param("mem", 0, POS[:, tb:tb + 1],
                              A["positions_2"][0, tb * P:(tb + 1) * P].rearrange("(p a) -> p a", a=1))
                    for i in range(2):
                        param("mem", 0, GQK[:, 2 * i:2 * i + 1], A["mem_qn_g_2"][i].rearrange("(p a) -> p a", a=1))
                        param("mem", 0, GQK[:, 2 * i + 1:2 * i + 2], A["mem_kn_g_2"][i].rearrange("(p a) -> p a", a=1))
                    for g in range(8):
                        param("mem", 0, BST[:, g:g + 1], A["a_b_s_2"][0, g, :].rearrange("(p a) -> p a", a=1))
                    for row_, src in zip(GROW, (A["mem_norm_g_2"], A["norm1_g_2"][0])):
                        param("mem", 0, row_[:, :], src.partition_broadcast(P))

            pool.wait_ge(*dve_ready.at(("moe_out", 1)))
            param("ws", 0, WSR[:, :, :], A["a_w_s_2"][0].rearrange("g t s -> t g s"))
            rows("aln", [(A["a_ln_g_2"][0], 0, 0), (A["a_ln_b_2"][0], 1, 0)], dve_ready.at(("norm1", 2)))
            rows(("norm2", 2), [(A["norm2_g_2"][0], 0, 0)], dve_ready.at("aln"))
            pool.wait_ge(*turn_lo.at((("cat", 2), 5)))
            route_params(2, ("moe_w_group_2", "moe_w_expert_2"), ("moe_b_group_2", "moe_b_expert_2"), 0)
            rows(("norm1", 3), [(A["norm1_g_2"][1], 0, 0)], dve_ready.at(("norm2", 2)))
            rows("bq", [(A["b_q_norm_g_2"][0], 0, 0), (A["b_kv_norm_g_2"][0], 0, 512)], dve_ready.at(("norm1", 3)))
            rows("qkn", [(A["b_qn_g_2"][0], 0, 0), (A["b_kn_g_2"][0], 0, 192)], dve_ready.at("bq"))
            rows(("norm2", 3), [(A["norm2_g_2"][1], 0, 0)], dve_ready.at("qkn"))
            pool.wait_ge(*turn_lo.at((("cat", 3), 5)))
            route_params(3, ("moe_w_group_2", "moe_w_expert_2"), ("moe_b_group_2", "moe_b_expert_2"), 1)

        @block.tensor
        def _(pe):
            s = Stream()
            owner = {}

            def claim(*banks):
                for b in banks:
                    if b in owner:
                        pe.wait_ge(*owner.pop(b))

            def three(out, ah, al, bh, bl, start, stop, loose=False):
                pe.matmul(out, ah, bh, start=start, stop=False, skip_group_check=loose)
                pe.matmul(out, ah, bl, start=False, stop=False, skip_group_check=loose)
                return pe.matmul(out, al, bh, start=False, stop=stop, skip_group_check=loose)

            def turn(key, src, chunks, after, low=True):
                for w in after:
                    pe.wait_ge(*w)
                for g in range(chunks // 2):
                    b = 4 + g % 2
                    claim(b)
                    for c in range(2):
                        for tb in range(TB):
                            a = (2 * g + c) * P
                            ins = pe.transpose(BK[b][:, c * T + tb * P:c * T + tb * P + P], src[:, tb, a:a + P], IDENT)
                    ins.then_inc(*turned.tick((key, g)))
                    owner[b] = (turn_lo if low else turn_hi).at((key, g))

            def linear(key, th=TH, tl_=TL, after={}):
                chunks, strips, per_unit = linear_shape(key)
                for i, (n0, width) in enumerate(strips):
                    wide = width > 512
                    banks = {(tb, j): 2 * tb + j if wide else 2 * (i % 2) + tb for tb in range(TB)
                             for j in range(2 if wide else 1)}
                    claim(*banks.values())
                    for c0 in range(0, chunks, per_unit):
                        pe.wait_ge(split_done, s.count(1))
                        for c in range(per_unit):
                            for (tb, j), b in banks.items():
                                w = min(width, 512)
                                a = c * width + j * 512
                                ins = three(BK[b][:, 0:w], th[:, c0 + c, tb * P:(tb + 1) * P],
                                            tl_[:, c0 + c, tb * P:(tb + 1) * P], WH[:, s.part(), a:a + w],
                                            WL[:, s.part(), a:a + w], c0 + c == 0, c0 + c == chunks - 1)
                        ins.then_inc(unit_used, 1)
                        s.unit += 1
                    for (tb, j), b in banks.items():
                        owner[b] = (evac_d if tb else evac_a).at((key, i))
                    if i in after:
                        after[i]()

            def attention(key, rounds, score, value):
                def scores(r):
                    claim(2 * (r % 2), 2 * (r % 2) + 1)
                    for i in range(4):
                        ins = score(r, i, BK[2 * (r % 2) + i % 2][:, (i // 2) * T:(i // 2) * T + P * rounds[r][1]])
                    ins.then_inc(*scores_ready.tick((key, r)))
                    for b in (2 * (r % 2), 2 * (r % 2) + 1):
                        owner[b] = probs_ready.at((key, r))

                scores(0)
                for r, (qb, kbs, heads, step, probs, at_) in enumerate(rounds):
                    if r + 1 < len(rounds):
                        scores(r + 1)
                    pe.wait_ge(*weights_ready.at((key, r)))
                    claim(4, 5)
                    for h in range(heads):
                        for kb in range(kbs):
                            n = h * kbs + kb
                            ins = pe.transpose(BK[4 + n // 4][:, (n % 4) * P:(n % 4) * P + P],
                                               probs[:, h * step, kb * P:(kb + 1) * P], IDENT)
                    ins.then_inc(*pturned.tick((key, r)))
                    owner[4] = owner[5] = at_ready.at((key, r))
                    pe.wait_ge(*at_ready.at((key, r)))
                    b = 6 + r % 2
                    claim(b)
                    for h in range(heads):
                        for kb in range(kbs):
                            ins = pe.matmul(BK[b][:, h * P:(h + 1) * P], at_[:, h * kbs + kb, :],
                                            value(r, h, kb), start=kb == 0, stop=kb == kbs - 1)
                    ins.then_inc(*heads_ready.tick((key, r)))
                    owner[b] = heads_taken.at((key, r))

            def experts(L):
                m = moe_signals[L]
                E = EPG[L]
                turns = E * 3 // TURN
                pe.wait_ge(*dve_ready.at(("rw", L)))
                claim(6, 7)
                for tb in range(TB):
                    for c in range(DC):
                        t_ = slice(tb * P, tb * P + P)
                        ins = three(BK[6][:, tb * 64:tb * 64 + NR[L]], TH[:, c, t_], TL[:, c, t_],
                                    RWH[:, c, 0:NR[L]], RWL[:, c, 0:NR[L]], c == 0, c == DC - 1)
                ins.then_inc(*small_ready.tick(("logits", L)))

                def ranks():
                    pe.wait_ge(*dve_ready.at(("onehot", L)))
                    R = BK[7]
                    pe.matmul(R[:, 0:4], LOWER, OH4[:, 0, :], start=True, stop=True)
                    pe.matmul(R[:, 4:8], LOWER, OH4[:, 1, :], start=True, stop=False)
                    pe.matmul(R[:, 4:8], ONES, OH4[:, 0, :], start=False, stop=True)
                    pe.matmul(R[:, 8:12], ONES, OH4[:, 0, :], start=True, stop=False)
                    pe.matmul(R[:, 8:12], ONES, OH4[:, 1, :], start=False, stop=True)\
                        .then_inc(*small_ready.tick(("ranks", L)))

                def key_row():
                    pe.wait_ge(*dve_ready.at(("diag", L)))
                    for tb in range(TB):
                        ins = pe.matmul(BK[6][:, tb * P:tb * P + P], ONES, DG[:, tb, :], start=True, stop=True)
                    ins.then_inc(*small_ready.tick(("keyrow", L)))

                if L < DEPTH:
                    pe.wait_ge(*params_in["p"].at(L))
                    turn(("p", L), PT, 2, [])
                    linear(f"ple_g{L}", after={0: ranks})
                    pe.wait_ge(*turn_lo.at((("p", L), 0)))
                    linear(f"ple_p{L}", PTH, PTL)
                else:
                    ranks()
                key_row()
                claim(0, 1, 2, 3, 4, 5, 6, 7)
                pe.wait_ge(*dve_ready.at(("table", L)))
                passes = pe.value_load(TAB[0:1, 0:1], min_val=4, max_val=5)
                for b in range(6):
                    ins = pe.matmul(BK[b][:, :], ZR[:, :], TH[:, 0:2, :].rearrange("p a b -> p (a b)"), start=True, stop=True)
                ins.then_inc(*small_ready.tick(("cleared", L)))

                def gather(q, chunks):
                    for c in chunks:
                        a = (4 * q + c) * P
                        o = BK[6 + q][:, c * P:(c + 1) * P]
                        for tb in range(TB):
                            pe.matmul(o, HH[:, tb, a:a + P], SP[:, tb, :], start=tb == 0, stop=False)
                            ins = pe.matmul(o, HL[:, tb, a:a + P], SP[:, tb, :], start=False, stop=tb == 1)
                    return ins

                def gather_gates():
                    for tb in range(TB):
                        pe.matmul(BK[7][:, 256:264], SP[:, tb, :], GH[:, tb, :], start=tb == 0, stop=False)
                        ins = pe.matmul(BK[7][:, 256:264], SP[:, tb, :], GL[:, tb, :], start=False, stop=tb == 1)
                    return ins

                def scatter():
                    for tb in range(TB):
                        for half in range(2):
                            for y in (YH, YL):
                                ins = pe.matmul(BK[2 * tb + half][:, :], ST[:, tb * P:(tb + 1) * P],
                                                y[:, half * 512:half * 512 + 512], start=False, stop=False,
                                                skip_group_check=True)
                    return ins

                pe.wait_ge(*m.sel.at(0, "sel"))
                gather_gates()
                gather(0, range(4)).then_inc(*m.gather_a.tick(0))
                m.gather_a.enter()
                start, unit = s.turns, s.unit
                with pe.Fori(0, passes) as p:
                    s.unit, s.turns = unit, start + p * turns
                    pe.wait_ge(*m.gs.at(p, 0))
                    gather(1, range(4)).then_inc(*m.gather_b.tick(0))

                    def up(e, half):
                        pe.wait_ge(split_done, s.count(1))
                        if e == 0:
                            pe.wait_ge(*(m.xl_b if half else m.xl_a).at(p, 0))
                        for k in range(4):
                            c = half * 4 + k
                            ins = three(BK[6 + e % 2][:, :], XH[:, c, :], XL[:, c, :],
                                        WH[:, s.part(), k * 512:k * 512 + 512],
                                        WL[:, s.part(), k * 512:k * 512 + 512], c == 0, c == 7)
                        ins.then_inc(unit_used, 1)
                        s.unit += 1

                    def turn_glu(e):
                        pe.wait_ge(*m.glu.at(p, e))
                        for f in range(2):
                            ins = pe.transpose(BK[6 + e % 2][:, f * P:(f + 1) * P], GLU[:, f * P:(f + 1) * P], IDENT)
                        if e == E - 1:
                            ins = gather_gates()
                        ins.then_inc(*m.at.tick(e))

                    def down(e):
                        pe.wait_ge(split_done, s.count(1))
                        pe.wait_ge(*m.al.at(p, e))
                        for f in range(2):
                            for half in range(2):
                                a = f * 1024 + half * 512
                                ins = three(BK[4 + half][:, :], AH[:, f, :], AL[:, f, :], WH[:, s.part(), a:a + 512],
                                            WL[:, s.part(), a:a + 512], e == 0 and f == 0, e == E - 1 and f == 1,
                                            True)
                        ins.then_inc(unit_used, 1)
                        s.unit += 1

                    up(0, 0)
                    up(0, 1)
                    pe.wait_ge(*m.yl.at(p, 1))
                    scatter().then_inc(*m.scattered.tick(0))
                    for e in range(1, E):
                        up(e, 0)
                        turn_glu(e - 1)
                        up(e, 1)
                        down(e - 1)
                    pe.wait_ge(*m.sel.at(p + 1, "sel"))
                    gather(0, range(2))
                    turn_glu(E - 1)
                    gather(0, range(2, 4)).then_inc(*m.gather_a.tick(0))
                    down(E - 1)
                s.unit, s.turns = unit, pe.snap(start + passes * turns)
                pe.wait_ge(*dve_ready.at(("yl", L)))
                scatter().then_inc(*small_ready.tick(("moe", L)))
                for b in range(8):
                    owner[b] = dve_ready.at(("moe_out", L))

            pe.wait_ge(*consts_in.at("consts"))
            for L in range(DEPTH):
                def filter1():
                    claim(7)
                    pe.wait_ge(*params_in["filt"].at(L))
                    pe.matmul(BK[7][0:64, 0:T], FW1[:, :], ZT[:, :], start=True, stop=True)\
                        .then_inc(*small_ready.tick(("f1", L)))

                def filter2():
                    pe.wait_ge(*act_ready.at(("sin1", L)))
                    pe.matmul(BK[7][0:64, T:2 * T], FW2[:, :], H1[:, :], start=True, stop=True)\
                        .then_inc(*small_ready.tick(("f2", L)))
                    owner[7] = dve_ready.at(("arg2", L))

                def filter3():
                    pe.wait_ge(*act_ready.at(("sin2", L)))
                    claim(4, 5)
                    for tb in range(TB):
                        ins = pe.matmul(BK[4 + tb][:, :], H2[:, tb * P:(tb + 1) * P], FW3[:, :], start=True, stop=True)
                    ins.then_inc(*small_ready.tick(("f3", L)))
                    owner[4] = owner[5] = dve_ready.at(("filt", L))

                def energy():
                    pe.wait_ge(*act_ready.at(("fsq", L)))
                    claim(6)
                    for tb in range(TB):
                        ins = pe.matmul(BK[6][:, :], ONES, PA[:, 2 * tb:2 * tb + 2, :].rearrange("p a b -> p (a b)"),
                                        start=tb == 0, stop=tb == 1)
                    ins.then_inc(*small_ready.tick(("energy", L)))
                    owner[6] = dve_ready.at(("fnorm", L))

                def spectrum(out, mat, cols, rhs):
                    for kb in range(2):
                        ins = pe.matmul(out, mat[:, kb, cols], rhs(kb), start=kb == 0, stop=kb == 1)
                    return ins

                b0, b1 = slice(0, P), slice(P, 2 * P)

                def spectra():
                    pe.wait_ge(*dve_ready.at(("fnorm", L)))
                    pe.wait_ge(*params_in["hy"].at(L))
                    claim(4, 5, 7)
                    fsum, fdif = (lambda kb: FF[:, kb, 0:HY]), (lambda kb: FF[:, kb, HY:2 * HY])
                    spectrum(BK[4][:, 0:HY], DC_, b0, fsum)
                    spectrum(BK[4][:, HY:2 * HY], DC_, b1, fsum)
                    spectrum(BK[5][:, 0:HY], DS0, b0, fdif)
                    spectrum(BK[5][:, HY:2 * HY], DS_, b1, fdif)
                    spectrum(BK[7][:, 0:HY], DC2, b0, fsum).then_inc(*small_ready.tick(("kspec", L)))
                    owner[4] = owner[5] = owner[7] = dve_ready.at(("kspec", L))

                turn(("h", L), X, DC, [dve_ready.at("ln0" if L == 0 else ("ln2", 0))])
                pe.wait_ge(*turn_lo.at((("h", L), 3)))
                linear(f"w_in{L}", after={0: filter1, 1: filter2, 2: filter3, 3: energy, 4: spectra})
                turn(("qk", L), U[:, :, 768:1792], 8, [dve_ready.at(("rope", L))], low=False)
                pe.wait_ge(*turn_hi.at((("qk", L), 3)))
                rounds = [(qb, 2, 2, 2, PA, ATA) for qb in range(TB) for _ in range(2)]

                def score(r, i, out):
                    qb, h, c = r // 2, 2 * (r % 2) + i // 2, i % 2
                    part = slice(64 * c, 64 * c + 64)
                    return pe.matmul(out, QKT[part, h, qb * P:(qb + 1) * P], QKT[part, 4 + h, :], start=True, stop=True)

                def value(r, h, kb):
                    a = 1792 + (2 * (r % 2) + h) * P
                    return U[:, kb, a:a + P]

                attention(("att", L), rounds, score, value)
                pe.wait_ge(*params_in["hy"].at(L))
                for g in range(4):
                    b = 4 + g // 2
                    if g % 2 == 0:
                        claim(b)
                    for kb in range(TB):
                        ins = pe.matmul(BK[b][0:64, (g % 2) * T:(g % 2) * T + T], U[:, kb, 2304 + 64 * g:2368 + 64 * g],
                                        BAND[:, kb, g, :], start=kb == 0, stop=kb == 1)
                    if g % 2:
                        ins.then_inc(*small_ready.tick(("pool", L, g // 2)))
                        owner[b] = act_ready.at(("pool", L, g // 2))
                for q in range(2):
                    pe.wait_ge(*act_ready.at(("pool", L, q)))
                claim(6)
                for tb in range(TB):
                    for g in range(4):
                        ins = pe.matmul(BK[6][:, tb * 256 + g * 64:tb * 256 + g * 64 + 64],
                                        YPT[:, g, tb * P:(tb + 1) * P], PW[:, g, :], start=True, stop=True)
                ins.then_inc(*small_ready.tick(("pool2", L)))
                owner[6] = dve_ready.at(("pool", L))
                pe.wait_ge(*pool_ready.at(("conv", L)))
                pe.wait_ge(*dve_ready.at(("kspec", L)))
                claim(1, 2)
                vv = lambda kb: VV[:, kb, :]
                spectrum(BK[1][:, 0:HY], DC_, b0, vv)
                spectrum(BK[1][:, HY:2 * HY], DC_, b1, vv)
                spectrum(BK[2][:, 0:HY], DS_, b0, vv)
                spectrum(BK[2][:, HY:2 * HY], DS_, b1, vv).then_inc(*small_ready.tick(("vspec", L)))
                pe.wait_ge(*dve_ready.at(("yspec", L)))
                owner[1] = owner[2] = dve_ready.at(("yspec", L))
                claim(3)
                for tb in range(TB):
                    for k in range(4):
                        ins = pe.matmul(BK[3][:, tb * HY:(tb + 1) * HY], INV[:, k, tb * P:(tb + 1) * P], YF[:, k, :],
                                        start=k == 0, stop=k == 3)
                ins.then_inc(*small_ready.tick(("conv", L)))
                owner[3] = dve_ready.at(("cat", L))
                turn(("cat", L), CAT8, 8, [dve_ready.at(("cat", L))])
                pe.wait_ge(*turn_lo.at((("cat", L), 3)))
                linear(f"w_out{L}")
                turn(("h1", L), X, DC, [dve_ready.at(("ln1", L))])
                pe.wait_ge(*turn_lo.at((("h1", L), 3)))
                experts(L)

            turn("mem", Y, DC, [dve_ready.at("memn")])
            pe.wait_ge(*turn_lo.at(("mem", 3)))
            linear("mem")

            def mem_attention(L, qt, probs, at_):
                rounds = [(qb, 2, 4, 1, probs, at_) for qb in range(TB)]
                attention(("mem", L), rounds,
                          lambda r, i, out: pe.matmul(out, qt[:, i, r * P:(r + 1) * P], MKT[:, i, :],
                                                      start=True, stop=True),
                          lambda r, h, kb: MV_[:, kb, h * P:(h + 1) * P])

            turn(("n1", 2), Y, DC, [dve_ready.at(("norm1", 2))])
            pe.wait_ge(*turn_lo.at((("n1", 2), 3)))
            linear("a_in")
            turn("mk", MK, 4, [dve_ready.at("mk")], low=False)
            pe.wait_ge(*params_in["ws"].at(0))
            for g in range(2):
                claim(4 + g)
                for k in range(4):
                    ins = pe.transpose(BK[4 + g][:, k * P:(k + 1) * P], WSR[:, 4 * g + k, :], IDENT)
                ins.then_inc(*small_ready.tick(("ws", g)))
                owner[4 + g] = dve_ready.at(("ws", g))
            pe.wait_ge(*dve_ready.at(("ws", 1)))
            pe.wait_ge(*dve_ready.at("aln"))
            for g in range(8):
                b = g // 2
                if g % 2 == 0:
                    claim(b)
                ins = pe.matmul(BK[b][:, (g % 2) * T:(g % 2) * T + T], WST[:, g, :],
                                UV[:, :, D + g * P:D + (g + 1) * P], start=True, stop=True)
                if g % 2:
                    ins.then_inc(*small_ready.tick(("spatial", g // 2)))
                    owner[b] = dve_ready.at(("spatial", g // 2))
            turn(("qm", 2), UV[:, :, 2048:2560], 4, [dve_ready.at(("qm", 2))], low=False)
            pe.wait_ge(*turn_hi.at((("qm", 2), 1)))
            mem_attention(2, QMT, PB, ATB)
            turn(("cat", 2), CAT12, 12, [dve_ready.at(("cat", 2))])
            pe.wait_ge(*turn_lo.at((("cat", 2), 5)))
            linear("a_out")
            turn(("h1", 2), Y, DC, [dve_ready.at(("norm2", 2))])
            pe.wait_ge(*turn_lo.at((("h1", 2), 3)))
            experts(2)

            turn(("n1", 3), Y, DC, [dve_ready.at(("norm1", 3))])
            pe.wait_ge(*turn_lo.at((("n1", 3), 3)))
            linear("b_in")
            turn("cq", ZB[:, :, 0:512], 4, [dve_ready.at("bq")])
            pe.wait_ge(*turn_lo.at(("cq", 1)))
            linear("q_up")
            turn("ckv", ZB[:, :, 512:768], 2, [])
            pe.wait_ge(*turn_lo.at(("ckv", 0)))
            linear("kv_up")
            turn(("qm", 3), ZB[:, :, 832:1344], 4, [dve_ready.at(("qm", 3))], low=False)
            pe.wait_ge(*turn_hi.at((("qm", 3), 1)))
            mem_attention(3, QMT2, PC, ATC)
            pe.wait_ge(*dve_ready.at("qkn"))
            n = 0
            for what, src, rot in (("q", lambda h: QQ[:, :, 192 * h:192 * h + P], lambda h: QQ[:, :, 192 * h + P:192 * h + 192]),
                                   ("k", lambda h: KV[:, :, 256 * h:256 * h + P], lambda h: KRP[:, :, 64 * h:64 * h + 64])):
                for h2 in range(4):
                    for part, f in (("n", src), ("r", rot)):
                        b = 4 + n % 2
                        n += 1
                        claim(b)
                        rowsn = P if part == "n" else 64
                        for h in range(2):
                            for tb in range(TB):
                                ins = pe.transpose(BK[b][0:rowsn, h * T + tb * P:h * T + tb * P + P],
                                                   f(2 * h2 + h)[:, tb, :], IDENT)
                        ins.then_inc(*turned.tick((what, part, h2)))
                        owner[b] = turn_hi.at((what, part, h2))
            pe.wait_ge(*turn_hi.at(("k", "r", 3)))
            rounds = [(qb, qb + 1, 4, 1, PC, ATC) for qb in range(TB) for _ in range(2)]

            def mla_score(r, i, out):
                qb, h, w = r // 2, 4 * (r % 2) + i, P * (r // 2 + 1)
                pe.matmul(out, QTN[:, h, qb * P:(qb + 1) * P], KTN[:, h, 0:w], start=True, stop=False)
                return pe.matmul(out, QTR[:, h, qb * P:(qb + 1) * P], KTR[:, h, 0:w], start=False, stop=True)

            def mla_value(r, h, kb):
                a = 256 * (4 * (r % 2) + h) + P
                return KV[:, kb, a:a + P]

            attention(("mla", 3), rounds, mla_score, mla_value)
            turn(("cat", 3), CAT12B, 12, [dve_ready.at(("cat", 3))])
            pe.wait_ge(*turn_lo.at((("cat", 3), 5)))
            linear("b_out")
            turn(("h1", 3), Y, DC, [dve_ready.at(("norm2", 3))])
            pe.wait_ge(*turn_lo.at((("h1", 3), 3)))
            experts(3)

        @block.scalar
        def _(act):
            s = Stream()
            ch = Chain(act, chain_sem["act"])

            def split(width=UNIT):
                act.wait_ge(raw_in[s.slot()], s.landed())
                if not s.early(1 - PARTS):
                    act.wait_ge(unit_used, s.count(1 - PARTS))
                act.activation(WH[:, s.part(), 0:width], RAW[:, s.slot(), 0:width], ACT.Copy).then_inc(hi_done, 1)
                s.unit += 1

            def turn(key, chunks, dst, free=None):
                if free is not None:
                    act.wait_ge(*free)
                for g in range(chunks // 2):
                    act.wait_ge(*turned.at((key, g)))
                    act.activation(dst[:, 2 * g:2 * g + 2, :],
                                   BK[4 + g % 2][:, :].rearrange("p (c t) -> p c t", c=2), ACT.Copy)\
                       .then_inc(*turn_hi.tick((key, g)))

            begun = {"w_in1": 1, "mem": 1, "b_in": 1}

            def begin(key, units):
                chunks, strips, per_unit = linear_shape(key)
                for _ in range(units):
                    split(per_unit * strips[0][1])
                begun[key] = begun.get(key, 0) + units

            def linear(key, evac, before={}, after={}):
                chunks, strips, per_unit = linear_shape(key)
                ends = []

                def ahead(i):
                    for _ in range(chunks // per_unit - (begun.get(key, 0) if i == 0 else 0)):
                        split(per_unit * strips[i][1])
                    ends.append(s.count(0))
                ahead(0)
                for i, (n0, width) in enumerate(strips):
                    if i + 1 < len(strips):
                        ahead(i + 1)
                    if i in before:
                        before[i]()
                    act.wait_ge(unit_used, ends[i])
                    if width > 512:
                        evac(n0, 512, BK[0])
                        evac(n0 + 512, 512, BK[1]).then_inc(*evac_a.tick((key, i)))
                    else:
                        evac(n0, width, BK[2 * (i % 2)]).then_inc(*evac_a.tick((key, i)))
                    if i in after:
                        after[i]()

            def copy_to(dst):
                return lambda n0, w, bank: act.activation(dst[:, 0, n0:n0 + w], bank[:, 0:w], ACT.Copy)

            def root(key, n):
                act.wait_ge(*dve_ready.at(("var", key)))
                act.activation(RT[:, 0:n], RS[:, 0:n], ACT.Sqrt).then_inc(*act_ready.tick(("root", key)))

            def attention(key, rounds, scale):
                for r, (qb, kbs, heads, step, probs, at_) in enumerate(rounds):
                    act.wait_ge(*negmax_ready.at((key, r)))
                    if r:
                        act.wait_ge(*pturned.at((key, r - 1)))
                    for i in range(4):
                        b = BK[2 * (r % 2) + i % 2]
                        ins = act.activation(probs[:, i, 0:P * kbs], b[:, (i // 2) * T:(i // 2) * T + P * kbs], ACT.Exp,
                                             bias=NM[:, i:i + 1], scale=scale, accum_out=SU[:, i:i + 1])
                        ch.go(ins)
                    ch.sync()
                    act.nop().then_inc(*probs_ready.tick((key, r)))
                    act.wait_ge(*pturned.at((key, r)))
                    if r:
                        act.wait_ge(*heads_ready.at((key, r - 1)))
                    n = heads * kbs
                    for b in range((n + 3) // 4):
                        k = min(4, n - 4 * b)
                        ch.go(act.activation(at_[:, 4 * b:4 * b + k, :],
                                             BK[4 + b][:, 0:k * P].rearrange("p (c t) -> p c t", t=P), ACT.Copy))
                    ch.sync()
                    act.nop().then_inc(*at_ready.tick((key, r)))

            def experts(L):
                m = moe_signals[L]
                E = EPG[L]
                turns = E * 3 // TURN
                src = X if L < DEPTH else Y
                act.wait_ge(*dve_ready.at(("ln1", L) if L < DEPTH else ("norm2", L)))
                act.wait_ge(*params_in["route"].at(L))
                act.activation(RWH[:, :, 0:NR[L]], RW[:, :, 0:NR[L]], ACT.Copy).then_inc(*act_ready.tick(("rwh", L)))
                turn(("h1", L), DC, TH)
                act.activation(HH[:, :, :], src[:, :, :], ACT.Copy).then_inc(*act_ready.tick(("hh", L)))

                def exponents():
                    act.wait_ge(*dve_ready.at(("diffs", L)))
                    act.activation(r1[:, :, 0:4], r2[:, :, 0:4], ACT.Exp).then_inc(*act_ready.tick(("exp4", L)))
                    act.wait_ge(*dve_ready.at(("diff2", L)))
                    act.activation(v[1][:, :], v[0][:, :], ACT.Exp).then_inc(*act_ready.tick(("exp2", L)))

                if L < DEPTH:
                    turn(("p", L), 2, PTH)

                    def sig(n0, w, bank):
                        act.wait_ge(*evac_d.at((f"ple_g{L}", n0 // 512)))
                        ch.do(act.activation(SG[:, 0, n0:n0 + w], SG[:, 0, n0:n0 + w], ACT.Sigmoid))
                        return act.activation(SG[:, 1, n0:n0 + w], SG[:, 1, n0:n0 + w], ACT.Sigmoid)
                    linear(f"ple_g{L}", sig, before={0: exponents, 1: lambda: begin(f"ple_p{L}", 1)})
                    linear(f"ple_p{L}", lambda n0, w, bank: act.activation(Y[:, 0, n0:n0 + w], bank[:, 0:w], ACT.Copy))
                else:
                    exponents()
                split()
                act.wait_ge(*dve_ready.at(("table", L)))
                passes = act.value_load(TAB[0:1, 0:1], min_val=4, max_val=5)
                start, unit = s.turns, s.unit

                def evac_x(q, gathered, done, p):
                    act.wait_ge(*gathered.at(p, 0))
                    act.activation(XH[:, 4 * q:4 * q + 4, :], BK[6 + q][:, :].rearrange("p (c t) -> p c t", t=P),
                                   ACT.Copy).then_inc(*done.tick(0))

                evac_x(0, m.gather_a, m.xh_a, 0)
                m.xh_a.enter()
                act.wait_ge(*small_ready.at(("cleared", L)))
                unit = s.unit
                with act.Fori(0, passes) as p:
                    s.unit, s.turns = unit, start + p * turns
                    split()
                    act.wait_ge(unit_used, s.count(-2))
                    for half in range(2):
                        act.activation(YH[:, half * 512:half * 512 + 512], BK[4 + half][:, :], ACT.Copy)\
                           .then_inc(*m.yh.tick(half))
                    evac_x(1, m.gather_b, m.xh_b, p)
                    for e in range(E):
                        split()
                        act.wait_ge(unit_used, s.count(-1 if e == 0 else -2))
                        act.activation(SIL[:, :], BK[6 + e % 2][:, 0:256], ACT.Silu).then_inc(*m.silu.tick(e))
                        if e + 1 < E:
                            split()
                        split()
                        if e + 1 < E:
                            act.wait_ge(*m.at.at(p, e))
                        else:
                            act.wait_ge(*m.gs.at(p + 1, 0))
                        act.activation(AH[:, :, :], BK[6 + e % 2][:, 0:256].rearrange("p (c t) -> p c t", t=P),
                                       ACT.Copy).then_inc(*m.ah.tick(e))
                    act.wait_ge(*m.scattered.at(p, 0))
                    evac_x(0, m.gather_a, m.xh_a, p + 1)
                s.unit, s.turns = unit, act.snap(start + passes * turns)
                act.wait_ge(unit_used, s.count(-1))
                for half in range(2):
                    act.activation(YH[:, half * 512:half * 512 + 512], BK[4 + half][:, :], ACT.Copy)\
                       .then_inc(*act_ready.tick(("yh", L, half)))

            root("ln0", 2)
            begin("w_in0", 1)
            for L in range(DEPTH):
                turn(("h", L), DC, TH)

                def sine(i, h):
                    act.wait_ge(*dve_ready.at((f"arg{i}", L)))
                    act.activation(h[:, :], ARG[:, :], ACT.Sin, scale=6.2831845).then_inc(*act_ready.tick((f"sin{i}", L)))

                def squares():
                    act.wait_ge(*dve_ready.at(("filt", L)))
                    act.activation(PA[:, :, :].rearrange("p (a b) c -> p a (b c)", a=2), FF[:, :, :], ACT.Square)\
                        .then_inc(*act_ready.tick(("fsq", L)))

                def norm():
                    act.wait_ge(*dve_ready.at(("energy", L)))
                    act.activation(PA[:, 0, :], PA[:, 0, :], ACT.Sqrt).then_inc(*act_ready.tick(("energy", L)))

                def mixing_weight():
                    act.wait_ge(*dve_ready.at(("lamd", L)))
                    act.activation(LAM[:, 2:4], LAM[:, 0:2], ACT.Exp).then_inc(*act_ready.tick(("lam", L)))

                linear(f"w_in{L}", copy_to(U),
                       after={0: lambda: sine(1, H1), 1: lambda: sine(2, H2), 2: squares, 3: norm, 4: mixing_weight})
                act.wait_ge(*evac_d.at((f"w_in{L}", 4)))
                turn(("qk", L), 8, QKT)
                attention(("att", L), [(qb, 2, 2, 2, PA, ATA) for qb in range(TB) for _ in range(2)], 64 ** -0.5)
                begin(f"w_out{L}", 2)
                for q in range(2):
                    act.wait_ge(*small_ready.at(("pool", L, q)))
                    act.activation(YPT[:, 2 * q:2 * q + 2, :], BK[4 + q][0:64, :].rearrange("p (c t) -> p c t", c=2),
                                   ACT.Copy).then_inc(*act_ready.tick(("pool", L, q)))
                root(("subln", L), 8)
                turn(("cat", L), 8, TH)
                linear(f"w_out{L}", copy_to(Y), before={1: lambda: begin(f"ple_g{L}", 1)})
                root(("ln1", L), 2)
                experts(L)
                if L < DEPTH - 1:
                    root(("ln2", L), 2)
            root("memn", 2)
            turn("mem", DC, TH)

            def last_norms():
                root(("ln2", 1), 2)
                root(("n1", 2), 2)

            def memory_to(n0, w, bank):
                dst = MV_[:, 0, :] if n0 else MK[:, 0, :]
                return act.activation(dst, bank[:, 0:w], ACT.Copy)
            linear("mem", memory_to, before={0: last_norms, 1: lambda: begin("a_in", 1)})

            def mem_attention(L, qt, probs, at_):
                root(("qm", L), 8)
                if L == 2:
                    begin("a_out", 2)
                for g in range(2):
                    act.wait_ge(*turned.at((("qm", L), g)))
                    act.activation(qt[:, 2 * g:2 * g + 2, :], BK[4 + g][:, :].rearrange("p (c t) -> p c t", c=2),
                                   ACT.Copy, scale=MEMG[:, L - 2:L - 1]).then_inc(*turn_hi.tick((("qm", L), g)))
                attention(("mem", L), [(qb, 2, 4, 1, probs, at_) for qb in range(TB)], P ** -0.5)

            turn(("n1", 2), DC, TH)

            def gelu(n0, w, bank):
                f = ACT.Gelu if n0 < 2 * D else ACT.Copy
                other = BK[BK.index(bank) + 1]
                ch.do(act.activation(UV[:, 0, n0:n0 + w], bank[:, 0:w], f))
                return act.activation(UV[:, 1, n0:n0 + w], other[:, 0:w], f)
            linear("a_in", gelu, before={1: lambda: root("mk", 8), 4: lambda: root("aln", 2)})
            for g in range(2):
                act.wait_ge(*turned.at(("mk", g)))
                act.activation(MKT[:, 2 * g:2 * g + 2, :], BK[4 + g][:, :].rearrange("p (c t) -> p c t", c=2), ACT.Copy)\
                   .then_inc(*turn_hi.tick(("mk", g)))
            mem_attention(2, QMT, PB, ATB)
            turn(("cat", 2), 12, TH)
            linear("a_out", copy_to(Y))
            root(("n2", 2), 2)
            experts(2)
            root(("n1", 3), 2)
            turn(("n1", 3), DC, TH)
            linear("b_in", copy_to(ZB))
            act.wait_ge(*dve_ready.at("angles"))
            act.activation(TRIG[:, 0:2, :, :], TRIG[:, 2:4, :, :], ACT.Sin, scale=6.2831845)\
               .then_inc(*act_ready.tick("trig"))
            root("bq", 4)
            begin("q_up", 1)
            turn("cq", 4, TH)
            linear("q_up", copy_to(QQ), before={2: lambda: begin("kv_up", 1)})
            turn("ckv", 2, TH)
            linear("kv_up", copy_to(KV), before={0: lambda: root(("qkn", 0), 16)})
            mem_attention(3, QMT2, PC, ATC)
            root(("qkn", 1), 16)
            begin("b_out", 2)
            n = 0
            for what, dn, dr in (("q", QTN, QTR), ("k", KTN, KTR)):
                for h2 in range(4):
                    for part, dst, rowsn in (("n", dn, P), ("r", dr, 64)):
                        act.wait_ge(*turned.at((what, part, h2)))
                        act.activation(dst[0:rowsn, 2 * h2:2 * h2 + 2, :],
                                       BK[4 + n % 2][0:rowsn, :].rearrange("p (c t) -> p c t", c=2), ACT.Copy)\
                           .then_inc(*turn_hi.tick((what, part, h2)))
                        n += 1
            attention(("mla", 3), [(qb, qb + 1, 4, 1, PC, ATC) for qb in range(TB) for _ in range(2)], 192 ** -0.5)
            turn(("cat", 3), 12, TH)
            linear("b_out", copy_to(Y))
            root(("n2", 3), 2)
            experts(3)


        @block.vector
        def _(dve):
            s = Stream()
            ch = Chain(dve, chain_sem["dve"])
            go, do, sync = ch.go, ch.do, ch.sync

            def done(key):
                sync()
                dve.nop().then_inc(*dve_ready.tick(key))

            def bc(ap, shape):
                return ap.to_broadcast(shape)

            def split(width=UNIT):
                dve.wait_ge(hi_done, s.count(1))
                dve.tensor_tensor(WL[:, s.part(), 0:width], RAW[:, s.slot(), 0:width],
                                  WH[:, s.part(), 0:width].bitcast(F32), ALU.subtract).then_inc(split_done, 1)
                s.unit += 1

            def turn(key, chunks, dh, dl):
                for g in range(chunks // 2):
                    dve.wait_ge(*turn_hi.at((key, g)))
                    dve.tensor_tensor(dl[:, 2 * g:2 * g + 2, :],
                                      BK[4 + g % 2][:, :].rearrange("p (c t) -> p c t", c=2),
                                      dh[:, 2 * g:2 * g + 2, :].bitcast(F32), ALU.subtract)\
                       .then_inc(*turn_lo.tick((key, g)))

            begun = {"w_in1": 1, "mem": 1, "b_in": 1}

            def begin(key, units):
                chunks, strips, per_unit = linear_shape(key)
                for _ in range(units):
                    split(per_unit * strips[0][1])
                begun[key] = begun.get(key, 0) + units

            def linear(key, evac, before={}, after={}):
                chunks, strips, per_unit = linear_shape(key)
                ends = []

                def ahead(i):
                    for _ in range(chunks // per_unit - (begun.get(key, 0) if i == 0 else 0)):
                        split(per_unit * strips[i][1])
                    ends.append(s.count(0))
                ahead(0)
                for i, (n0, width) in enumerate(strips):
                    if i + 1 < len(strips):
                        ahead(i + 1)
                    if i in before:
                        before[i]()
                    dve.wait_ge(unit_used, ends[i])
                    if width > 512:
                        do(evac(n0, 512, BK[2]))
                        evac(n0 + 512, 512, BK[3]).then_inc(*evac_d.tick((key, i)))
                    else:
                        evac(n0, width, BK[2 * (i % 2) + 1]).then_inc(*evac_d.tick((key, i)))
                    if i in after:
                        after[i]()

            def copy_to(dst):
                return lambda n0, w, bank: dve.tensor_copy(dst[:, 1, n0:n0 + w], bank[:, 0:w])

            def stats(src, n, width, i):
                for k in range(n):
                    c = max(1, width // 512)
                    for j in range(c):
                        a = k * width + j * min(width, 512)
                        go(dve.bn_stats(NST[:, j, :], src[:, a:a + min(width, 512)]))
                    sync()
                    do(dve.bn_aggr(MV[:, i + k, :], NST[:, 0:c, :]))

            def inverse_root(key, n, rms, eps, gain=1.0):
                if rms:
                    do(dve.tensor_tensor(RS[:, 0:n], MV[:, 0:n, 0], MV[:, 0:n, 0], ALU.mult))
                    do(dve.tensor_tensor(RS[:, 0:n], RS[:, 0:n], MV[:, 0:n, 1], ALU.add))
                    do(dve.tensor_scalar(RS[:, 0:n], RS[:, 0:n], eps, None, ALU.add))
                else:
                    do(dve.tensor_scalar(RS[:, 0:n], MV[:, 0:n, 1], eps, None, ALU.add))
                finish_root(key, n, gain)

            def finish_root(key, n, gain=1.0):
                dve.nop().then_inc(*dve_ready.tick(("var", key)))
                dve.wait_ge(*act_ready.at(("root", key)))
                do(dve.reciprocal(RS[:, 0:n], RT[:, 0:n]))
                if gain != 1.0:
                    do(dve.tensor_scalar(RS[:, 0:n], RS[:, 0:n], gain, None, ALU.mult))

            def layer_norm(key, buf, eps, rows_key, width=D, at=0):
                for tb in range(TB):
                    stats(buf[:, tb, at:at + width], 1, width, tb)
                inverse_root(key, TB, False, eps)
                dve.wait_ge(*rows_in.at(rows_key))
                for slot, by, op1, op2 in ((0, MV[:, :, 0], ALU.subtract, ALU.mult), (1, RS, ALU.mult, ALU.add)):
                    for tb in range(TB):
                        x_ = buf[:, tb, at:at + width]
                        go(dve.scalar_tensor_tensor(x_, x_, by[:, tb:tb + 1], ROW[:, slot, 0:width], op1, op2))
                    sync()

            def rms_norm(key, dst, src, rows_key, gain):
                for tb in range(TB):
                    stats(src[:, tb, :], 1, D, tb)
                inverse_root(key, TB, True, EPS)
                if rows_key is not None:
                    dve.wait_ge(*rows_in.at(rows_key))
                for tb in range(TB):
                    go(dve.scalar_tensor_tensor(dst[:, tb, :], src[:, tb, :], RS[:, tb:tb + 1], gain[:, 0:D],
                                                ALU.mult, ALU.mult))
                sync()

            def attention(key, rounds, scale, cat, col, diff=False, causal=False):
                def negmax(r):
                    qb, kbs = rounds[r][0:2]
                    dve.wait_ge(*scores_ready.at((key, r)))
                    w = P * kbs
                    for b in range(2):
                        ps = BK[2 * (r % 2) + b][:, :].rearrange("p (c t) -> p c t", c=2)
                        if causal:
                            do(dve.tensor_tensor(ps[:, :, w - P:w], ps[:, :, w - P:w],
                                                 bc(CMASK.unsqueeze(1), [P, 2, P]), ALU.add))
                        do(dve.tensor_reduce(MX[:, b:4:2], ps[:, :, 0:w], X_AXIS, ALU.max))
                    dve.tensor_scalar(NM[:, 0:4], MX[:, 0:4], -scale, None, ALU.mult)\
                       .then_inc(*negmax_ready.tick((key, r)))

                negmax(0)
                for r, (qb, kbs, heads, step, probs, at_) in enumerate(rounds):
                    dve.wait_ge(*probs_ready.at((key, r)))
                    if r:
                        dve.wait_ge(*heads_taken.at((key, r - 1)))
                    do(dve.reciprocal(RC[:, 0:4], SU[:, 0:4]))
                    if diff:
                        do(dve.tensor_scalar(RC[:, 1:4:2], RC[:, 1:4:2], LAM[:, 4:5], None, ALU.mult))
                        for h in range(2):
                            go(dve.tensor_scalar(probs[:, 2 * h, :], probs[:, 2 * h, :], RC[:, 2 * h:2 * h + 1], None,
                                                 ALU.mult))
                        sync()
                        for h in range(2):
                            go(dve.scalar_tensor_tensor(probs[:, 2 * h, :], probs[:, 2 * h + 1, :],
                                                        RC[:, 2 * h + 1:2 * h + 2], probs[:, 2 * h, :],
                                                        ALU.mult, ALU.add))
                        sync()
                    dve.nop().then_inc(*weights_ready.tick((key, r)))
                    if r + 1 < len(rounds):
                        negmax(r + 1)
                    dve.wait_ge(*heads_ready.at((key, r)))
                    bank = BK[6 + r % 2]
                    a = col + (r * heads % 4 if diff else 4 * (r % 2) if causal else 0) * P
                    n = heads * P
                    if diff:
                        ins = dve.tensor_copy(cat[:, qb, a:a + n], bank[:, 0:n])
                    else:
                        ins = dve.tensor_tensor(cat[:, qb, a:a + n].rearrange("p (h c) -> p h c", c=P),
                                                bank[:, 0:n].rearrange("p (h c) -> p h c", c=P),
                                                bc(RC[:, 0:heads].unsqueeze(2), [P, heads, P]), ALU.mult)
                    ins.then_inc(*heads_taken.tick((key, r)))
                dve.wait_ge(*heads_taken.at((key, len(rounds) - 1)))

            def first_best(score, n, pri, out, m, t):
                full = [P, TB, n]
                do(dve.tensor_reduce(m, score, X_AXIS, ALU.max))
                do(dve.tensor_tensor(t, score, bc(m.unsqueeze(2), full), ALU.is_equal))
                do(dve.tensor_tensor(t, t, bc(pri.unsqueeze(1), full), ALU.mult))
                do(dve.tensor_reduce(v[11][:, :], t, X_AXIS, ALU.max))
                do(dve.tensor_tensor(out, t, bc(v[11][:, :].unsqueeze(2), full), ALU.is_equal))

            def experts(L):
                m = moe_signals[L]
                E = EPG[L]
                turns = E * 3 // TURN
                src = X if L < DEPTH else Y
                go(dve.memset(ZR[:, :].bitcast(F32), 0.0))
                do(dve.memset(ST[:, :].bitcast(F32), 0.0))
                dve.wait_ge(*params_in["route"].at(L))
                dve.wait_ge(*act_ready.at(("rwh", L)))
                do(dve.tensor_tensor(RWL[:, :, 0:NR[L]], RW[:, :, 0:NR[L]], RWH[:, :, 0:NR[L]].bitcast(F32), ALU.subtract))
                done(("rw", L))
                turn(("h1", L), DC, TH, TL)
                dve.wait_ge(*act_ready.at(("hh", L)))
                do(dve.tensor_tensor(HL[:, :, :], src[:, :, :], HH[:, :, :].bitcast(F32), ALU.subtract))

                def routing():
                    dve.wait_ge(*small_ready.at(("logits", L)))
                    full = [P, TB, E]
                    for tb in range(TB):
                        go(dve.tensor_tensor(LG[:, tb, 0:NR[L]], BK[6][:, tb * 64:tb * 64 + NR[L]], RB[:, 0:NR[L]], ALU.add))
                    sync()
                    V = [x[:, :] for x in v]
                    first_best(LG[:, :, 0:4], 4, PRI4, OH4[:, :, :], V[2], r1[:, :, 0:4])
                    done(("onehot", L))
                    do(dve.tensor_tensor(r2[:, :, 0:4], LG[:, :, 0:4], bc(V[2].unsqueeze(2), [P, TB, 4]), ALU.subtract))
                    done(("diffs", L))
                    for tb in range(TB):
                        go(dve.tensor_tensor(r3[:, tb, 0:4 * E].rearrange("p (g e) -> p g e", g=4),
                                             LG[:, tb, 4:4 + 4 * E].rearrange("p (g e) -> p g e", g=4),
                                             bc(OH4[:, tb, :].unsqueeze(2), [P, 4, E]), ALU.mult))
                    sync()
                    for tb in range(TB):
                        go(dve.tensor_reduce(FS[:, tb, 0:E], r3[:, tb, 0:4 * E].rearrange("p (g e) -> p e g", g=4), X_AXIS, ALU.add))
                    sync()
                    pri = PRI4 if E == 4 else PRI8
                    dve.wait_ge(*act_ready.at(("exp4", L)))
                    do(dve.tensor_reduce(V[4], r1[:, :, 0:4], X_AXIS, ALU.add))
                    first_best(FS[:, :, 0:E], E, pri, OH1[:, :, 0:E], V[2], r4[:, :, 0:E])
                    do(dve.scalar_tensor_tensor(FS[:, :, 0:E], OH1[:, :, 0:E], -1e30, FS[:, :, 0:E], ALU.mult, ALU.add))
                    first_best(FS[:, :, 0:E], E, pri, OH2[:, :, 0:E], V[3], r4[:, :, 0:E])
                    do(dve.tensor_tensor(V[0], V[3], V[2], ALU.subtract))
                    done(("diff2", L))
                    do(dve.reciprocal(V[4], V[4]))
                    dve.wait_ge(*act_ready.at(("exp2", L)))
                    do(dve.tensor_scalar(V[5], V[1], 1.0, None, ALU.add))
                    do(dve.reciprocal(V[5], V[5]))
                    do(dve.tensor_tensor(V[5], V[5], V[4], ALU.mult))
                    do(dve.tensor_tensor(V[6], V[5], V[1], ALU.mult))
                    do(dve.tensor_tensor(OH1[:, :, 0:E], OH1[:, :, 0:E], bc(V[5].unsqueeze(2), full), ALU.mult))
                    do(dve.tensor_tensor(OH2[:, :, 0:E], OH2[:, :, 0:E], bc(V[6].unsqueeze(2), full), ALU.mult))
                    if E < 8:
                        do(dve.memset(FS[:, :, E:8], 0.0))
                    do(dve.tensor_tensor(FS[:, :, 0:E], OH1[:, :, 0:E], OH2[:, :, 0:E], ALU.add))
                    do(dve.tensor_copy(GH[:, :, :], FS[:, :, :]))
                    do(dve.tensor_tensor(GL[:, :, :], FS[:, :, :], GH[:, :, :].bitcast(F32), ALU.subtract))
                    dve.wait_ge(*small_ready.at(("ranks", L)))
                    do(dve.tensor_tensor(r1[:, :, 0:4], BK[7][:, 0:8].rearrange("p (t g) -> p t g", g=4), OH4[:, :, :], ALU.mult))
                    do(dve.tensor_reduce(V[7], r1[:, :, 0:4], X_AXIS, ALU.add))
                    do(dve.tensor_tensor(r1[:, :, 0:4], OH4[:, :, :], bc(IDX4.unsqueeze(1), [P, TB, 4]), ALU.mult))
                    do(dve.tensor_reduce(V[8], r1[:, :, 0:4], X_AXIS, ALU.add))
                    do(dve.tensor_scalar(V[8], V[8], 128.0, None, ALU.mult))
                    do(dve.tensor_scalar(V[9], V[7], 128.0, None, ALU.is_ge))
                    do(dve.tensor_scalar(V[10], V[8], -1.0, 384.0, ALU.mult, ALU.add))
                    do(dve.tensor_tensor(V[10], V[10], V[9], ALU.mult))
                    do(dve.tensor_tensor(V[7], V[7], V[8], ALU.add))
                    do(dve.tensor_tensor(KEY[:, :], V[7], V[10], ALU.add))
                    for tb in range(TB):
                        go(dve.tensor_scalar(DG[:, tb, :], IDENT, KEY[:, tb:tb + 1], None, ALU.mult))
                    done(("diag", L))
                    do(dve.tensor_copy(JP[:, 0:1], PCOL))
                    do(dve.tensor_scalar(r2[:, 0, 0:4], BK[7][:, 8:12], 128.0, None, ALU.is_gt))
                    do(dve.tensor_reduce(r2[:, 0, 4:5], r2[:, 0, 0:4], X_AXIS, ALU.add))
                    do(dve.tensor_scalar(TABF[:, 0:1], r2[:, 0, 4:5], 4.0, None, ALU.add))
                    do(dve.tensor_copy(TABF[:, 1:5], IDX4))
                    do(dve.tensor_tensor(r2[:, 0, 0:4], r2[:, 0, 0:4], IDX4, ALU.mult))
                    do(dve.tensor_reduce(TABF[:, 5:6], r2[:, 0, 0:4], X_AXIS, ALU.add))
                    do(dve.tensor_copy(TAB[:, 0:6], TABF[:, 0:6]))

                if L < DEPTH:
                    turn(("p", L), 2, PTH, PTL)
                    dve.wait_ge(*rows_in.at(("ple", L)))

                    def bias(n0, w, bank):
                        other = BK[BK.index(bank) - 1]
                        do(dve.tensor_tensor(SG[:, 0, n0:n0 + w], other[:, 0:w], ROW[:, 0, n0:n0 + w], ALU.add))
                        return dve.tensor_tensor(SG[:, 1, n0:n0 + w], bank[:, 0:w], ROW[:, 0, n0:n0 + w], ALU.add)
                    linear(f"ple_g{L}", bias, before={0: routing, 1: lambda: begin(f"ple_p{L}", 1)})
                    sync()
                    dve.wait_ge(*evac_d.at((f"ple_g{L}", 1)))
                    done(("ple_b", L))
                    linear(f"ple_p{L}", copy_to(Y))
                else:
                    routing()
                split()
                dve.wait_ge(*small_ready.at(("keyrow", L)))
                do(dve.tensor_copy(PKROW[:, :], BK[6][:, 0:T]))
                done(("table", L))
                passes = dve.value_load(TAB[0:1, 0:1], min_val=4, max_val=5)
                start, unit = s.turns, s.unit

                def select(c):
                    for tb in range(TB):
                        c.go(dve.tensor_scalar(SP[:, tb, :], IOTA, KEY[:, tb:tb + 1], None, ALU.is_equal))
                    c.sync()
                    dve.nop().then_inc(*m.sel.tick("sel"))
                    c.do(dve.tensor_scalar(KEY[:, :], KEY[:, :], -128.0, None, ALU.add))

                def low_x(q, high, done, p):
                    dve.wait_ge(*high.at(p, 0))
                    dve.tensor_tensor(XL[:, 4 * q:4 * q + 4, :], BK[6 + q][:, :].rearrange("p (c t) -> p c t", t=P),
                                      XH[:, 4 * q:4 * q + 4, :].bitcast(F32), ALU.subtract).then_inc(*done.tick(0))

                select(ch)
                dve.wait_ge(*m.gather_a.at(0, 0))
                dve.tensor_copy(GS[:, :], BK[7][:, 256:264]).then_inc(*m.gs.tick(0))
                low_x(0, m.xh_a, m.xl_a, 0)
                for signal_ in (m.sel, m.gs, m.xl_a):
                    signal_.enter()
                unit = s.unit
                with dve.Fori(0, passes) as p:
                    s.unit, s.turns = unit, start + p * turns
                    lc = LoopChain(dve, m.chain, p, m.chain_values)
                    split()
                    for half in range(2):
                        dve.wait_ge(*m.yh.at(p, half))
                        a = slice(half * 512, half * 512 + 512)
                        dve.tensor_tensor(YL[:, a], BK[4 + half][:, :], YH[:, a].bitcast(F32), ALU.subtract)\
                           .then_inc(*m.yl.tick(half))
                    low_x(1, m.xh_b, m.xl_b, p)
                    for e in range(E):
                        split()
                        dve.wait_ge(*m.silu.at(p, e))
                        if e == 0:
                            dve.wait_ge(*m.gs.at(p, 0))
                        dve.scalar_tensor_tensor(GLU[:, :], SIL[:, :], GS[:, e:e + 1], BK[6 + e % 2][:, 256:512],
                                                 ALU.mult, ALU.mult).then_inc(*m.glu.tick(e))
                        if e + 1 < E:
                            split()
                        split()
                        if e == E - 1:
                            dve.wait_ge(*m.at.at(p, e))
                            dve.tensor_copy(GS[:, :], BK[7][:, 256:264]).then_inc(*m.gs.tick(0))
                        dve.wait_ge(*m.ah.at(p, e))
                        dve.tensor_tensor(AL[:, :, :], BK[6 + e % 2][:, 0:256].rearrange("p (c t) -> p c t", t=P),
                                          AH[:, :, :].bitcast(F32), ALU.subtract).then_inc(*m.al.tick(e))
                        if e == 0:
                            dve.wait_ge(*m.scattered.at(p, 0))
                            lc.go(dve.tensor_scalar(ST[:, :], PKROW[:, :], JP[:, 0:1], None, ALU.is_equal))
                            select(lc)
                            lc.do(dve.tensor_scalar(JP[:, 0:1], JP[:, 0:1], 128.0, None, ALU.add))
                    low_x(0, m.xh_a, m.xl_a, p + 1)
                s.unit, s.turns = unit, dve.snap(start + passes * turns)
                for half in range(2):
                    dve.wait_ge(*act_ready.at(("yh", L, half)))
                    a = slice(half * 512, half * 512 + 512)
                    go(dve.tensor_tensor(YL[:, a], BK[4 + half][:, :], YH[:, a].bitcast(F32), ALU.subtract))
                done(("yl", L))
                dve.wait_ge(*small_ready.at(("moe", L)))
                if L < DEPTH:
                    dve.wait_ge(*pool_ready.at(("ple", L)))
                for tb in range(TB):
                    for half in range(2):
                        a = slice(half * 512, half * 512 + 512)
                        go(dve.tensor_tensor(X[:, tb, a], X[:, tb, a], BK[2 * tb + half][:, :], ALU.add))
                done(("moe_out", L))

            dve.wait_ge(*x_in.at("x"))
            layer_norm("ln0", X, LN_EPS, "ln0")
            done("ln0")
            begin("w_in0", 1)
            for L in range(DEPTH):
                lam_init = (0.2, 0.8 - 0.6 * 0.7408182206817179)[L]
                turn(("h", L), DC, TH, TL)

                def argument(i):
                    cb, cf = 2 * i - 2, 2 * i - 1
                    dve.wait_ge(*small_ready.at((f"f{i}", L)))
                    ps = BK[7][0:64, (i - 1) * T:i * T]
                    do(dve.tensor_scalar(ARG[:, :], ps, HCOL[:, cb:cb + 1], HCOL[:, cf:cf + 1], ALU.add, ALU.mult))
                    do(dve.tensor_scalar(ARG[:, :], ARG[:, :], 1.0 / TWO_PI, None, ALU.mult))
                    do(dve.tensor_scalar(FR[:, :], ARG[:, :], ROUND, None, ALU.add))
                    do(dve.tensor_scalar(FR[:, :], FR[:, :], -ROUND, None, ALU.add))
                    do(dve.tensor_tensor(ARG[:, :], ARG[:, :], FR[:, :], ALU.subtract))
                    done((f"arg{i}", L))

                def window():
                    dve.wait_ge(*small_ready.at(("f3", L)))
                    for tb in range(TB):
                        for half in range(2):
                            a = slice(half * HY, (half + 1) * HY)
                            go(dve.tensor_tensor(FF[:, tb, a], BK[4 + tb][:, a], WIN[:, tb, :], ALU.mult))
                    sync()
                    do(dve.memset(FF[0:1, 0, HY:2 * HY], 0.0))
                    done(("filt", L))

                def normalise():
                    dve.wait_ge(*small_ready.at(("energy", L)))
                    do(dve.tensor_scalar(PA[:, 0, :], BK[6][:, 0:HY], 1e-6, None, ALU.add))
                    do(dve.tensor_tensor(PA[:, 0, :], PA[:, 0, :], BK[6][:, HY:2 * HY], ALU.add))
                    done(("energy", L))
                    go(dve.tensor_tensor(PA[:, 1:3, :], FF[:, :, 0:HY], FF[:, :, HY:2 * HY], ALU.add))
                    do(dve.tensor_tensor(FF[:, :, HY:2 * HY], FF[:, :, 0:HY], FF[:, :, HY:2 * HY], ALU.subtract))
                    dve.wait_ge(*act_ready.at(("energy", L)))
                    do(dve.reciprocal(PA[:, 3, :], PA[:, 0, :]))
                    for src_, a in ((PA[:, 1:3, :], 0), (FF[:, :, HY:2 * HY], HY)):
                        go(dve.tensor_tensor(FF[:, :, a:a + HY], src_, bc(PA[:, 3, :].unsqueeze(1), [P, 2, HY]), ALU.mult))
                    done(("fnorm", L))
                    dve.wait_ge(*params_in["hy"].at(L))
                    for i in range(2):
                        do(dve.tensor_tensor_reduce(KR[:, i, 0:64], LQ[:, 2 * i, :], LQ[:, 2 * i + 1, :], 1.0, 0.0,
                                                    ALU.mult, ALU.add, LAM[:, i:i + 1]))
                    done(("lamd", L))

                def keep_spectra():
                    dve.wait_ge(*small_ready.at(("kspec", L)))
                    go(dve.tensor_copy(KR[:, :, :], BK[4][:, :].rearrange("p (b c) -> p b c", b=2)))
                    go(dve.tensor_copy(KI[:, :, :], BK[5][:, :].rearrange("p (b c) -> p b c", b=2)))
                    go(dve.tensor_copy(K2[:, 0, :], BK[7][:, 0:HY]))
                    go(dve.tensor_copy(K2[:, 1, :], BK[4][:, HY:2 * HY]))
                    done(("kspec", L))

                linear(f"w_in{L}", copy_to(U), after={0: lambda: argument(1), 1: lambda: argument(2), 2: window,
                                                      3: normalise})
                dve.wait_ge(*evac_d.at((f"w_in{L}", 4)))
                dve.wait_ge(*evac_a.at((f"w_in{L}", 4)))
                for tb in range(TB):
                    qk = U[:, tb, 768:1792].rearrange("p (h c) -> p h c", c=64)
                    x1, x2 = qk[:, :, 0:8], qk[:, :, 8:16]
                    c = bc(COS8[:, tb * 8:tb * 8 + 8].unsqueeze(1), [P, 16, 8])
                    sn = bc(SIN8[:, tb * 8:tb * 8 + 8].unsqueeze(1), [P, 16, 8])
                    t = [PA[:, i, 0:128].rearrange("p (h c) -> p h c", c=8) for i in range(4)]
                    for o, a, b in ((0, x1, c), (1, x2, sn), (2, x1, sn), (3, x2, c)):
                        go(dve.tensor_tensor(t[o], a, b, ALU.mult))
                    sync()
                    go(dve.tensor_tensor(x1, t[0], t[1], ALU.subtract))
                    do(dve.tensor_tensor(x2, t[2], t[3], ALU.add))
                done(("rope", L))
                keep_spectra()
                dve.wait_ge(*act_ready.at(("lam", L)))
                do(dve.tensor_tensor(LAM[:, 4:5], LAM[:, 3:4], LAM[:, 2:3], ALU.subtract))
                do(dve.tensor_scalar(LAM[:, 4:5], LAM[:, 4:5], -lam_init, None, ALU.add))
                attention(("att", L), [(qb, 2, 2, 2, PA, ATA) for qb in range(TB) for _ in range(2)], 64 ** -0.5,
                          CAT8, 256, diff=True)
                begin(f"w_out{L}", 2)
                dve.wait_ge(*small_ready.at(("pool2", L)))
                for tb in range(TB):
                    go(dve.tensor_tensor(CAT8[:, tb, 768:1024], BK[6][:, tb * 256:tb * 256 + 256], SROW[:, 384:640], ALU.add))
                sync()
                for tb in range(TB):
                    go(dve.tensor_tensor(CAT8[:, tb, 768:1024], CAT8[:, tb, 768:1024], SROW[:, 640:896], ALU.mult))
                done(("pool", L))
                dve.wait_ge(*small_ready.at(("vspec", L)))
                vr = BK[1][:, :].rearrange("p (b c) -> p b c", b=2)
                vi = BK[2][:, :].rearrange("p (b c) -> p b c", b=2)
                go(dve.tensor_tensor(YF[:, 0:2, :], vr, KR[:, :, :], ALU.mult))
                go(dve.tensor_tensor(YF[:, 2:4, :], vr, KI[:, :, :], ALU.mult))
                go(dve.tensor_tensor(PA[:, 0:2, :], vi, KI[:, :, :], ALU.mult))
                go(dve.tensor_tensor(PA[:, 2:4, :], vi, K2[:, :, :], ALU.mult))
                sync()
                go(dve.tensor_tensor(YF[:, 0:2, :], YF[:, 0:2, :], PA[:, 0:2, :], ALU.subtract))
                go(dve.tensor_tensor(YF[:, 2:4, :], YF[:, 2:4, :], PA[:, 2:4, :], ALU.add))
                done(("yspec", L))
                for tb in range(TB):
                    go(dve.tensor_tensor(VV[:, tb, :], VV[:, tb, :], SROW[:, 0:HY], ALU.mult))
                sync()
                for qb in range(TB):
                    stats(CAT8[:, qb, 256:768], 4, P, 4 * qb)
                inverse_root(("subln", L), 8, True, LN_EPS, 1.0 - lam_init)
                heads = [CAT8[:, qb, 256:768].rearrange("p (h c) -> p h c", c=P) for qb in range(TB)]
                for qb, hd in enumerate(heads):
                    go(dve.tensor_tensor(hd, hd, bc(RS[:, 4 * qb:4 * qb + 4].unsqueeze(2), [P, 4, P]), ALU.mult))
                sync()
                for hd in heads:
                    go(dve.tensor_tensor(hd, hd, bc(SROW[:, 256:384].unsqueeze(1), [P, 4, P]), ALU.mult))
                sync()
                dve.wait_ge(*small_ready.at(("conv", L)))
                for tb in range(TB):
                    go(dve.tensor_tensor(VV[:, tb, :], VV[:, tb, :], BK[3][:, tb * HY:(tb + 1) * HY], ALU.add))
                sync()
                for tb in range(TB):
                    go(dve.tensor_tensor(CAT8[:, tb, 0:HY], VV[:, tb, :], UM[:, tb, 0:HY], ALU.mult))
                sync()
                done(("cat", L))
                turn(("cat", L), 8, TH, TL)
                linear(f"w_out{L}", copy_to(Y), before={1: lambda: begin(f"ple_g{L}", 1)})
                dve.wait_ge(*evac_d.at((f"w_out{L}", 1)))
                dve.wait_ge(*evac_a.at((f"w_out{L}", 1)))
                for tb in range(TB):
                    go(dve.scalar_tensor_tensor(X[:, tb, :], X[:, tb, :], ALPHA, Y[:, tb, :], ALU.mult, ALU.add))
                sync()
                layer_norm(("ln1", L), X, LN_EPS, ("ln1", L))
                done(("ln1", L))
                experts(L)
                if L < DEPTH - 1:
                    layer_norm(("ln2", L), X, LN_EPS, ("ln2", L))
                    done(("ln2", L))

            dve.wait_ge(*params_in["mem"].at(0))
            rms_norm("memn", Y, MEM, None, GROW[0])
            done("memn")
            turn("mem", DC, TH, TL)

            def last_norms():
                layer_norm(("ln2", 1), X, LN_EPS, ("ln2", 1))
                rms_norm(("n1", 2), Y, X, None, GROW[1])
                done(("norm1", 2))

            def memory_to(n0, w, bank):
                dst = MV_[:, 1, :] if n0 else MK[:, 1, :]
                return dve.tensor_copy(dst, bank[:, 0:w])
            linear("mem", memory_to, before={0: last_norms, 1: lambda: begin("a_in", 1)})
            dve.wait_ge(*evac_d.at(("mem", 1)))
            dve.wait_ge(*evac_a.at(("mem", 1)))

            def head_norm(key, src, done_key):
                for tb in range(TB):
                    stats(src(tb), 4, P, 4 * tb)
                inverse_root(key, 8, True, EPS)
                for tb in range(TB):
                    hd = src(tb).rearrange("p (h c) -> p h c", c=P)
                    go(dve.tensor_tensor(hd, hd, bc(RS[:, 4 * tb:4 * tb + 4].unsqueeze(2), [P, 4, P]), ALU.mult))
                done(done_key)

            turn(("n1", 2), DC, TH, TL)

            def memory_keys():
                for i in range(2):
                    do(dve.tensor_tensor(MEMG[:, i:i + 1], GQK[:, 2 * i:2 * i + 1], GQK[:, 2 * i + 1:2 * i + 2], ALU.mult))
                head_norm("mk", lambda tb: MK[:, tb, :], "mk")

            def gelu_done(n0, w, bank):
                dve.wait_ge(*evac_a.at(("a_in", n0 // 512)))
                return dve.nop()

            def gate_norm():
                dve.wait_ge(*evac_a.at(("a_in", 3)))
                layer_norm("aln", UV, EPS, "aln", D, D)
                done("aln")
            linear("a_in", gelu_done, before={1: memory_keys, 4: gate_norm})
            dve.wait_ge(*evac_d.at(("a_in", 4)))
            for g in range(2):
                dve.wait_ge(*small_ready.at(("ws", g)))
                do(dve.tensor_tensor(WST[:, 4 * g:4 * g + 4, :], BK[4 + g][:, :].rearrange("p (c t) -> p c t", t=P),
                                     bc(UPPER1.unsqueeze(1), [P, 4, P]), ALU.mult))
                done(("ws", g))
            head_norm(("qm", 2), lambda tb: UV[:, tb, 2048:2560], ("qm", 2))
            begin("a_out", 2)
            for q in range(4):
                dve.wait_ge(*small_ready.at(("spatial", q)))
                for g in (2 * q, 2 * q + 1):
                    a = slice(g * P, g * P + P)
                    go(dve.scalar_tensor_tensor(CAT12[:, :, a], BK[q][:, (g % 2) * T:(g % 2) * T + T]
                                                .rearrange("p (b c) -> p b c", b=2), BST[:, g:g + 1], UV[:, :, a],
                                                ALU.add, ALU.mult))
                done(("spatial", q))
            attention(("mem", 2), [(qb, 2, 4, 1, PB, ATB) for qb in range(TB)], P ** -0.5, CAT12, 1024)
            done(("cat", 2))
            turn(("cat", 2), 12, TH, TL)

            def residual(key):
                dve.wait_ge(*evac_d.at((key, 1)))
                dve.wait_ge(*evac_a.at((key, 1)))
                for tb in range(TB):
                    go(dve.tensor_tensor(X[:, tb, :], X[:, tb, :], Y[:, tb, :], ALU.add))
                sync()

            linear("a_out", copy_to(Y))
            residual("a_out")
            rms_norm(("n2", 2), Y, X, ("norm2", 2), ROW[:, 0, :])
            done(("norm2", 2))
            experts(2)
            rms_norm(("n1", 3), Y, X, ("norm1", 3), ROW[:, 0, :])
            done(("norm1", 3))
            turn(("n1", 3), DC, TH, TL)
            def angles():
                do(dve.tensor_copy(POSF[:, :], POS[:, :]))
                for tb in range(TB):
                    a, k = TRIG[:, 4, tb, :], TRIG[:, 5, tb, :]
                    do(dve.tensor_scalar(a, INVF, POSF[:, tb:tb + 1], None, ALU.mult))
                    for dst, shift in ((TRIG[:, 2, tb, :], 0.25), (TRIG[:, 3, tb, :], 0.0)):
                        do(dve.tensor_scalar(k, a, 1.0 / TWO_PI, shift, ALU.mult, ALU.add))
                        do(dve.tensor_scalar(k, k, ROUND, None, ALU.add))
                        do(dve.tensor_scalar(k, k, -ROUND, None, ALU.add))
                        do(dve.scalar_tensor_tensor(dst, k, -TURN1, a, ALU.mult, ALU.add))
                        do(dve.scalar_tensor_tensor(dst, k, -TURN2, dst, ALU.mult, ALU.add))
                        do(dve.scalar_tensor_tensor(dst, k, -TURN3, dst, ALU.mult, ALU.add))
                        do(dve.tensor_scalar(dst, dst, 1.0 / TWO_PI, shift, ALU.mult, ALU.add))
                        do(dve.tensor_scalar(k, dst, ROUND, None, ALU.add))
                        do(dve.tensor_scalar(k, k, -ROUND, None, ALU.add))
                        do(dve.tensor_tensor(dst, dst, k, ALU.subtract))
                done("angles")
            linear("b_in", copy_to(ZB), before={1: angles})
            dve.wait_ge(*evac_d.at(("b_in", 2)))
            dve.wait_ge(*evac_a.at(("b_in", 2)))
            for tb in range(TB):
                stats(ZB[:, tb, 0:512], 1, 512, tb)
                stats(ZB[:, tb, 512:768], 1, 256, 2 + tb)
            inverse_root("bq", 4, True, EPS)
            dve.wait_ge(*rows_in.at("bq"))
            for tb in range(TB):
                go(dve.scalar_tensor_tensor(ZB[:, tb, 0:512], ZB[:, tb, 0:512], RS[:, tb:tb + 1], ROW[:, 0, 0:512],
                                            ALU.mult, ALU.mult))
                go(dve.scalar_tensor_tensor(ZB[:, tb, 512:768], ZB[:, tb, 512:768], RS[:, 2 + tb:3 + tb],
                                            ROW[:, 0, 512:768], ALU.mult, ALU.mult))
            done("bq")
            begin("q_up", 1)
            turn("cq", 4, TH, TL)
            linear("q_up", copy_to(QQ), before={2: lambda: begin("kv_up", 1)})
            turn("ckv", 2, TH, TL)

            def rotate(x3, tb):
                c = bc(TRIG[:, 0, tb, :].unsqueeze(1), [P, 8, 32])
                sn = bc(TRIG[:, 1, tb, :].unsqueeze(1), [P, 8, 32])
                x1, x2 = x3[:, :, 0:32], x3[:, :, 32:64]
                t = [SCR[:, 256 * i:256 * i + 256].rearrange("p (h c) -> p h c", c=32) for i in range(4)]
                for o, a, b in ((0, x1, c), (1, x2, sn), (2, x1, sn), (3, x2, c)):
                    go(dve.tensor_tensor(t[o], a, b, ALU.mult))
                sync()
                go(dve.tensor_tensor(x1, t[0], t[1], ALU.subtract))
                do(dve.tensor_tensor(x2, t[2], t[3], ALU.add))

            def query_roots():
                dve.wait_ge(*evac_a.at(("q_up", 2)))
                dve.wait_ge(*evac_d.at(("q_up", 2)))
                for tb in range(TB):
                    do(dve.tensor_tensor(SCR[:, :], QQ[:, tb, :], QQ[:, tb, :], ALU.mult))
                    do(dve.tensor_reduce(RS[:, 8 * tb:8 * tb + 8], SCR[:, :].rearrange("p (h c) -> p h c", c=192), X_AXIS, ALU.add))
                do(dve.tensor_scalar(RS[:, :], RS[:, :], 1.0 / 192, EPS, ALU.mult, ALU.add))
                finish_root(("qkn", 0), 16)

            def queries():
                dve.wait_ge(*rows_in.at("qkn"))
                for tb in range(TB):
                    q3 = QQ[:, tb, :].rearrange("p (h c) -> p h c", c=192)
                    do(dve.tensor_tensor(q3, q3, bc(RS[:, 8 * tb:8 * tb + 8].unsqueeze(2), [P, 8, 192]), ALU.mult))
                    do(dve.tensor_tensor(q3, q3, bc(ROW[:, 0, 0:192].unsqueeze(1), [P, 8, 192]), ALU.mult))
                dve.wait_ge(*act_ready.at("trig"))
                for tb in range(TB):
                    rotate(QQ[:, tb, :].rearrange("p (h c) -> p h c", c=192)[:, :, 128:192], tb)

            linear("kv_up", copy_to(KV), before={0: query_roots, 1: queries})
            dve.wait_ge(*evac_d.at(("kv_up", 1)))
            dve.wait_ge(*evac_a.at(("kv_up", 1)))
            head_norm(("qm", 3), lambda tb: ZB[:, tb, 832:1344], ("qm", 3))
            attention(("mem", 3), [(qb, 2, 4, 1, PC, ATC) for qb in range(TB)], P ** -0.5, CAT12B, 1024)
            for tb in range(TB):
                kn = KV[:, tb, :].rearrange("p (h c) -> p h c", c=256)[:, :, 0:P]
                do(dve.tensor_tensor(SCR[:, 0:1024].rearrange("p (h c) -> p h c", c=P), kn, kn, ALU.mult))
                do(dve.tensor_reduce(RS[:, 8 * tb:8 * tb + 8], SCR[:, 0:1024].rearrange("p (h c) -> p h c", c=P), X_AXIS, ALU.add))
                kr = ZB[:, tb, 768:832]
                do(dve.tensor_tensor(SCR[:, 0:64], kr, kr, ALU.mult))
                do(dve.tensor_reduce(SCR[:, 64:65], SCR[:, 0:64], X_AXIS, ALU.add))
                do(dve.tensor_scalar(RS[:, 8 * tb:8 * tb + 8], RS[:, 8 * tb:8 * tb + 8], SCR[:, 64:65], None, ALU.add))
            do(dve.tensor_scalar(RS[:, :], RS[:, :], 1.0 / 192, EPS, ALU.mult, ALU.add))
            finish_root(("qkn", 1), 16)
            for tb in range(TB):
                kn = KV[:, tb, :].rearrange("p (h c) -> p h c", c=256)[:, :, 0:P]
                rb = RS[:, 8 * tb:8 * tb + 8].unsqueeze(2)
                do(dve.tensor_tensor(kn, kn, bc(rb, [P, 8, P]), ALU.mult))
                do(dve.tensor_tensor(kn, kn, bc(ROW[:, 0, 192:320].unsqueeze(1), [P, 8, P]), ALU.mult))
                kr = KRP[:, tb, :].rearrange("p (h c) -> p h c", c=64)
                do(dve.tensor_tensor(kr, bc(ZB[:, tb, 768:832].unsqueeze(1), [P, 8, 64]), bc(rb, [P, 8, 64]), ALU.mult))
                do(dve.tensor_tensor(kr, kr, bc(ROW[:, 0, 320:384].unsqueeze(1), [P, 8, 64]), ALU.mult))
            for tb in range(TB):
                rotate(KRP[:, tb, :].rearrange("p (h c) -> p h c", c=64), tb)
            done("qkn")
            begin("b_out", 2)
            attention(("mla", 3), [(qb, qb + 1, 4, 1, PC, ATC) for qb in range(TB) for _ in range(2)], 192 ** -0.5,
                      CAT12B, 0, causal=True)
            done(("cat", 3))
            turn(("cat", 3), 12, TH, TL)
            linear("b_out", copy_to(Y))
            residual("b_out")
            rms_norm(("n2", 3), Y, X, ("norm2", 3), ROW[:, 0, :])
            done(("norm2", 3))
            experts(3)
            done("out")


_INS = ['x', 'p', 'ln0_g', 'ln0_b', 'w_in', 'hy_conv_w', 'hy_conv_b', 'hy_fw1', 'hy_fb1', 'hy_freq1', 'hy_fw2',
        'hy_fb2', 'hy_freq2', 'hy_fw3', 'hy_bias', 'att_lq1', 'att_lk1', 'att_lq2', 'att_lk2', 'att_subln_g',
        'pool_w', 'pool_b', 'pool_scale', 'w_out', 'ln1_g', 'ln1_b', 'moe_wgc', 'moe_bgc', 'moe_wgf', 'moe_bgf',
        'moe_w1', 'moe_w3', 'moe_w2', 'ple_wg', 'ple_bg', 'ple_wp', 'ln2_g', 'ln2_b', 'mem_2', 'positions_2',
        'mem_norm_g_2', 'w_mem_kv_2', 'mem_qn_g_2', 'mem_kn_g_2', 'norm1_g_2', 'norm2_g_2', 'a_w_in_2', 'a_ln_g_2',
        'a_ln_b_2', 'a_w_s_2', 'a_b_s_2', 'a_w_out_2', 'b_w_in_2', 'b_q_norm_g_2', 'b_kv_norm_g_2', 'b_w_q_up_2',
        'b_w_kv_up_2', 'b_qn_g_2', 'b_kn_g_2', 'b_w_out_2', 'moe_w_group_2', 'moe_b_group_2', 'moe_w_expert_2',
        'moe_b_expert_2', 'moe_w_gate_2', 'moe_w_up_2', 'moe_w_down_2']


def constants():
    import numpy as np

    f = np.float32
    i, j = np.arange(P)[:, None], np.arange(P)[None, :]
    inv8 = np.power(f(500000.0), -np.arange(0, 16, 2, dtype=f) / f(16)).astype(f)
    ang = np.arange(T, dtype=f)[:, None] * inv8[None, :]
    by_block = lambda a: a.reshape(TB, P, -1).transpose(1, 0, 2)
    inv32 = np.power(f(10000.0), -(np.arange(32, dtype=f) * f(2.0) / f(64))).astype(f)
    parts = [i == j, i < j, np.ones((P, P)), np.broadcast_to(j, (P, P)), i <= j, np.where(j <= i, 0.0, -1e30), i,
             np.broadcast_to(4 - np.arange(4), (P, 4)), np.broadcast_to(8 - np.arange(8), (P, 8)),
             np.broadcast_to(np.arange(4), (P, 4)), np.zeros((P, 1)), by_block(np.cos(ang)).reshape(P, 16),
             by_block(np.sin(ang)).reshape(P, 16), np.broadcast_to(inv32, (P, 32))]
    c = {"c_small": np.concatenate([np.asarray(a, f) for a in parts], axis=1)}
    band = np.zeros((T, 4, T))
    pos = np.arange(T)
    for g, win in enumerate((2, 4, 8, 16)):
        lo, hi = np.clip(pos - win // 2, 0, T - 1), np.clip(pos + win // 2 - 1, 0, T - 1)
        inside = (pos[:, None] >= lo[None, :]) & (pos[:, None] <= hi[None, :])
        band[:, g, :] = inside / (hi - lo + 1)[None, :] - np.eye(T)
    c["c_band"] = band.reshape(TB, P, 4, T).transpose(1, 0, 2, 3)
    n = 2 * T
    tau, fr = np.arange(T)[:, None], np.arange(T)[None, :]
    a = 2 * np.pi * ((tau * fr) % n) / n
    alt = (-1.0) ** np.arange(T)
    dc, ds0 = np.cos(a), -np.sin(a)
    ds, dc2 = ds0.copy(), dc[:, 0:P].copy()
    ds[:, 0], dc2[:, 0] = alt, alt
    c["c_dc"], c["c_ds"], c["c_ds0"], c["c_dc2"] = (by_block(m) for m in (dc, ds, ds0[:, 0:P], dc2))
    w = np.full((T, 1), 2.0)
    w[0] = 1.0
    ir, ii = w * np.cos(a) / n, -2.0 * np.sin(a) / n
    ii[0] = alt / n
    c["c_inv"] = np.concatenate([ir, ii]).reshape(4, P, T).transpose(1, 0, 2)
    t = np.linspace(0.0, 1.0, T, dtype=f)[:, None]
    wpos = f(2.0 * np.pi) * np.arange(T, dtype=f)[:, None] / f(T)
    bands = np.linspace(1e-4, 15, 16, dtype=f)[None, :]
    c["c_zt"] = np.concatenate([t, np.cos(wpos * bands), -np.sin(wpos * bands)], axis=-1).T
    deltas = np.linspace(np.log(1e-2) / 1.5, np.log(1e-2) / 0.3, HY, dtype=f)[None, :]
    c["c_win"] = by_block(np.exp(-t * np.abs(deltas)))
    return {k: np.ascontiguousarray(m.astype(f)) for k, m in c.items()}


def kernel(**inputs):
    import numpy as _np
    import concourse.bacc as _bacc
    from concourse import mybir as _mybir
    from concourse.bass_utils import run_bass_kernel_spmd as _run

    consts = constants()
    arrays, seen = {}, {}
    for build in range(2):
        nc = _bacc.Bacc("TRN2", target_bir_lowering=False, num_devices=1)
        tensors = {}
        for name in _INS:
            a = _np.ascontiguousarray(inputs[name])
            arrays[f"in_{name}_dram"] = a
            tensors[name] = nc.dram_tensor(f"in_{name}_dram", a.shape, _mybir.dt.from_np(a.dtype), kind="ExternalInput").ap()
        for name, a in consts.items():
            arrays[f"{name}_dram"] = a
            tensors[name] = nc.dram_tensor(f"{name}_dram", a.shape, _mybir.dt.float32, kind="ExternalInput").ap()
        tensors["out"] = nc.dram_tensor("out_0_dram", (1, T, D), _mybir.dt.float32, kind="ExternalOutput").ap()
        program(nc, tensors, seen)
    r = _run(nc, [arrays], core_ids=[0])
    return r.results[0]["out_0_dram"]
```
